# Optimizing a Trainium2 kernel written in Bass

```python
import math
import jax, jax.numpy as jnp
from jax import lax
import numpy as np
import jax
import jax.numpy as jnp

D_MODEL = 1024
BATCH = 1
SEQ = 512
DEPTH = 2

DEEPNORM_ALPHA = (2 * DEPTH) ** 0.25
DEEPNORM_BETA = (8 * DEPTH) ** -0.25
LN_EPS = 1e-5
ROPE_THETA = 500000.0
ROPE_FRACTION = 4
RWKV_HEAD_DIM = 64
RWKV_DIM = D_MODEL // 2
RWKV_HEADS = RWKV_DIM // RWKV_HEAD_DIM
DECAY_LORA = max(32, int(round(1.8 * D_MODEL ** 0.5 / 32)) * 32)
ICLR_LORA = max(32, int(round(1.8 * D_MODEL ** 0.5 / 32)) * 32)
GATE_LORA = max(32, int(round(0.6 * D_MODEL ** 0.8 / 32)) * 32)
RWKV_GN_EPS = 64e-5
RWKV_PROJ_COLS = 3 * RWKV_DIM + DECAY_LORA + ICLR_LORA + GATE_LORA
MOBA_HEAD_DIM = 128
MOBA_WIDTH = D_MODEL - RWKV_DIM
MOBA_HEADS = MOBA_WIDTH // MOBA_HEAD_DIM
MOBA_BLOCK = 256
MOBA_TOPK = 3
MOBA_Q_CHUNK = 16
AB_IN_COLS = RWKV_PROJ_COLS + 3 * MOBA_WIDTH
AB_OUT_COLS = RWKV_DIM + MOBA_WIDTH
DIL_PAIRS = ((128, 1), (512, 4), (2048, 16))
DIL_GROUPS = len(DIL_PAIRS)
DIL_HEAD_DIM = 128
DIL_HEADS = D_MODEL // DIL_HEAD_DIM
C_WIDTH = DIL_HEADS * DIL_HEAD_DIM
C_IN_COLS = DIL_GROUPS * C_WIDTH + 2 * C_WIDTH
MLP_HIDDEN = 4 * D_MODEL
NEG_INF = -1e30


def _layer_norm(x, g, b):
    xf = x.astype(jnp.float32)
    mu = jnp.mean(xf, -1, keepdims=True)
    var = jnp.mean(jnp.square(xf - mu), -1, keepdims=True)
    return ((xf - mu) * lax.rsqrt(var + LN_EPS) * g + b).astype(x.dtype)

def _partial_rotary(x, pos):
    rot = x.shape[-1] // ROPE_FRACTION
    half = rot // 2
    inv_freq = ROPE_THETA ** (-jnp.arange(half, dtype=jnp.float32) / half)
    ang = pos.astype(jnp.float32)[:, None] * inv_freq[None, :]
    cos = jnp.cos(ang).astype(x.dtype)
    sin = jnp.sin(ang).astype(x.dtype)
    x1, x2, rest = x[..., :half], x[..., half:rot], x[..., rot:]
    return jnp.concatenate([x1 * cos - x2 * sin, x2 * cos + x1 * sin, rest], axis=-1)

def _token_shift(z):
    return jnp.pad(z, ((0, 0), (1, 0), (0, 0)))[:, :-1]

def _rwkv7_time_mix(z, shift_mix, w0, w_up, a0, a_up, g_up, k_k, k_a, r_k, lnx_g, lnx_b):
    B, T, _ = z.shape
    H, N = RWKV_HEADS, RWKV_HEAD_DIM
    f32 = jnp.float32
    z = z + (_token_shift(z) - z) * shift_mix
    o1, o2, o3 = RWKV_DIM, 2 * RWKV_DIM, 3 * RWKV_DIM
    o4 = o3 + DECAY_LORA
    o5 = o4 + ICLR_LORA
    r, k, v = z[..., :o1], z[..., o1:o2], z[..., o2:o3]
    w_d, a_d, g_d = z[..., o3:o4], z[..., o4:o5], z[..., o5:]
    w = -jax.nn.softplus(-(w0 + jnp.tanh(w_d) @ w_up)) - 0.5
    decay = jnp.exp(-jnp.exp(w.astype(f32)))
    a = jax.nn.sigmoid(a0 + a_d @ a_up).astype(f32)
    g = jax.nn.sigmoid(g_d) @ g_up
    heads = lambda t: t.astype(f32).reshape(B, T, H, N)
    kk = heads(k * k_k)
    kk = kk / jnp.maximum(jnp.linalg.norm(kk, axis=-1, keepdims=True), 1e-12)
    k = k.astype(f32) * (1.0 + (a - 1.0) * k_a)
    r, k, v, a, decay = heads(r), heads(k), heads(v), heads(a), heads(decay)

    def step(S, inp):
        r_t, w_t, k_t, v_t, a_t, b_t = inp
        sa = jnp.einsum('bhvk,bhk->bhv', S, a_t)
        S = S * w_t[:, :, None, :] + sa[..., None] * b_t[:, :, None, :] + v_t[..., None] * k_t[:, :, None, :]
        return S, jnp.einsum('bhvk,bhk->bhv', S, r_t)

    seq_first = lambda t: jnp.moveaxis(t, 1, 0)
    xs = (seq_first(r), seq_first(decay), seq_first(k), seq_first(v), seq_first(-kk), seq_first(kk * a))
    _, y = lax.scan(step, jnp.zeros((B, H, N, N), f32), xs)
    y = jnp.moveaxis(y, 0, 1)
    mu = jnp.mean(y, -1, keepdims=True)
    var = jnp.mean(jnp.square(y - mu), -1, keepdims=True)
    y = ((y - mu) * lax.rsqrt(var + RWKV_GN_EPS)).reshape(B, T, RWKV_DIM) * lnx_g + lnx_b
    bonus = jnp.sum(r * k * r_k, -1, keepdims=True) * v
    y = y + bonus.reshape(B, T, RWKV_DIM)
    return y * g

def _moba_attention(q, k, v):
    B, H, T, Dh = q.shape
    f32 = jnp.float32
    nb = -(-T // MOBA_BLOCK)
    Tp = nb * MOBA_BLOCK
    pad = ((0, 0), (0, 0), (0, Tp - T), (0, 0))
    q, k, v = jnp.pad(q, pad), jnp.pad(k, pad), jnp.pad(v, pad)
    scale = Dh ** -0.5
    kb = k.reshape(B, H, nb, MOBA_BLOCK, Dh)
    vb = v.reshape(B, H, nb, MOBA_BLOCK, Dh)
    n_sel = min(MOBA_TOPK, nb - 1)
    sel = None
    if n_sel > 0:
        k_mean = jnp.mean(kb.astype(f32), axis=3)
        gate = jnp.einsum('bhtd,bhnd->bhtn', q.astype(f32), k_mean)
        q_blk = jnp.arange(Tp) // MOBA_BLOCK
        past = jnp.arange(nb)[None, :] < q_blk[:, None]
        gate = jnp.where(past, gate, NEG_INF)
        _, sel = lax.top_k(gate, n_sel)
    bi = jnp.arange(B)[:, None, None, None]
    hi = jnp.arange(H)[None, :, None, None]

    def chunk(c):
        t0 = c * MOBA_Q_CHUNK
        i = t0 // MOBA_BLOCK
        qc = lax.dynamic_slice_in_dim(q, t0, MOBA_Q_CHUNK, axis=2)
        k_own = lax.dynamic_slice_in_dim(k, i * MOBA_BLOCK, MOBA_BLOCK, axis=2)
        v_own = lax.dynamic_slice_in_dim(v, i * MOBA_BLOCK, MOBA_BLOCK, axis=2)
        s_own = jnp.einsum('bhqd,bhkd->bhqk', qc, k_own).astype(f32) * scale
        causal = (i * MOBA_BLOCK + jnp.arange(MOBA_BLOCK))[None, :] <= (t0 + jnp.arange(MOBA_Q_CHUNK))[:, None]
        s_own = jnp.where(causal, s_own, NEG_INF)
        if n_sel == 0:
            p = jax.nn.softmax(s_own, axis=-1).astype(v.dtype)
            return jnp.einsum('bhqk,bhkd->bhqd', p, v_own)
        idx = lax.dynamic_slice_in_dim(sel, t0, MOBA_Q_CHUNK, axis=2)
        k_sel = kb[bi, hi, idx]
        v_sel = vb[bi, hi, idx]
        s_sel = jnp.einsum('bhqd,bhqskd->bhqsk', qc, k_sel).astype(f32) * scale
        valid = jnp.arange(n_sel) < i
        s_sel = jnp.where(valid[:, None], s_sel, NEG_INF)
        n_k = n_sel * MOBA_BLOCK
        s_all = jnp.concatenate([s_sel.reshape(B, H, MOBA_Q_CHUNK, n_k), s_own], axis=-1)
        p = jax.nn.softmax(s_all, axis=-1).astype(v.dtype)
        p_sel = p[..., :n_k].reshape(B, H, MOBA_Q_CHUNK, n_sel, MOBA_BLOCK)
        return (jnp.einsum('bhqsk,bhqskd->bhqd', p_sel, v_sel)
                + jnp.einsum('bhqk,bhkd->bhqd', p[..., n_k:], v_own))

    out = lax.map(chunk, jnp.arange(Tp // MOBA_Q_CHUNK))
    out = jnp.moveaxis(out, 0, 2).reshape(B, H, Tp, Dh)
    return out[:, :, :T]

def _dilated_window_branch(q, k, v, span, dilation):
    B, H, T, Dh = q.shape
    f32 = jnp.float32
    L = T // dilation
    W = span // dilation
    nblk = -(-L // W)
    Lp = nblk * W

    def strided(t):
        t = t.reshape(B, H, L, dilation, Dh).transpose(0, 1, 3, 2, 4)
        return jnp.pad(t, ((0, 0), (0, 0), (0, 0), (0, Lp - L), (0, 0)))

    qb = strided(q).reshape(B, H, dilation, nblk, W, Dh)
    kb = strided(k).reshape(B, H, dilation, nblk, W, Dh)
    vb = strided(v).reshape(B, H, dilation, nblk, W, Dh)
    prev = lambda t: jnp.pad(t, ((0, 0), (0, 0), (0, 0), (1, 0), (0, 0), (0, 0)))[:, :, :, :-1]
    k_band = jnp.concatenate([prev(kb), kb], axis=4)
    v_band = jnp.concatenate([prev(vb), vb], axis=4)
    s = jnp.einsum('bhrnqd,bhrnkd->bhrnqk', qb, k_band).astype(f32) * (Dh ** -0.5)
    qi = jnp.arange(W)[:, None]
    kj = jnp.arange(2 * W)[None, :]
    dist = W + qi - kj
    blk = jnp.arange(nblk)[:, None, None]
    mask = (dist >= 0) & (dist <= W) & ((blk > 0) | (kj >= W))
    s = jnp.where(mask, s, NEG_INF)
    lse = jax.nn.logsumexp(s, axis=-1)
    p = jnp.exp(s - lse[..., None]).astype(v.dtype)
    o = jnp.einsum('bhrnqk,bhrnkd->bhrnqd', p, v_band)
    o = o.reshape(B, H, dilation, Lp, Dh)[:, :, :, :L].transpose(0, 1, 3, 2, 4).reshape(B, H, T, Dh)
    lse = lse.reshape(B, H, dilation, Lp)[..., :L].transpose(0, 1, 3, 2).reshape(B, H, T)
    return o, lse

def _rwkv_moba_mixer(x, w_in, shift_mix, w0, w_up, a0, a_up, g_up, k_k, k_a, r_k, lnx_g, lnx_b, w_out, pos):
    B, T, _ = x.shape
    z = x @ w_in
    y_a = _rwkv7_time_mix(z[..., :RWKV_PROJ_COLS], shift_mix, w0, w_up, a0, a_up, g_up,
                          k_k, k_a, r_k, lnx_g, lnx_b)
    qkv = z[..., RWKV_PROJ_COLS:].reshape(B, T, 3, MOBA_HEADS, MOBA_HEAD_DIM).transpose(2, 0, 3, 1, 4)
    q = _partial_rotary(qkv[0], pos)
    k = _partial_rotary(qkv[1], pos)
    y_b = _moba_attention(q, k, qkv[2]).transpose(0, 2, 1, 3).reshape(B, T, MOBA_WIDTH)
    y = jnp.concatenate([y_a.astype(x.dtype), y_b.astype(x.dtype)], axis=-1)
    return (y @ w_out).astype(x.dtype)

def _dilated_mixer(x, w_in, w_out, pos):
    B, T, _ = x.shape
    z = x @ w_in
    nq = DIL_GROUPS * C_WIDTH
    q = z[..., :nq].reshape(B, T, DIL_GROUPS, DIL_HEADS, DIL_HEAD_DIM).transpose(0, 2, 3, 1, 4)
    kv = z[..., nq:].reshape(B, T, 2, DIL_HEADS, DIL_HEAD_DIM).transpose(2, 0, 3, 1, 4)
    q = _partial_rotary(q, pos)
    k = _partial_rotary(kv[0], pos)
    v = kv[1]
    outs, lses = [], []
    for g, (span, dilation) in enumerate(DIL_PAIRS):
        o, l = _dilated_window_branch(q[:, g], k, v, span, dilation)
        outs.append(o)
        lses.append(l)
    wts = jax.nn.softmax(jnp.stack(lses, axis=0), axis=0).astype(v.dtype)
    o = jnp.einsum('gbht,gbhtd->bhtd', wts, jnp.stack(outs, axis=0))
    o = o.transpose(0, 2, 1, 3).reshape(B, T, C_WIDTH)
    return (o @ w_out).astype(x.dtype)

def _sq_relu_mlp(x, w1, w2):
    return jnp.square(jax.nn.relu(x @ w1)) @ w2

def first_inputs(seed: int = 0) -> dict:
    key = jax.random.key(seed)
    ks = iter(jax.random.split(key, 24))
    f32 = jnp.float32
    nrm = lambda shape, scale: jax.random.normal(next(ks), shape, f32) * scale
    D = D_MODEL
    NE = (DEPTH + 1) // 2
    NO = DEPTH // 2
    x = nrm((BATCH, SEQ, D), 1.0)
    ab_w_in = nrm((NE, D, AB_IN_COLS), D ** -0.5)
    ab_shift_mix = jax.random.uniform(next(ks), (NE, RWKV_PROJ_COLS), f32)
    ab_w0 = jax.random.uniform(next(ks), (NE, RWKV_DIM), f32, minval=-6.0, maxval=0.0)
    ab_w_up = nrm((NE, DECAY_LORA, RWKV_DIM), 0.5 * DECAY_LORA ** -0.5)
    ab_a0 = nrm((NE, RWKV_DIM), 0.1)
    ab_a_up = nrm((NE, ICLR_LORA, RWKV_DIM), 0.5 * ICLR_LORA ** -0.5)
    ab_g_up = nrm((NE, GATE_LORA, RWKV_DIM), GATE_LORA ** -0.5)
    ab_k_k = 0.85 + nrm((NE, RWKV_DIM), 0.02)
    ab_k_a = 1.0 + nrm((NE, RWKV_DIM), 0.02)
    ab_r_k = nrm((NE, RWKV_HEADS, RWKV_HEAD_DIM), 0.1)
    ab_lnx_g = 1.0 + nrm((NE, RWKV_DIM), 0.02)
    ab_lnx_b = nrm((NE, RWKV_DIM), 0.02)
    ab_w_out = nrm((NE, AB_OUT_COLS, D), DEEPNORM_BETA * AB_OUT_COLS ** -0.5)
    c_w_in = nrm((NO, D, C_IN_COLS), D ** -0.5)
    c_w_out = nrm((NO, C_WIDTH, D), DEEPNORM_BETA * C_WIDTH ** -0.5)
    ln1_g = 1.0 + nrm((DEPTH, D), 0.02)
    ln1_b = nrm((DEPTH, D), 0.02)
    mlp_w1 = nrm((DEPTH, D, MLP_HIDDEN), D ** -0.5)
    mlp_w2 = nrm((DEPTH, MLP_HIDDEN, D), DEEPNORM_BETA * MLP_HIDDEN ** -0.5)
    ln2_g = 1.0 + nrm((DEPTH, D), 0.02)
    ln2_b = nrm((DEPTH, D), 0.02)
    return {'x': x, 'ab_w_in': ab_w_in, 'ab_shift_mix': ab_shift_mix, 'ab_w0': ab_w0,
            'ab_w_up': ab_w_up, 'ab_a0': ab_a0, 'ab_a_up': ab_a_up, 'ab_g_up': ab_g_up,
            'ab_k_k': ab_k_k, 'ab_k_a': ab_k_a, 'ab_r_k': ab_r_k, 'ab_lnx_g': ab_lnx_g,
            'ab_lnx_b': ab_lnx_b, 'ab_w_out': ab_w_out, 'c_w_in': c_w_in, 'c_w_out': c_w_out,
            'ln1_g': ln1_g, 'ln1_b': ln1_b, 'mlp_w1': mlp_w1, 'mlp_w2': mlp_w2,
            'ln2_g': ln2_g, 'ln2_b': ln2_b}

def first_block(x, ab_w_in, ab_shift_mix, ab_w0, ab_w_up, ab_a0, ab_a_up, ab_g_up, ab_k_k, ab_k_a,
              ab_r_k, ab_lnx_g, ab_lnx_b, ab_w_out, c_w_in, c_w_out, ln1_g, ln1_b, mlp_w1, mlp_w2,
              ln2_g, ln2_b):
    T = x.shape[1]
    pos = jnp.arange(T)
    for layer in range(DEPTH):
        j = layer // 2
        if layer % 2 == 0:
            h = _rwkv_moba_mixer(x, ab_w_in[j], ab_shift_mix[j], ab_w0[j], ab_w_up[j], ab_a0[j],
                                 ab_a_up[j], ab_g_up[j], ab_k_k[j], ab_k_a[j], ab_r_k[j],
                                 ab_lnx_g[j], ab_lnx_b[j], ab_w_out[j], pos)
        else:
            h = _dilated_mixer(x, c_w_in[j], c_w_out[j], pos)
        x = _layer_norm(DEEPNORM_ALPHA * x + h, ln1_g[layer], ln1_b[layer])
        x = _layer_norm(DEEPNORM_ALPHA * x + _sq_relu_mlp(x, mlp_w1[layer], mlp_w2[layer]),
                        ln2_g[layer], ln2_b[layer])
    return x


DEPTH_2 = 1

CHUNK = 64
Q_BLOCK = 128
EPS = 1e-6
NEG_BIG = -1e30
EXP_CLIP = 60.0

D_MIX = D_MODEL
N_MIXERS = 4
GROUP_W = D_MIX // N_MIXERS

S5_CH = 16
S5_GROUPS = GROUP_W // S5_CH
S5_STATE = 64
S5_DT_MIN = 1e-3
S5_DT_MAX = 1e-1

HG_HEADS = 4
HG_DH = GROUP_W // HG_HEADS

FOX_HEADS = 4
FOX_DH = GROUP_W // FOX_HEADS

ML_HEADS = 4
ML_DH = GROUP_W // ML_HEADS
ML_CONV = 4

D_FF = int(math.ceil(8 * D_MODEL / 3 / 256)) * 256

COL_WIDTHS = (GROUP_W,) * 8 + (FOX_HEADS,) + (GROUP_W,) * 4 + (ML_HEADS, ML_HEADS)
D_IN = sum(COL_WIDTHS)
SPLIT_IDX = tuple(int(c) for c in np.cumsum(COL_WIDTHS)[:-1])


F32 = jnp.float32

def rms_norm(x, gain):
    xf = x.astype(F32)
    y = xf * lax.rsqrt(jnp.mean(xf * xf, axis=-1, keepdims=True) + EPS)
    return (y * gain.astype(F32)).astype(x.dtype)

def headwise_rms_norm(x, gain, head_dim):
    shp = x.shape
    xf = x.astype(F32).reshape(shp[:-1] + (shp[-1] // head_dim, head_dim))
    y = xf * lax.rsqrt(jnp.mean(xf * xf, axis=-1, keepdims=True) + EPS)
    return (y.reshape(shp) * gain.astype(F32)).astype(x.dtype)

def causal_depthwise_conv(x, w):
    k_w, ch = w.shape
    return lax.conv_general_dilated(
        x, w[:, None, :].astype(x.dtype), window_strides=(1,), padding=[(k_w - 1, 0)],
        dimension_numbers=('NWC', 'WIO', 'NWC'), feature_group_count=ch)

def to_chunks(t):
    b, s, h, d = t.shape
    return t.reshape(b, s // CHUNK, CHUNK, h, d).transpose(1, 0, 3, 2, 4)

def from_chunks(t):
    nc, b, h, l, d = t.shape
    return t.transpose(1, 0, 3, 2, 4).reshape(b, nc * l, h, d)

def _complex_affine_combine(e1, e2):
    a1r, a1i, b1r, b1i = e1
    a2r, a2i, b2r, b2i = e2
    return (a2r * a1r - a2i * a1i, a2r * a1i + a2i * a1r,
            a2r * b1r - a2i * b1i + b2r, a2r * b1i + a2i * b1r + b2i)

def s5_mixer(u, lam_re, lam_im, b_re, b_im, c_re, c_im, d_skip, log_dt, w_glu, gain):
    bsz, seq, _ = u.shape
    uf = u.astype(F32)
    ug = uf.reshape(bsz, seq, S5_GROUPS, S5_CH)
    lr = jnp.minimum(lam_re.astype(F32), -1e-4)
    li = lam_im.astype(F32)
    dt = jnp.exp(log_dt.astype(F32))[:, None]
    mag = jnp.exp(lr * dt)
    ab_re = mag * jnp.cos(li * dt)
    ab_im = mag * jnp.sin(li * dt)
    den = lr * lr + li * li
    cf_re = ((ab_re - 1.0) * lr + ab_im * li) / den
    cf_im = (ab_im * lr - (ab_re - 1.0) * li) / den
    bre = b_re.astype(F32)
    bim = b_im.astype(F32)
    bb_re = cf_re[..., None] * bre - cf_im[..., None] * bim
    bb_im = cf_re[..., None] * bim + cf_im[..., None] * bre
    bu_re = jnp.einsum('bsgp,gnp->bsgn', ug, bb_re)
    bu_im = jnp.einsum('bsgp,gnp->bsgn', ug, bb_im)
    a_re = jnp.broadcast_to(ab_re, bu_re.shape)
    a_im = jnp.broadcast_to(ab_im, bu_im.shape)
    _, _, x_re, x_im = lax.associative_scan(
        _complex_affine_combine, (a_re, a_im, bu_re, bu_im), axis=1)
    y = (jnp.einsum('bsgn,gpn->bsgp', x_re, c_re.astype(F32))
         - jnp.einsum('bsgn,gpn->bsgp', x_im, c_im.astype(F32))).reshape(bsz, seq, GROUP_W)
    y = y + d_skip.astype(F32) * uf
    g = jax.nn.gelu(y)
    y = g * jax.nn.sigmoid(g @ w_glu.astype(F32))
    return rms_norm(y, gain).astype(u.dtype)

def _hgrn2_chunk(state, inp):
    q, k, v, lf = inp
    l = q.shape[2]
    b = jnp.cumsum(lf, axis=2)
    o_inter = jnp.einsum('bhtk,bhkv->bhtv', q * jnp.exp(b), state)
    causal = jnp.tril(jnp.ones((l, l), dtype=bool))
    diff = b[:, :, :, None, :] - b[:, :, None, :, :]
    decay = jnp.exp(jnp.where(causal[:, :, None], diff, NEG_BIG))
    scores = jnp.einsum('bhtk,bhsk,bhtsk->bhts', q, k, decay)
    o_intra = jnp.einsum('bhts,bhsv->bhtv', scores, v)
    b_last = b[:, :, -1:, :]
    new_state = (jnp.exp(b_last[:, :, 0, :])[..., None] * state
                 + jnp.einsum('bhsk,bhsv->bhkv', k * jnp.exp(b_last - b), v))
    return new_state, o_inter + o_intra

def hgrn2_mixer(q, fz, i, g, lb, gain):
    bsz, seq, _ = q.shape
    z = fz.astype(F32)
    logf = jax.nn.log_sigmoid(z) + jnp.log1p(lb * jnp.exp(jnp.minimum(-z, EXP_CLIP)))
    k = (1.0 - lb) * jax.nn.sigmoid(-z)

    def heads(t):
        return to_chunks(t.astype(F32).reshape(bsz, seq, HG_HEADS, HG_DH))

    s0 = jnp.zeros((bsz, HG_HEADS, HG_DH, HG_DH), F32)
    _, o = lax.scan(_hgrn2_chunk, s0, (heads(q), heads(k), heads(i), heads(logf)))
    o = from_chunks(o).reshape(bsz, seq, GROUP_W)
    o = headwise_rms_norm(o, gain, HG_DH) * jax.nn.silu(g.astype(F32))
    return o.astype(q.dtype)

def fox_mixer(q, k, v, fz, gain):
    bsz, seq, _ = q.shape

    def heads(t):
        return t.reshape(bsz, seq, FOX_HEADS, FOX_DH).transpose(0, 2, 1, 3)

    qh, kh, vh = heads(q), heads(k), heads(v)
    cum_logf = jnp.cumsum(jax.nn.log_sigmoid(fz.astype(F32)), axis=1).transpose(0, 2, 1)
    n_blk = seq // Q_BLOCK
    q_blocks = qh.reshape(bsz, FOX_HEADS, n_blk, Q_BLOCK, FOX_DH).transpose(2, 0, 1, 3, 4)
    f_blocks = cum_logf.reshape(bsz, FOX_HEADS, n_blk, Q_BLOCK).transpose(2, 0, 1, 3)
    k_pos = jnp.arange(seq)
    scale = FOX_DH ** -0.5

    def attend(args):
        blk, qb, fq = args
        q_pos = blk * Q_BLOCK + jnp.arange(Q_BLOCK)
        s = (jnp.einsum('bhqd,bhkd->bhqk', qb, kh).astype(F32) * scale
             + fq[..., None] - cum_logf[:, :, None, :])
        s = jnp.where(k_pos[None, :] <= q_pos[:, None], s, NEG_BIG)
        p = jax.nn.softmax(s, axis=-1)
        return jnp.einsum('bhqk,bhkd->bhqd', p.astype(vh.dtype), vh)

    out = lax.map(attend, (jnp.arange(n_blk), q_blocks, f_blocks))
    out = out.transpose(1, 0, 3, 2, 4).reshape(bsz, seq, GROUP_W)
    return headwise_rms_norm(out, gain, FOX_DH)

def _mlstm_chunk(carry, inp):
    c_mat, n_vec, m_prev = carry
    q, k, v, ig, lf = inp
    l = q.shape[2]
    b = jnp.cumsum(lf, axis=-1)
    causal = jnp.tril(jnp.ones((l, l), dtype=bool))
    d_log = jnp.where(causal, b[..., :, None] - b[..., None, :] + ig[..., None, :], NEG_BIG)
    inter_log = b + m_prev[..., None]
    m_t = jnp.maximum(inter_log, jnp.max(d_log, axis=-1))
    w_inter = jnp.exp(inter_log - m_t)
    qk = jnp.einsum('bhtd,bhsd->bhts', q, k) * jnp.exp(d_log - m_t[..., None])
    num = (w_inter[..., None] * jnp.einsum('bhtk,bhkv->bhtv', q, c_mat)
           + jnp.einsum('bhts,bhsv->bhtv', qk, v))
    den = w_inter * jnp.einsum('bhtk,bhk->bht', q, n_vec) + jnp.sum(qk, axis=-1)
    h = num / jnp.maximum(jnp.abs(den), jnp.exp(-m_t))[..., None]
    b_last = b[..., -1]
    src_log = b_last[..., None] - b + ig
    m_new = jnp.maximum(b_last + m_prev, jnp.max(src_log, axis=-1))
    w_src = jnp.exp(src_log - m_new[..., None])
    decay = jnp.exp(b_last + m_prev - m_new)
    c_new = decay[..., None, None] * c_mat + jnp.einsum('bhs,bhsk,bhsv->bhkv', w_src, k, v)
    n_new = decay[..., None] * n_vec + jnp.einsum('bhs,bhsk->bhk', w_src, k)
    return (c_new, n_new, m_new), h

def mlstm_mixer(q, k, v, o, ig, fz, conv_w, gain):
    bsz, seq, _ = q.shape
    qk = jax.nn.silu(causal_depthwise_conv(jnp.concatenate([q, k], axis=-1), conv_w))
    q_c, k_c = qk[..., :GROUP_W], qk[..., GROUP_W:]

    def heads(t):
        return to_chunks(t.astype(F32).reshape(bsz, seq, ML_HEADS, ML_DH))

    def gates(t):
        return to_chunks(t.astype(F32)[..., None])[..., 0]

    lf = jax.nn.log_sigmoid(fz.astype(F32))
    init = (jnp.zeros((bsz, ML_HEADS, ML_DH, ML_DH), F32),
            jnp.zeros((bsz, ML_HEADS, ML_DH), F32),
            jnp.zeros((bsz, ML_HEADS), F32))
    _, h = lax.scan(_mlstm_chunk, init,
                    (heads(q_c), heads(k_c * ML_DH ** -0.5), heads(v), gates(ig), gates(lf)))
    h = from_chunks(h).reshape(bsz, seq, GROUP_W)
    h = headwise_rms_norm(h, gain, ML_DH) * jax.nn.sigmoid(o.astype(F32))
    return h.astype(q.dtype)

def second_inputs(seed: int = 0) -> dict:
    key = jax.random.key(seed)
    ks = jax.random.split(key, 26)

    def nrm(k, shape, scale):
        return scale * jax.random.normal(k, shape, F32)

    x = nrm(ks[0], (BATCH, SEQ, D_MODEL), 1.0)
    w_in = nrm(ks[1], (DEPTH_2, D_MODEL, D_IN), D_MODEL ** -0.5)
    fox_fb = 2.0 + nrm(ks[2], (DEPTH_2, FOX_HEADS), 0.1)
    ml_ib = nrm(ks[3], (DEPTH_2, ML_HEADS), 0.1)
    ml_fb = jnp.linspace(3.0, 6.0, ML_HEADS, dtype=F32)[None, :] + nrm(ks[4], (DEPTH_2, ML_HEADS), 0.1)
    gate_bias = jnp.concatenate([fox_fb, ml_ib, ml_fb], axis=-1)
    n_idx = jnp.arange(S5_STATE, dtype=F32)
    s5_lambda_re = -0.5 + nrm(ks[5], (DEPTH_2, S5_GROUPS, S5_STATE), 0.01)
    s5_lambda_im = math.pi * n_idx + nrm(ks[6], (DEPTH_2, S5_GROUPS, S5_STATE), 0.01)
    s5_b_re = nrm(ks[7], (DEPTH_2, S5_GROUPS, S5_STATE, S5_CH), (2 * S5_CH) ** -0.5)
    s5_b_im = nrm(ks[8], (DEPTH_2, S5_GROUPS, S5_STATE, S5_CH), (2 * S5_CH) ** -0.5)
    s5_c_re = nrm(ks[9], (DEPTH_2, S5_GROUPS, S5_CH, S5_STATE), (2 * S5_STATE) ** -0.5)
    s5_c_im = nrm(ks[10], (DEPTH_2, S5_GROUPS, S5_CH, S5_STATE), (2 * S5_STATE) ** -0.5)
    s5_d = nrm(ks[11], (DEPTH_2, GROUP_W), 1.0)
    s5_log_dt = jax.random.uniform(ks[12], (DEPTH_2, S5_GROUPS), F32,
                                   math.log(S5_DT_MIN), math.log(S5_DT_MAX))
    s5_w_glu = nrm(ks[13], (DEPTH_2, GROUP_W, GROUP_W), GROUP_W ** -0.5)
    hgrn_lb_logits = nrm(ks[14], (DEPTH_2, GROUP_W), 0.5)
    mlstm_conv_w = nrm(ks[15], (DEPTH_2, ML_CONV, 2 * GROUP_W), ML_CONV ** -0.5)
    mix_gain = 1.0 + nrm(ks[16], (DEPTH_2, D_MIX), 0.02)
    w_out = nrm(ks[17], (DEPTH_2, D_MIX, D_MODEL), D_MIX ** -0.5)
    ln_mix_pre = 1.0 + nrm(ks[18], (DEPTH_2, D_MODEL), 0.02)
    ln_mix_post = 1.0 + nrm(ks[19], (DEPTH_2, D_MODEL), 0.02)
    ln_ffn_pre = 1.0 + nrm(ks[20], (DEPTH_2, D_MODEL), 0.02)
    ln_ffn_post = 1.0 + nrm(ks[21], (DEPTH_2, D_MODEL), 0.02)
    w_ffn_gate = nrm(ks[22], (DEPTH_2, D_MODEL, D_FF), D_MODEL ** -0.5)
    w_ffn_up = nrm(ks[23], (DEPTH_2, D_MODEL, D_FF), D_MODEL ** -0.5)
    w_ffn_down = nrm(ks[24], (DEPTH_2, D_FF, D_MODEL), D_FF ** -0.5)
    return {'x': x, 'w_in': w_in, 'gate_bias': gate_bias,
            's5_lambda_re': s5_lambda_re, 's5_lambda_im': s5_lambda_im,
            's5_b_re': s5_b_re, 's5_b_im': s5_b_im, 's5_c_re': s5_c_re, 's5_c_im': s5_c_im,
            's5_d': s5_d, 's5_log_dt': s5_log_dt, 's5_w_glu': s5_w_glu,
            'hgrn_lb_logits': hgrn_lb_logits, 'mlstm_conv_w': mlstm_conv_w,
            'mix_gain': mix_gain, 'w_out': w_out,
            'ln_mix_pre': ln_mix_pre, 'ln_mix_post': ln_mix_post,
            'ln_ffn_pre': ln_ffn_pre, 'ln_ffn_post': ln_ffn_post,
            'w_ffn_gate': w_ffn_gate, 'w_ffn_up': w_ffn_up, 'w_ffn_down': w_ffn_down}

def second_block(x, w_in, gate_bias, s5_lambda_re, s5_lambda_im, s5_b_re, s5_b_im, s5_c_re, s5_c_im,
              s5_d, s5_log_dt, s5_w_glu, hgrn_lb_logits, mlstm_conv_w, mix_gain, w_out,
              ln_mix_pre, ln_mix_post, ln_ffn_pre, ln_ffn_post, w_ffn_gate, w_ffn_up, w_ffn_down):
    lb_prob = jax.nn.softmax(hgrn_lb_logits.astype(F32), axis=0)
    lb_all = jnp.maximum(jnp.cumsum(lb_prob, axis=0) - lb_prob[0:1], 0.0)

    h = x
    for l in range(DEPTH_2):
        a = rms_norm(h, ln_mix_pre[l])
        proj = a @ w_in[l]
        (s5_u, hg_q, hg_f, hg_i, hg_g, fox_q, fox_k, fox_v, fox_f,
         ml_q, ml_k, ml_v, ml_o, ml_i, ml_f) = jnp.split(proj, SPLIT_IDX, axis=-1)
        gb = gate_bias[l]
        gain = mix_gain[l]
        y_a = s5_mixer(s5_u, s5_lambda_re[l], s5_lambda_im[l], s5_b_re[l], s5_b_im[l],
                       s5_c_re[l], s5_c_im[l], s5_d[l], s5_log_dt[l], s5_w_glu[l],
                       gain[0:GROUP_W])
        y_b = hgrn2_mixer(hg_q, hg_f, hg_i, hg_g, lb_all[l], gain[GROUP_W:2 * GROUP_W])
        y_c = fox_mixer(fox_q, fox_k, fox_v, fox_f + gb[0:FOX_HEADS],
                        gain[2 * GROUP_W:3 * GROUP_W])
        y_d = mlstm_mixer(ml_q, ml_k, ml_v, ml_o,
                          ml_i + gb[FOX_HEADS:FOX_HEADS + ML_HEADS],
                          ml_f + gb[FOX_HEADS + ML_HEADS:FOX_HEADS + 2 * ML_HEADS],
                          mlstm_conv_w[l], gain[3 * GROUP_W:4 * GROUP_W])
        mix = jnp.concatenate([y_a, y_b, y_c, y_d], axis=-1) @ w_out[l]
        h = h + rms_norm(mix, ln_mix_post[l])

        a = rms_norm(h, ln_ffn_pre[l])
        ff = (jax.nn.silu(a @ w_ffn_gate[l]) * (a @ w_ffn_up[l])) @ w_ffn_down[l]
        h = h + rms_norm(ff, ln_ffn_post[l])
    return h


def setup_inputs(seed=0):
    out = dict(first_inputs(seed))
    for name, value in second_inputs(seed + 1).items():
        if name != "x":
            out[name + "_2"] = value
    return out


def reference(
    x, ab_w_in, ab_shift_mix, ab_w0, ab_w_up, ab_a0, ab_a_up, ab_g_up, ab_k_k, ab_k_a, ab_r_k,
    ab_lnx_g, ab_lnx_b, ab_w_out, c_w_in, c_w_out, ln1_g, ln1_b, mlp_w1, mlp_w2, ln2_g, ln2_b,
    w_in_2, gate_bias_2, s5_lambda_re_2, s5_lambda_im_2, s5_b_re_2, s5_b_im_2, s5_c_re_2,
    s5_c_im_2, s5_d_2, s5_log_dt_2, s5_w_glu_2, hgrn_lb_logits_2, mlstm_conv_w_2, mix_gain_2,
    w_out_2, ln_mix_pre_2, ln_mix_post_2, ln_ffn_pre_2, ln_ffn_post_2, w_ffn_gate_2, w_ffn_up_2,
    w_ffn_down_2,
):
    x = first_block(
        x, ab_w_in, ab_shift_mix, ab_w0, ab_w_up, ab_a0, ab_a_up, ab_g_up, ab_k_k, ab_k_a,
        ab_r_k, ab_lnx_g, ab_lnx_b, ab_w_out, c_w_in, c_w_out, ln1_g, ln1_b, mlp_w1, mlp_w2,
        ln2_g, ln2_b,
    )
    return second_block(
        x, w_in_2, gate_bias_2, s5_lambda_re_2, s5_lambda_im_2, s5_b_re_2, s5_b_im_2, s5_c_re_2,
        s5_c_im_2, s5_d_2, s5_log_dt_2, s5_w_glu_2, hgrn_lb_logits_2, mlstm_conv_w_2,
        mix_gain_2, w_out_2, ln_mix_pre_2, ln_mix_post_2, ln_ffn_pre_2, ln_ffn_post_2,
        w_ffn_gate_2, w_ffn_up_2, w_ffn_down_2,
    )


_drawn_inputs = setup_inputs


def setup_inputs(seed=0):
    import zlib

    import numpy as np

    out = dict(_drawn_inputs(seed))
    spreads = {}
    factors = {'ab_w_up': 8.0,
     'ab_a0': 6.435,
     'ab_k_k': 156.455,
     'ab_k_a': 8.0,
     'ab_lnx_g': 8.0,
     'ab_lnx_b': 8.0,
     's5_lambda_re_2': 200.0,
     'mix_gain_2': 3.59,
     'ln_mix_post_2': 3.131,
     'ln_ffn_pre_2': 3.376,
     'ln_ffn_post_2': 48.163,
     's5_lambda_im_2': 24.221,
     's5_b_re_2': 33.704,
     's5_b_im_2': 34.184,
     's5_c_re_2': 34.68,
     's5_c_im_2': 33.864,
     's5_log_dt_2': 24.345}
    for name, (base, spread) in spreads.items():
        noise = np.random.default_rng([zlib.crc32(name.encode()), seed]).standard_normal(out[name].shape)
        drawn = base * np.exp(spread * noise) if base else spread * noise
        out[name] = jnp.asarray(drawn.astype(out[name].dtype))
    for name, factor in factors.items():
        out[name] = (out[name] * factor).astype(out[name].dtype)
    return out
```

```python
from collections import namedtuple
from contextlib import ExitStack

import numpy as np
import concourse.bass as bass
from concourse import mybir

F32 = mybir.dt.float32
F32R = mybir.dt.float32r
BF16 = mybir.dt.bfloat16
ALU = mybir.AluOpType
ACT = mybir.ActivationFunctionType
AX = mybir.AxisListType

P = 128
T = 512
D = 1024
KD = D // P
ALPHA = 4 ** 0.25
LN_EPS = 1e-5
GN_EPS = 64e-5
RMS_EPS = 1e-6
NEG = -1e30
C = 64
NCH = T // C
NT = T // P
HALF = 4096 // P // 2
FT = 2816 // P // 2
RING = 4
BANKS = 4
KT_MAX = 11

CONST_COLS = {"ident": P, "ones": P, "blk": P, "ropec": T, "ropes": T, "chunk": T, "rmask": 5 * C,
              "lmask": 7 * C, "lmaskt": 6 * C, "s5mask": 8 * P, "sel": 4 * P}
MASK_COLS = {"identb": P, "causal": P, "prev": P, "mod4": 4 * P, "mod16": 4 * P}


def offsets(cols):
    at, out = 0, {}
    for name, n in cols.items():
        out[name] = (at, at + n)
        at += n
    return out, at


CONST_AT, CONST_N = offsets(CONST_COLS)
MASK_AT, MASK_N = offsets(MASK_COLS)

PARAM_COLS = {"mix": 15, "w0": 4, "a0": 4, "kk": 4, "ka": 4, "rk": 4, "gng": 4, "gnb": 4,
              "ln1g0": 8, "ln1b0": 8, "ln2g0": 8, "ln2b0": 8, "ln1g1": 8, "ln1b1": 8,
              "ln2g1": 8, "ln2b1": 8, "pre": 8, "post": 8, "fpre": 8, "fpost": 8,
              "gain": 8, "gateb": 1, "s5d": 2, "lre": 8, "lim": 8, "ldt": 8, "conv": 16,
              "bre": 128, "bim": 128, "cre": 128, "cim": 128}
PARAM_AT, PARAM_N = offsets(PARAM_COLS)

SMALL_COLS = {"lora": 512, "gup0": 512, "gup1": 512, "wglu": 512}
SMALL_AT, SMALL_N = offsets(SMALL_COLS)


def const_array():
    a = {k: np.zeros((P, n), np.float32) for k, n in CONST_COLS.items()}
    p = np.arange(P)
    a["ident"][:] = np.eye(P)
    a["ones"][:] = 1
    a["blk"][:] = (p[:, None] // 64 == p[None, :] // 64)
    inv = np.float32(500000.0) ** (-np.arange(16, dtype=np.float32) / np.float32(16))
    ang = inv[:, None] * np.arange(T, dtype=np.float32)[None]
    a["ropec"][0:16] = a["ropec"][16:32] = np.cos(ang)
    a["ropes"][0:16] = -np.sin(ang)
    a["ropes"][16:32] = np.sin(ang)
    a["chunk"][:] = (np.arange(T) % C != 0)
    s, t = np.arange(C)[:, None], np.arange(C)[None]
    both = lambda m: np.concatenate([m, m], 0)
    a["rmask"][:] = both(np.concatenate([s < t, s <= t, s < t, s <= t, s > t], 1))
    level = lambda m: (s // (2 * m) == t // (2 * m)) & (s % (2 * m) < m) & (t % (2 * m) >= m)
    levels = [level(m) for m in (1, 2, 4, 8, 16, 32)]
    a["lmask"][:] = both(np.concatenate(levels + [s == t], 1))
    a["lmaskt"][:] = both(np.concatenate([m.T for m in levels], 1))
    m = a["s5mask"].reshape(P, 8, P)
    for j in range(8):
        m[:, j] = ((2 * j + p[:, None] // 64) % 8 == p[None, :] // 16)
    m = a["sel"].reshape(P, 4, P)
    for h in range(4):
        m[:, h] = (p[:, None] % 32 == h)
    return np.concatenate([a[k] for k in CONST_COLS], 1)


def mask_array():
    q, k = np.arange(P)[:, None], np.arange(P)[None]
    bias = lambda ok: np.where(ok, 0.0, NEG)
    mod = lambda n: np.concatenate([bias((q - k) % n == 0)] * 3 + [bias(((q - k) % n == 0) & (k <= q))], 1)
    parts = {"identb": np.eye(P), "causal": bias(k <= q), "prev": bias(k >= q), "mod4": mod(4), "mod16": mod(16)}
    return np.concatenate([parts[n] for n in MASK_COLS], 1).astype(np.float32)


class Core:

    def __init__(self, nc, io, ctx):
        self.nc, self.io = nc, io
        COUNTS.clear()
        sb = lambda n, s, d=F32: ctx.enter_context(nc.sbuf_tensor(n, s, d))
        sem = lambda n: ctx.enter_context(nc.semaphore(n))
        self.consts = sb("consts", [P, CONST_N])
        self.masks = sb("masks", [P, MASK_N], BF16)
        self.params = sb("params", [P, PARAM_N])
        self.X = sb("X", [P, KD, T])
        self.Y = sb("Y", [P, KD, T])
        self.eps_ln, self.eps_gn, self.eps_rms = sb("eps_ln", [P, 1]), sb("eps_gn", [P, 1]), sb("eps_rms", [P, 1])
        self.raw = [sb(f"w_raw{i}", [P, KT_MAX * P]) for i in range(RING)]
        self.banks = ctx.enter_context(nc.psum_tensor("banks", [P, 8, T], F32))
        self.psum = [self.banks[:, i, :] for i in range(8)]
        self.w_landed = [sem(f"w_landed{i}") for i in range(RING)]
        self.hi_ready = sem("hi_ready")
        self.split_ready = sem("split_ready")
        self.unit_used = sem("unit_used")
        self.block_out = sem("block_out")
        self.units = self.blocks = 0
        self.gemms = []
        self.n_gemm = 0
        self.to_clear = []
        self.stage = 0

    def const(self, name, rows=slice(None)):
        a, b = CONST_AT[name]
        return self.consts[rows, a:b]

    def mask(self, name):
        a, b = MASK_AT[name]
        return self.masks[:, a:b]

    def param(self, name, j=None):
        a, b = PARAM_AT[name]
        return self.params[:, a:b] if j is None else self.params[:, a + j:a + j + 1]


class Stage:

    def __init__(self, core, name):
        core.stage += 1
        self.core, self.nc, self.tag = core, core.nc, f"{name}{core.stage}_"
        self.ctx = ExitStack()
        self.own, self.cleared = [], []

    def __enter__(self):
        return self

    def __exit__(self, *e):
        self.ctx.close()
        for h in self.cleared:
            self.nc.release_semaphore(h)
        self.core.to_clear += self.own

    def sb(self, name, shape, dt=F32):
        return self.ctx.enter_context(self.nc.sbuf_tensor(self.tag + name, shape, dt))

    def sems(self, names, prefix=""):
        made = [self.nc.alloc_semaphore(self.tag + prefix + n) for n in names.split()]
        self.own += made
        return namedtuple("Semaphores", names)(*made)

    def block(self, pool=None):
        block = self.ctx.enter_context(self.nc.Block(no_gpsimd_drain=True))
        self.cleared, self.core.to_clear = self.core.to_clear, []

        @block.gpsimd
        def _(eng):
            nums = sorted(h.num for h in self.cleared)
            while nums:
                n = 1
                while n < len(nums) and nums[n] == nums[0] + n:
                    n += 1
                eng.sem_clear(range(nums[0], nums[0] + n))
                nums = nums[n:]
            if pool:
                pool(eng)
        return block


def done(eng, ins, sem):
    ins.then_inc(sem, 1)
    COUNTS[sem.name] = COUNTS.get(sem.name, 0) + 1
    eng.wait_ge(sem, COUNTS[sem.name])


COUNTS = {}


def in_groups(eng, n, group, body, lo=0):
    whole = n // group
    for j in range(lo, min(group, n)):
        body(0, j)
    if whole > 2:
        with eng.Fori(1, whole, 1) as it:
            for j in range(group):
                body(it, j)
    elif whole == 2:
        for j in range(group):
            body(1, j)
    if whole:
        for j in range(n - whole * group):
            body(whole, j)


def at_start(it):
    return isinstance(it, int) and it == 0


def stream_weights(core, sp, g, lo=0, hi=None, base=None):
    w, kt, n = core.gemms[g]
    base = core.units if base is None else base
    n = n if hi is None else min(hi, n)

    def body(it, j):
        at = base + j
        if at >= RING or not at_start(it):
            sp.wait_ge(core.split_ready, at - RING + 1 + it * RING)
        sp.dma_start(core.raw[at % RING][:, 0:kt * P], w[it * RING + j]).then_inc(core.w_landed[at % RING], 16)

    in_groups(sp, n, RING, body, lo)


class Evac:
    pair = 1
    act = dve = None

    def setup(self, st, tag):
        pass

    def start(self, dve):
        pass


class Plain(Evac):

    def __init__(self, Z, off=0, scale=1.0):
        self.Z, self.off, self.scale = Z, off, scale

    def act(self, act, b, nth, banks, core, b0):
        act.activation(self.Z[:, bass.ds(b + self.off, 1), :], banks[0], ACT.Copy, scale=self.scale).then_inc(core.block_out, 1)


class Residual(Evac):

    def __init__(self, Y, X):
        self.Y, self.X = Y, X

    def dve(self, dve, b, nth, banks, core, b0):
        dve.scalar_tensor_tensor(self.Y[:, bass.ds(b, 1), :], self.X[:, bass.ds(b, 1), :], ALPHA, banks[0],
                                 ALU.mult, ALU.add).then_inc(core.block_out, 1)


class Accumulate(Evac):

    def __init__(self, Y):
        self.Y = Y

    def dve(self, dve, b, nth, banks, core, b0):
        y = self.Y[:, bass.ds(b, 1), :]
        dve.tensor_tensor(y, y, banks[0], ALU.add).then_inc(core.block_out, 1)


class SquaredRelu(Evac):

    def __init__(self, hh, hl):
        self.hh, self.hl = hh, hl

    def setup(self, st, tag):
        self.relu, self.sq = st.sb(tag + "relu", [P, T]), st.sb(tag + "sq", [P, T])
        self.s = st.sems("squared hidden_hi hidden_lo", tag)

    def act(self, act, b, nth, banks, core, b0):
        if not (isinstance(b, int) and b == 0):
            act.wait_ge(self.s.squared, nth - 1)
        act.activation(self.relu[:], banks[0], ACT.Relu).then_inc(core.block_out, 1)
        act.wait_ge(core.block_out, b0 + nth)
        act.activation(self.hh[:, bass.ds(b, 1), :], self.relu[:], ACT.Square).then_inc(self.s.hidden_hi, 1)
        act.wait_ge(self.s.hidden_hi, nth)

    def dve(self, dve, b, nth, banks, core, b0):
        if not (isinstance(b, int) and b == 0):
            dve.wait_ge(self.s.hidden_lo, nth - 1)
        dve.wait_ge(core.block_out, b0 + nth)
        dve.tensor_tensor(self.sq[:], self.relu[:], self.relu[:], ALU.mult).then_inc(self.s.squared, 1)
        dve.wait_ge(self.s.squared, nth)
        dve.wait_ge(self.s.hidden_hi, nth)
        dve.tensor_tensor(self.hl[:, bass.ds(b, 1), :], self.sq[:], self.hh[:, bass.ds(b, 1), :].bitcast(F32),
                          ALU.subtract).then_inc(self.s.hidden_lo, 1)


class Gated(Evac):
    pair = 2

    def __init__(self, hh, hl):
        self.hh, self.hl = hh, hl

    def setup(self, st, tag):
        self.sg, self.gs, self.prod = (st.sb(tag + n, [P, T]) for n in ("sg", "gs", "prod"))
        self.s = st.sems("sig gated hidden_hi hidden_lo", tag)

    def act(self, act, b, nth, banks, core, b0):
        act.activation(self.sg[:], banks[0], ACT.Sigmoid).then_inc(self.s.sig, 1)
        act.wait_ge(core.block_out, b0 + 2 * nth)
        act.activation(self.hh[:, bass.ds(nth - 1, 1), :], self.prod[:], ACT.Copy).then_inc(self.s.hidden_hi, 1)

    def dve(self, dve, b, nth, banks, core, b0):
        dve.wait_ge(self.s.sig, nth)
        if not (isinstance(b, int) and b == 1):
            dve.wait_ge(self.s.hidden_lo, nth - 1)
        dve.tensor_tensor(self.gs[:], self.sg[:], banks[0], ALU.mult).then_inc(self.s.gated, 1)
        dve.wait_ge(self.s.gated, nth)
        dve.tensor_tensor(self.prod[:], self.gs[:], banks[1], ALU.mult).then_inc(core.block_out, 2)
        dve.wait_ge(self.s.hidden_hi, nth)
        h = bass.ds(nth - 1, 1)
        dve.tensor_tensor(self.hl[:, h, :], self.prod[:], self.hh[:, h, :].bitcast(F32), ALU.subtract).then_inc(self.s.hidden_lo, 1)


class Shift(Evac):

    def __init__(self, Z):
        self.Z = Z

    def setup(self, st, tag):
        self.tmp = [st.sb(f"{tag}tmp{i}", [P, T + 1]) for i in range(2)]
        self.diff = st.sb(tag + "diff", [P, T])
        self.s = st.sems("zeroed copied diffed", tag)

    def start(self, dve):
        for t in self.tmp:
            dve.memset(t[:, 0:1], 0.0).then_inc(self.s.zeroed, 1)

    def act(self, act, b, nth, banks, core, b0):
        jb = self.jb
        if not (isinstance(b, int) and b < 2):
            act.wait_ge(core.block_out, b0 + nth - 2)
        act.activation(self.tmp[jb % 2][:, 1:T + 1], banks[0], ACT.Copy).then_inc(self.s.copied, 1)

    def dve(self, dve, b, nth, banks, core, b0):
        tmp = self.tmp[self.jb % 2]
        if isinstance(b, int) and b == 0:
            dve.wait_ge(self.s.zeroed, 2)
        dve.wait_ge(self.s.copied, nth)
        if not (isinstance(b, int) and b == 0):
            dve.wait_ge(core.block_out, b0 + nth - 1)
        dve.tensor_tensor(self.diff[:], tmp[:, 0:T], banks[0], ALU.subtract).then_inc(self.s.diffed, 1)
        dve.wait_ge(self.s.diffed, nth)
        a, _ = PARAM_AT["mix"]
        dve.scalar_tensor_tensor(self.Z[:, bass.ds(b, 1), :], self.diff[:], core.params[:, bass.ds(b + a, 1)],
                                 tmp[:, 1:T + 1], ALU.mult, ALU.add).then_inc(core.block_out, 1)


SWAP = list(range(16, 32)) + list(range(16))


class Rope(Evac):

    def __init__(self, Z, off, scale=1.0):
        self.Z, self.off, self.scale = Z, off, scale

    def setup(self, st, tag):
        self.sw, self.sn, self.cs = (st.core.Y[0:32, i, :] for i in range(3))
        self.s = st.sems("copied swapped turned", tag)

    def act(self, act, b, nth, banks, core, b0):
        act.activation(self.Z[:, bass.ds(b + self.off, 1), :], banks[0], ACT.Copy, scale=self.scale).then_inc(self.s.copied, 1)

    def dve(self, dve, b, nth, banks, core, b0):
        r = slice(0, 32)
        if not (isinstance(b, int) and b == 0):
            dve.wait_ge(core.block_out, b0 + nth - 1)
        dve.wait_ge(self.s.copied, nth)
        dve.scalar_tensor_tensor(self.cs, banks[0][r], self.scale, core.const("ropec", r), ALU.mult, ALU.mult).then_inc(self.s.turned, 1)
        dve.stream_shuffle(self.sw, banks[0][r], SWAP).then_inc(self.s.swapped, 1)
        dve.wait_ge(self.s.swapped, nth)
        dve.scalar_tensor_tensor(self.sn, self.sw, self.scale, core.const("ropes", r), ALU.mult, ALU.mult).then_inc(self.s.turned, 1)
        dve.wait_ge(self.s.turned, 2 * nth)
        dve.tensor_tensor(self.Z[r, bass.ds(b + self.off, 1), :], self.cs, self.sn, ALU.add).then_inc(core.block_out, 1)


def gemm(st, segments, src, src_parts, U=1, split_src=True):
    core = st.core
    g = core.n_gemm
    w, kt, n_units = core.gemms[g]
    assert n_units == U * sum(n for n, _ in segments)
    u0, b0 = core.units, core.blocks
    group = 4 * U
    hi = [st.sb(f"w_hi{i}", [P, kt * P], F32R) for i in range(2)]
    lo = [st.sb(f"w_lo{i}", [P, kt * P], F32R) for i in range(2)]
    s = st.sems("src_hi src_ready")
    src_hi, src_lo = src_parts
    for i, (_, e) in enumerate(segments):
        e.setup(st, f"seg{i}_")
    block = st.block()
    KT = kt * U

    def walk(unit, out, eng):
        ub = 0
        for n, e in segments:
            def leave(it, jn, e=e, ub=ub):
                if out and jn % e.pair == 0:
                    nth = it * (4 // e.pair) + jn // e.pair
                    e.jb = (jn - 1) % 4
                    banks = [core.psum[(b0 + ub // U + jn - 1 - i) % 4] for i in range(e.pair)][::-1]
                    out(e, it * 4 + jn - 1, nth, banks, ub)

            def body(it, j, ub=ub, leave=leave):
                unit(it, j, ub)
                if j % U == 0 and not (at_start(it) and j == 0):
                    leave(it, j // U)
            in_groups(eng, n * U, group, body)
            leave((n - 1) // 4, (n - 1) % 4 + 1)
            ub += n * U

    @block.sync
    def _(sp):
        stream_weights(core, sp, g, lo=min(RING, n_units), base=u0)
        if g + 1 < len(core.gemms):
            stream_weights(core, sp, g + 1, hi=RING, base=u0 + n_units)

    def leaving(eng, part):
        def out(e, b, nth, banks, ub):
            f = e.act if part == "act" else e.dve
            if f:
                eng.wait_ge(core.unit_used, u0 + ub + nth * e.pair * U)
                f(eng, b, nth, banks, core, b0 + ub // U)
        return out

    @block.scalar
    def _(act):
        if split_src:
            for k in range(KT):
                act.activation(src_hi[:, k, :], src[:, k, :], ACT.Copy).then_inc(s.src_hi, 1)

        def unit(it, j, ub):
            at = u0 + ub + j
            act.wait_ge(core.w_landed[at % RING], 16 * (at // RING + 1) + it * (16 * group // RING))
            if at >= 2 or not at_start(it):
                act.wait_ge(core.unit_used, at - 1 + it * group)
            act.activation(hi[at % 2][:], core.raw[at % RING][:, 0:kt * P], ACT.Copy).then_inc(core.hi_ready, 1)
        walk(unit, leaving(act, "act"), act)

    @block.vector
    def _(dve):
        for _, e in segments:
            e.start(dve)
        if split_src:
            for k in range(KT):
                dve.wait_ge(s.src_hi, k + 1)
                dve.tensor_tensor(src_lo[:, k, :], src[:, k, :], src_hi[:, k, :].bitcast(F32),
                                  ALU.subtract).then_inc(s.src_ready, 1)

        def unit(it, j, ub):
            at = u0 + ub + j
            dve.wait_ge(core.hi_ready, at + 1 + it * group)
            dve.tensor_tensor(lo[at % 2][:], core.raw[at % RING][:, 0:kt * P], hi[at % 2][:].bitcast(F32),
                              ALU.subtract).then_inc(core.split_ready, 1)
        walk(unit, leaving(dve, "dve"), dve)

    @block.tensor
    def _(pe):
        def unit(it, j, ub):
            at = u0 + ub + j
            pe.wait_ge(core.split_ready, at + 1 + it * group)
            gb = b0 + (ub + j) // U
            bank = core.psum[gb % 4]
            if j % U == 0 and (gb >= BANKS or not at_start(it)):
                pe.wait_ge(core.block_out, gb - BANKS + 1 + it * 4)
            for k in range(kt):
                kk = (j % U) * kt + k
                if split_src and ub + j < U and at_start(it):
                    pe.wait_ge(s.src_ready, kk + 1)
                wh, wl = hi[at % 2][:, k * P:(k + 1) * P], lo[at % 2][:, k * P:(k + 1) * P]
                pe.matmul(bank, wh, src_hi[:, kk, :], start=kk == 0, stop=False)
                pe.matmul(bank, wh, src_lo[:, kk, :], start=False, stop=False)
                mm = pe.matmul(bank, wl, src_hi[:, kk, :], start=False, stop=kk == KT - 1)
            mm.then_inc(core.unit_used, 1)
        walk(unit, None, pe)

    core.units += n_units
    core.blocks += n_units // U
    core.n_gemm += 1


def layer_norm(core, gain, bias):
    X, Y = core.X, core.Y
    with Stage(core, "ln") as st:
        sq = st.sb("sq", [P, KD, T])
        std, rstd = st.sb("std", [P, T]), st.sb("rstd", [P, T])
        s = st.sems("mean centred squared var stdev inv scaled")
        mean, var = core.psum[4], core.psum[5]
        ones = core.const("ones")
        block = st.block()

        @block.tensor
        def _(pe):
            for k in range(KD):
                mm = pe.matmul(mean, ones, Y[:, k, :], start=k == 0, stop=k == KD - 1)
            mm.then_inc(s.mean, 1)
            for k in range(KD):
                pe.wait_ge(s.squared, k + 1)
                mm = pe.matmul(var, ones, sq[:, k, :], start=k == 0, stop=k == KD - 1)
            mm.then_inc(s.var, 1)

        @block.vector
        def _(dve):
            dve.wait_ge(s.mean, 1)
            for k in range(KD):
                done(dve, dve.scalar_tensor_tensor(Y[:, k, :], mean, -1.0 / D, Y[:, k, :], ALU.mult, ALU.add), s.centred)
            dve.wait_ge(s.stdev, 1)
            done(dve, dve.reciprocal(rstd[:], std[:]), s.inv)
            for k in range(KD):
                done(dve, dve.tensor_tensor(X[:, k, :], Y[:, k, :], rstd[:], ALU.mult), s.scaled)

        @block.scalar
        def _(act):
            for k in range(KD):
                act.wait_ge(s.centred, k + 1)
                done(act, act.activation(sq[:, k, :], Y[:, k, :], ACT.Square), s.squared)
            act.wait_ge(s.var, 1)
            done(act, act.activation(std[:], var, ACT.Sqrt, bias=core.eps_ln[:], scale=1.0 / D), s.stdev)
            for k in range(KD):
                act.wait_ge(s.scaled, k + 1)
                act.activation(X[:, k, :], X[:, k, :], ACT.Identity, bias=core.param(bias, k), scale=core.param(gain, k))


def rms_norm(core, src, gain, dst, add=False):
    with Stage(core, "rms") as st:
        sq = st.sb("sq", [P, KD, T])
        std, rstd = st.sb("std", [P, T]), st.sb("rstd", [P, T])
        s = st.sems("squared total stdev inv normed")
        total = core.psum[4]
        block = st.block()

        @block.tensor
        def _(pe):
            for k in range(KD):
                pe.wait_ge(s.squared, k + 1)
                mm = pe.matmul(total, core.const("ones"), sq[:, k, :], start=k == 0, stop=k == KD - 1)
            mm.then_inc(s.total, 1)

        @block.scalar
        def _(act):
            for k in range(KD):
                done(act, act.activation(sq[:, k, :], src[:, k, :], ACT.Square), s.squared)
            act.wait_ge(s.total, 1)
            done(act, act.activation(std[:], total, ACT.Sqrt, bias=core.eps_rms[:], scale=1.0 / D), s.stdev)

        @block.vector
        def _(dve):
            dve.wait_ge(s.stdev, 1)
            done(dve, dve.reciprocal(rstd[:], std[:]), s.inv)
            for k in range(KD):
                to = sq[:, k, :] if add else dst[:, k, :]
                done(dve, dve.scalar_tensor_tensor(to, src[:, k, :], core.param(gain, k), rstd[:], ALU.mult, ALU.mult), s.normed)
            for k in range(KD if add else 0):
                dve.wait_ge(s.normed, k + 1)
                dve.tensor_tensor(dst[:, k, :], dst[:, k, :], sq[:, k, :], ALU.add)


def attention(core, name, heads, kinds, bias=None):
    nc = core.nc
    G = len(kinds)
    H = len(heads)
    K = heads[0]["k"].shape[0]
    tiles = [(h, qb) for h in range(H) for qb in range(NT)]

    def span(kind, qb):
        return (max(0, qb - 1), qb + 1) if kind == "band" else (0, qb + 1)

    with Stage(core, name) as st:
        prob = st.sb("prob", [P, 2, G, T])
        probt = st.sb("probt", [P, 2, NT, T])
        vtok = st.sb("vtok", [P, 2, NT, K])
        mx, nm = st.sb("mx", [P, 2, 2]), st.sb("nm", [P, 2, 1])
        ssum, tot, inv = st.sb("ssum", [P, 2, 4]), st.sb("tot", [P, 2, 1]), st.sb("inv", [P, 2, 1])
        s = st.sems("scored maxed negmax expd summed inverted added prob_ready turned turned_out mixed mixed_out")
        turn, mix = core.psum[6], core.psum[7]
        block = st.block()
        ident = core.const("ident")

        def sbank(i, g):
            return core.psum[3 * (i % 2) + g]

        def turn_of(i):
            return i + i // NT + 2

        @block.tensor
        def _(pe):
            def score(i):
                h, qb = tiles[i]
                hd = heads[h]
                if i >= 2:
                    pe.wait_ge(s.expd, i - 1)
                for g, kind in enumerate(kinds):
                    a, b = span(kind, qb)
                    n = (b - a) * P
                    out = sbank(i, g)[:, 0:n]
                    pe.matmul(out, hd["q"][g][:, qb * P:(qb + 1) * P], hd["k"][:, a * P:b * P], start=True, stop=False)
                    if bias:
                        lhs, rhs = bias(h)
                        pe.matmul(out, lhs, rhs[:, a * P:b * P], start=False, stop=False)
                    idb = core.mask("identb")
                    if kind == "causal":
                        mm = pe.matmul(sbank(i, g)[:, n - P:n], idb, core.mask("causal"), start=False, stop=True)
                    elif kind == "band":
                        if qb:
                            pe.matmul(sbank(i, g)[:, 0:P], idb, core.mask("prev"), start=False, stop=False)
                        mm = pe.matmul(sbank(i, g)[:, n - P:n], idb, core.mask("causal"), start=False, stop=True)
                    else:
                        mm = pe.matmul(out, idb, core.mask(kind)[:, NT * P - n:], start=False, stop=True)
                mm.then_inc(s.scored, 1)

            score(0)
            for i, (h, qb) in enumerate(tiles):
                if i + 1 < len(tiles):
                    score(i + 1)
                v = heads[h]["v"]
                row = heads[h]["row"]
                rows = slice(row, row + K)
                if qb == 0:
                    if i:
                        pe.wait_ge(s.turned_out, turn_of(i) - 2)
                    for b in range(NT):
                        mm = pe.transpose(turn[:, b * K:(b + 1) * K], v[:, b * P:(b + 1) * P], ident[rows, row:row + K])
                    mm.then_inc(s.turned, 1)
                pe.wait_ge(s.turned_out, turn_of(i) - 1)
                pe.wait_ge(s.prob_ready, i + 1)
                for b in range(qb + 1):
                    mm = pe.transpose(turn[:, b * P:(b + 1) * P], prob[:, i % 2, G - 1, b * P:(b + 1) * P], ident)
                mm.then_inc(s.turned, 1)
                if qb == NT - 1:
                    pe.wait_ge(s.turned_out, turn_of(i))
                    if h:
                        pe.wait_ge(s.mixed_out, h)
                    for b in range(NT):
                        mm = pe.matmul(mix[rows, b * P:T], vtok[:, h % 2, b, :], probt[:, h % 2, b, b * P:T],
                                       start=b == 0, stop=b == NT - 1)
                    mm.then_inc(s.mixed, 1)

        @block.vector
        def _(dve):
            def top(i):
                h, qb = tiles[i]
                p = i % 2
                dve.wait_ge(s.scored, i + 1)
                if i >= 2:
                    dve.wait_ge(s.expd, i - 1)
                n = (qb + 1) * P
                if G == 1:
                    done(dve, dve.tensor_reduce(nm[:, p, :], sbank(i, 0)[:, 0:n], AX.X, ALU.max, negate=True), s.negmax)
                    return
                a, b = span(kinds[0], qb)
                done(dve, dve.tensor_reduce(mx[:, p, 0:1], sbank(i, 0)[:, 0:(b - a) * P], AX.X, ALU.max), s.maxed)
                done(dve, dve.tensor_reduce(mx[:, p, 1:2], core.banks[:, 3 * p + 1:3 * p + 3, 0:n], AX.XY, ALU.max), s.maxed)
                dve.wait_ge(s.maxed, 2 * i + 2)
                done(dve, dve.tensor_reduce(nm[:, p, :], mx[:, p, :], AX.X, ALU.max, negate=True), s.negmax)

            top(0)
            for i, (h, qb) in enumerate(tiles):
                if i + 1 < len(tiles):
                    top(i + 1)
                p = i % 2
                n = (qb + 1) * P
                dve.wait_ge(s.expd, i + 1)
                total = ssum[:, p, 0:1]
                last = prob[:, p, G - 1, 0:n]
                if G > 1:
                    total = tot[:, p, :]
                    done(dve, dve.tensor_reduce(total, ssum[:, p, 0:G], AX.X, ALU.add), s.summed)
                    done(dve, dve.tensor_tensor(last, last, prob[:, p, 1, 0:n], ALU.add), s.added)
                    dve.wait_ge(s.summed, i + 1)
                done(dve, dve.reciprocal(inv[:, p, :], total), s.inverted)
                if G > 1:
                    a, b = span(kinds[0], qb)
                    dve.wait_ge(s.added, 2 * i + 1)
                    part = prob[:, p, G - 1, a * P:b * P]
                    done(dve, dve.tensor_tensor(part, part, prob[:, p, 0, 0:(b - a) * P], ALU.add), s.added)
                    dve.wait_ge(s.added, 2 * i + 2)
                dve.wait_ge(s.inverted, i + 1)
                done(dve, dve.tensor_scalar(last, last, inv[:, p, :], None, ALU.mult), s.prob_ready)

        @block.scalar
        def _(act):
            def expo(i):
                h, qb = tiles[i]
                p = i % 2
                act.wait_ge(s.negmax, i + 1)
                if i >= 2:
                    act.wait_ge(s.turned, turn_of(i - 2))
                for g, kind in enumerate(kinds):
                    a, b = span(kind, qb)
                    n = (b - a) * P
                    e = act.activation(prob[:, p, g, 0:n], sbank(i, g)[:, 0:n], ACT.Exp, bias=nm[:, p, :],
                                       accum_out=ssum[:, p, g:g + 1])
                e.then_inc(s.expd, 1)

            expo(0)
            for i, (h, qb) in enumerate(tiles):
                if qb == 0:
                    act.wait_ge(s.turned, turn_of(i) - 1)
                    done(act, act.activation(vtok[:, h % 2, :, :], turn[:, 0:NT * K].rearrange("p (b k) -> p b k", k=K), ACT.Copy), s.turned_out)
                if i + 1 < len(tiles):
                    expo(i + 1)
                act.wait_ge(s.turned, turn_of(i))
                done(act, act.activation(probt[:, h % 2, 0:qb + 1, qb * P:(qb + 1) * P],
                               turn[:, 0:(qb + 1) * P].rearrange("p (b k) -> p b k", k=P), ACT.Copy), s.turned_out)
                if qb == NT - 1:
                    act.wait_ge(s.mixed, h + 1)
                    out = heads[h]["out"]
                    row = heads[h]["row"]
                    rows = slice(row, row + K)
                    done(act, act.activation(out, mix[rows, :], ACT.Copy), s.mixed_out)


DECAY = float(np.exp(-0.5))


def rwkv(core, Z, O):
    nc, Y = core.nc, core.Y
    heads = [(c, e) for c in range(4) for e in range(2)]
    half = lambda e: slice(64 * e, 64 * e + 64)
    chunked = lambda ap: ap.rearrange("p c (n t) -> p c n t", t=C)
    with Stage(core, "rwkv") as st:
        AR = st.sb("AR", [P, 4, NCH, 2, C])
        tokB, tokK, tokV = (st.sb(n, [P, 4, NCH, C]) for n in ("tokB", "tokK", "tokV"))
        Q = st.sb("Q", [P, 4, NCH, C])
        prod = [st.sb(f"prod{i}", [P, NCH, C]) for i in range(2)]
        elast = st.sb("elast", [P, 4, NCH])
        Hs = [st.sb(f"H{i}", [P, 4, C]) for i in range(2)]
        Dsb, SA = st.sb("D", [P, 4, C]), st.sb("SA", [P, 4, C])
        small = Y[:, 4:8, :]
        lora = lambda rows, c: small[rows, 0, c * P:(c + 1) * P]
        r, k, v = Z[:, 0:4, :], Z[:, 4:8, :], Z[:, 8:12, :]
        lw, a, kk = Z[:, 15:19, :], Z[:, 19:23, :], Z[:, 23:27, :]
        flat = lambda ap: ap[:].rearrange("p c n t -> p c (n t)")
        cum, norm, temp = flat(tokB), flat(tokK), flat(tokV)
        at, rt = AR[:, :, :, 0, :], AR[:, :, :, 1, :]
        bt, kt, bonus = kk, k, O[:, 0:4, :]
        Nt, X = chunked(kk), chunked(k)
        Arb, Aak, Ark = chunked(lw), chunked(a), chunked(r)
        XT = chunked(Y[:, 0:4, :])
        s = st.sems("small_in tanhed decay_in rate_in rate decay cum before e_before e_in e_neg elast_kept "
                    "kk_raw kk_squared kk_sum kk_clamped kk_root kk_inv kk_unit at_ready rate_less k_new rk rk_sum bonus_ready "
                    "b_ready bt_ready kt_ready rt_ready tok tok_out pairs masked n_left x_left x_first "
                    "q_ready q_out x_prod xt_prod x_next "
                    "d_ready d_out sa_ready sa_out h_ready h_sum h_out y_ready y_out "
                    "gate_sig gate mean centred squared var root inv y_scaled y_affine y_bonus")
        block = st.block()
        ident = core.const("ident")

        def level_products(pe, n, c):
            pe.wait_ge(s.q_out, n)
            if n > 2:
                pe.wait_ge(s.xt_prod, 2 * (n - 2))
            for i in range(NCH):
                for e in range(2):
                    cols = slice(i * C, (i + 1) * C)
                    pe.matmul(core.psum[2 + c % 2][half(e), cols], XT[half(e), c, i], Q[half(e), c, i], start=True, stop=True)
                    mm = pe.matmul(core.psum[4 + c % 2][half(e), cols], Q[half(e), c, i], XT[half(e), c, i], start=True, stop=True)
            mm.then_inc(s.x_prod, 1)

        @block.sync
        def _(sp):
            sp.dma_start(small, core.io["small"].rearrange("p (j t) -> p j t", t=T)).then_inc(s.small_in, 16)

        def lvl(name, i, n=NCH):
            m = core.const(name)[:, i * C:(i + 1) * C]
            return m.rearrange("p (o t) -> p o t", o=1).broadcast_to([P, n, C])

        @block.scalar
        def _(act):
            done(act, act.activation(Z[0:64, 12, :], Z[0:64, 12, :], ACT.Tanh), s.tanhed)
            for c in range(4):
                act.wait_ge(s.rate_in, c + 1)
                done(act, act.activation(a[:, c, :], core.psum[4 + c], ACT.Sigmoid, bias=core.param("a0", c)), s.rate)
            for c in range(4):
                act.wait_ge(s.decay_in, c + 1)
                done(act, act.activation(lw[:, c, :], core.psum[c], ACT.Sigmoid, bias=core.param("w0", c)), s.decay)
            act.wait_ge(s.kk_raw, 4)
            done(act, act.activation(norm, kk, ACT.Square), s.kk_squared)
            act.wait_ge(s.kk_clamped, 1)
            done(act, act.activation(norm, norm, ACT.Sqrt), s.kk_root)
            for c in range(4):
                act.wait_ge(s.cum, c + 1)
                done(act, act.activation(rt[:, c], tokB[:, c], ACT.Exp, scale=-DECAY), s.e_in)
            act.wait_ge(s.before, 1)
            for c in range(4):
                done(act, act.activation(at[:, c], chunked(lw)[:, c], ACT.Exp, scale=-DECAY), s.e_before)
            act.wait_ge(s.e_before, 4)
            done(act, act.activation(lw, cum, ACT.Exp, scale=DECAY), s.e_neg)
            for i, to in enumerate((tokV, tokB, tokK)):
                for c in range(4):
                    act.wait_ge(s.tok, 4 * i + c + 1)
                    done(act, act.activation(to[:, c], core.psum[4 + (4 * i + c) % 4].rearrange("p (n t) -> p n t", t=C), ACT.Copy), s.tok_out)
            for l in range(1, 6):
                for c in range(4):
                    act.wait_ge(s.q_ready, 4 * (l - 1) + c + 1)
                    done(act, act.activation(Q[:, c], core.psum[c % 2].rearrange("p (n t) -> p n t", t=C), ACT.Copy), s.q_out)
            for n in range(NCH):
                act.wait_ge(s.d_ready, n + 1)
                done(act, act.activation(Dsb[:], core.psum[0][:, 0:4 * C].rearrange("p (c t) -> p c t", t=C), ACT.Copy), s.d_out)
                act.wait_ge(s.sa_ready, n + 1)
                done(act, act.activation(SA[:], core.psum[1][:, 0:4 * C].rearrange("p (c t) -> p c t", t=C), ACT.Copy), s.sa_out)
                act.wait_ge(s.y_ready, n + 1)
                done(act, act.activation(at[:, :, n, :], core.psum[3][:, 0:4 * C].rearrange("p (c t) -> p c t", t=C), ACT.Copy), s.y_out)
            done(act, act.activation(Z[:, 13, :], Z[:, 13, :], ACT.Sigmoid), s.gate_sig)
            done(act, act.activation(Z[0:32, 14, :], Z[0:32, 14, :], ACT.Sigmoid), s.gate_sig)
            for c in range(4):
                act.wait_ge(s.centred, c + 1)
                done(act, act.activation(rt[:, c], at[:, c], ACT.Square), s.squared)
            for c in range(4):
                act.wait_ge(s.var, c + 1)
                done(act, act.activation(r[:, c, :], core.psum[c], ACT.Sqrt, bias=core.eps_gn[:], scale=1.0 / 64), s.root)

        @block.vector
        def _(dve):
            for c in range(4):
                done(dve, dve.tensor_scalar(kk[:, c, :], k[:, c, :], core.param("kk", c), None, ALU.mult), s.kk_raw)
            for c in range(4):
                dve.wait_ge(s.rate, c + 1)
                done(dve, dve.tensor_scalar(temp[:, c, :], a[:, c, :], -1.0, core.param("ka", c), ALU.add, ALU.mult), s.rate_less)
            dve.wait_ge(s.kk_squared, 1)
            dve.wait_ge(s.rate_less, 4)
            done(dve, dve.scalar_tensor_tensor(k, temp, 1.0, k, ALU.add, ALU.mult), s.k_new)
            for c in range(4):
                dve.wait_ge(s.decay, c + 1)
                done(dve, dve.tensor_tensor_scan(cum[:, c, :], core.const("chunk"), lw[:, c, :], 0.0, ALU.mult, ALU.add), s.cum)
            dve.wait_ge(s.cum, 4)
            done(dve, dve.tensor_tensor(lw, cum, lw, ALU.subtract), s.before)
            dve.wait_ge(s.kk_sum, 4)
            done(dve, dve.tensor_scalar(norm, core.banks[:, 4:8, :], 1e-24, None, ALU.max), s.kk_clamped)
            dve.wait_ge(s.k_new, 1)
            for c in range(4):
                done(dve, dve.scalar_tensor_tensor(temp[:, c, :], r[:, c, :], core.param("rk", c), k[:, c, :], ALU.mult, ALU.mult), s.rk)
            dve.wait_ge(s.kk_root, 1)
            done(dve, dve.reciprocal(norm, norm), s.kk_inv)
            done(dve, dve.tensor_tensor(kk, kk, norm, ALU.mult), s.kk_unit)
            dve.wait_ge(s.e_before, 4)
            done(dve, dve.scalar_tensor_tensor(at, chunked(kk), -1.0, at, ALU.mult, ALU.mult), s.at_ready)
            dve.wait_ge(s.e_in, 4)
            done(dve, dve.tensor_copy(elast[:], rt[:, :, :, C - 1]), s.elast_kept)
            done(dve, dve.tensor_tensor(rt, rt, chunked(r), ALU.mult), s.rt_ready)
            done(dve, dve.tensor_tensor(kk, kk, a, ALU.mult), s.b_ready)
            dve.wait_ge(s.e_neg, 1)
            done(dve, dve.tensor_tensor(bt, kk, lw, ALU.mult), s.bt_ready)
            done(dve, dve.tensor_tensor(kt, k, lw, ALU.mult), s.kt_ready)
            dve.wait_ge(s.rk_sum, 4)
            done(dve, dve.tensor_tensor(bonus, core.banks[:, 0:4, :], v, ALU.mult), s.bonus_ready)
            for c in range(4):
                dve.wait_ge(s.pairs, c + 1)
                dve.wait_ge(s.tok_out, 12)
                for i, to in enumerate((Nt, Arb, Aak, Ark, None)):
                    bank = core.psum[i].rearrange("p (n t) -> p n t", t=C)
                    m = core.const("rmask")[:, i * C:(i + 1) * C].rearrange("p (o t) -> p o t", o=1).broadcast_to([P, NCH, C])
                    out = to[:, c] if to is not None else prod[0][:]
                    done(dve, dve.tensor_tensor(out, bank, m, ALU.mult), s.masked)
                dve.wait_ge(s.masked, 5 * c + 5)
                eye = ident[:, 0:C]
                done(dve, dve.tensor_tensor(X[:, c], prod[0][:], lvl("lmaskt", 0), ALU.mult), s.n_left)
                done(dve, dve.tensor_tensor(XT[:, c], Nt[:, c], lvl("lmask", 0), ALU.mult), s.n_left)
                dve.wait_ge(s.n_left, 2 * c + 2)
                done(dve, dve.tensor_tensor(X[:, c], X[:, c], lvl("lmask", 6), ALU.add), s.x_first)
                done(dve, dve.tensor_tensor(XT[:, c], XT[:, c], lvl("lmask", 6), ALU.add), s.x_first)
            n = 0
            for l in range(1, 6):
                for c in range(4):
                    n += 1
                    view = lambda i: core.psum[i].rearrange("p (n t) -> p n t", t=C)
                    dve.wait_ge(s.x_prod, n)
                    done(dve, dve.tensor_tensor(prod[0][:], view(2 + c % 2), lvl("lmaskt", l), ALU.mult), s.xt_prod)
                    done(dve, dve.tensor_tensor(prod[1][:], view(4 + c % 2), lvl("lmask", l), ALU.mult), s.xt_prod)
                    dve.wait_ge(s.xt_prod, 2 * n)
                    done(dve, dve.tensor_tensor(X[:, c], X[:, c], prod[0][:], ALU.add), s.x_next)
                    done(dve, dve.tensor_tensor(XT[:, c], XT[:, c], prod[1][:], ALU.add), s.x_next)
            for n in range(NCH - 1):
                new, old = Hs[(n + 1) % 2], Hs[n % 2]
                dve.wait_ge(s.h_ready, n + 1)
                bank = core.psum[2][:, 0:4 * C].rearrange("p (c t) -> p c t", t=C)
                last = elast[:, :, n:n + 1].broadcast_to([P, 4, C])
                if n:
                    dve.wait_ge(s.y_ready, n)
                    done(dve, dve.tensor_tensor(new[:], bank, old[:], ALU.add), s.h_sum)
                    dve.wait_ge(s.h_sum, n)
                    done(dve, dve.tensor_tensor(new[:], new[:], last, ALU.mult), s.h_out)
                    dve.wait_ge(s.h_out, n + 1)
                else:
                    done(dve, dve.tensor_tensor(new[:], bank, last, ALU.mult), s.h_out)
                    dve.wait_ge(s.h_out, 1)
            for c in range(4):
                dve.wait_ge(s.mean, c + 1)
                bank = core.psum[c].rearrange("p (n t) -> p n t", t=C)
                done(dve, dve.scalar_tensor_tensor(at[:, c], bank, -1.0 / 64, at[:, c], ALU.mult, ALU.add), s.centred)
            for c in range(4):
                dve.wait_ge(s.root, c + 1)
                done(dve, dve.reciprocal(r[:, c, :], r[:, c, :]), s.inv)
                done(dve, dve.tensor_tensor(at[:, c], at[:, c], chunked(r)[:, c], ALU.mult), s.y_scaled)
                done(dve, dve.tensor_scalar(at[:, c], at[:, c], core.param("gng", c), core.param("gnb", c), ALU.mult, ALU.add), s.y_affine)
                o = chunked(O[:, 0:4, :])[:, c]
                done(dve, dve.tensor_tensor(o, o, at[:, c], ALU.add), s.y_bonus)
                dve.wait_ge(s.gate, c + 1)
                dve.tensor_tensor(O[:, c, :], O[:, c, :], core.psum[4 + c], ALU.mult)

        @block.tensor
        def _(pe):
            pe.wait_ge(s.small_in, 16)
            for c in range(4):
                pe.matmul(core.psum[4 + c], lora(slice(64, 128), c), Z[64:128, 12, :], start=True, stop=True).then_inc(s.rate_in, 1)
            pe.wait_ge(s.tanhed, 1)
            for c in range(4):
                pe.matmul(core.psum[c], lora(slice(0, 64), c), Z[0:64, 12, :], start=True, stop=True).then_inc(s.decay_in, 1)
            pe.wait_ge(s.kk_squared, 1)
            pe.wait_ge(s.rate, 4)
            for c in range(4):
                pe.matmul(core.psum[4 + c], core.const("blk"), norm[:, c, :], start=True, stop=True).then_inc(s.kk_sum, 1)
            pe.wait_ge(s.decay, 4)
            for c in range(4):
                pe.wait_ge(s.rk, c + 1)
                pe.matmul(core.psum[c], core.const("blk"), temp[:, c, :], start=True, stop=True).then_inc(s.rk_sum, 1)

            def tok(i, src):
                for c in range(4):
                    if i + c:
                        pe.wait_ge(s.tok_out, max(1, 4 * i + c - 3))
                    for n in range(NCH):
                        for e in range(2):
                            mm = pe.matmul(core.psum[4 + (4 * i + c) % 4][half(e), n * C:(n + 1) * C],
                                           src[half(e), c, n * C:(n + 1) * C], ident[half(e), 64 * e:64 * e + 64], start=True, stop=True)
                    mm.then_inc(s.tok, 1)

            pe.wait_ge(s.kk_clamped, 1)
            tok(0, v)
            pe.wait_ge(s.bt_ready, 1)
            tok(1, bt)
            pe.wait_ge(s.kt_ready, 1)
            tok(2, kt)
            pe.wait_ge(s.at_ready, 1)
            pe.wait_ge(s.rt_ready, 1)
            pe.wait_ge(s.bonus_ready, 1)
            pe.wait_ge(s.tok_out, 12)
            for c in range(4):
                if c:
                    pe.wait_ge(s.masked, 5 * c)
                for n in range(NCH):
                    for e in range(2):
                        cols = slice(n * C, (n + 1) * C)
                        ae, re = AR[half(e), c, n, 0, :], AR[half(e), c, n, 1, :]
                        be, ke = bt[half(e), c, cols], kt[half(e), c, cols]
                        for i, (lhs, rhs) in enumerate(((be, ae), (be, re), (ke, ae), (ke, re), (ae, be))):
                            mm = pe.matmul(core.psum[i][half(e), cols], lhs, rhs, start=True, stop=True)
                mm.then_inc(s.pairs, 1)
            n = 0
            pe.wait_ge(s.masked, 20)
            for l in range(1, 6):
                for c in range(4):
                    n += 1
                    pe.wait_ge(s.x_first, 2 * c + 2)
                    if l > 1:
                        pe.wait_ge(s.x_next, 2 * (4 * (l - 2) + c) + 2)
                    if n > 2:
                        pe.wait_ge(s.q_out, n - 2)
                    for i in range(NCH):
                        for e in range(2):
                            mm = pe.matmul(core.psum[c % 2][half(e), i * C:(i + 1) * C], Nt[half(e), c, i], X[half(e), c, i], start=True, stop=True)
                    mm.then_inc(s.q_ready, 1)
                    if n > 1:
                        level_products(pe, n - 1, (c - 1) % 4)
            level_products(pe, n, 3)
            pe.wait_ge(s.x_next, 40)
            for n in range(NCH):
                H = Hs[n % 2]
                if n:
                    pe.wait_ge(s.h_out, n)
                    pe.wait_ge(s.d_out, n)
                for c, e in heads:
                    out = core.psum[0][half(e), c * C:(c + 1) * C]
                    if n:
                        pe.matmul(out, AR[half(e), c, n, 0, :], H[half(e), c, :], start=True, stop=False)
                    mm = pe.matmul(out, Aak[half(e), c, n], tokV[half(e), c, n], start=n == 0, stop=True)
                mm.then_inc(s.d_ready, 1)
                pe.wait_ge(s.d_out, n + 1)
                if n:
                    pe.wait_ge(s.sa_out, n)
                for c, e in heads:
                    mm = pe.matmul(core.psum[1][half(e), c * C:(c + 1) * C], XT[half(e), c, n], Dsb[half(e), c, :], start=True, stop=True)
                mm.then_inc(s.sa_ready, 1)
                pe.wait_ge(s.sa_out, n + 1)
                if n < NCH - 1:
                    for c, e in heads:
                        out = core.psum[2][half(e), c * C:(c + 1) * C]
                        pe.matmul(out, tokK[half(e), c, n], tokV[half(e), c, n], start=True, stop=False)
                        mm = pe.matmul(out, tokB[half(e), c, n], SA[half(e), c, :], start=False, stop=True)
                    mm.then_inc(s.h_ready, 1)
                if n:
                    pe.wait_ge(s.y_out, n)
                for c, e in heads:
                    out = core.psum[3][half(e), c * C:(c + 1) * C]
                    pe.matmul(out, tokV[half(e), c, n], Ark[half(e), c, n], start=True, stop=False)
                    if n:
                        pe.matmul(out, H[half(e), c, :], AR[half(e), c, n, 1, :], start=False, stop=False)
                    mm = pe.matmul(out, SA[half(e), c, :], Arb[half(e), c, n], start=False, stop=True)
                mm.then_inc(s.y_ready, 1)
            pe.wait_ge(s.gate_sig, 2)
            for c in range(4):
                pe.matmul(core.psum[4 + c], small[:, 1, c * P:(c + 1) * P], Z[:, 13, :], start=True, stop=False)
                pe.matmul(core.psum[4 + c], small[0:32, 2, c * P:(c + 1) * P], Z[0:32, 14, :], start=False, stop=True).then_inc(s.gate, 1)
            for c in range(4):
                pe.wait_ge(s.y_out, NCH)
                pe.matmul(core.psum[c], core.const("blk"), at[:, c], start=True, stop=True).then_inc(s.mean, 1)
            for c in range(4):
                pe.wait_ge(s.squared, c + 1)
                pe.matmul(core.psum[c], core.const("blk"), rt[:, c], start=True, stop=True).then_inc(s.var, 1)




def gate_rows(core, Z, G):
    with Stage(core, "gates") as st:
        x, l = st.sb("x", [P, T]), st.sb("l", [P, T])
        s = st.sems("biased part ln logsig summed moved source maxed out")
        block = st.block()
        ml = slice(32, 36)

        @block.scalar
        def _(act):
            done(act, act.activation(x[:], Z[:, 24, :], ACT.Identity, bias=core.param("gateb")), s.biased)
            done(act, act.activation(l[:], x[:], ACT.Abs), s.part)
            done(act, act.activation(l[:], l[:], ACT.Exp, scale=-1.0), s.part)
            done(act, act.activation(l[:], l[:], ACT.Ln, bias=1.0), s.ln)

        @block.vector
        def _(dve):
            dve.wait_ge(s.ln, 1)
            done(dve, dve.scalar_tensor_tensor(l[:], x[:], 0.0, l[:], ALU.min, ALU.subtract), s.logsig)
            one = core.const("ones")[:, 0:1].broadcast_to([P, T])
            done(dve, dve.tensor_tensor_scan(G[:, 1, :], one, l[:], 0.0, ALU.mult, ALU.add), s.summed)
            done(dve, dve.tensor_copy(l[ml], G[64:68, 1, :]), s.moved)
            done(dve, dve.tensor_tensor(G[ml, 0, :], x[ml], l[ml], ALU.subtract), s.source)
            done(dve, dve.tensor_tensor_scan(x[ml], G[ml, 0, :], G[ml, 0, :], 0.0, ALU.max, ALU.max), s.maxed)
            done(dve, dve.tensor_scalar(G[0:4, 1, :], G[0:4, 1, :], -1.0, None, ALU.mult), s.out)
            done(dve, dve.tensor_scalar(G[ml, 2, :], x[ml], -1.0, None, ALU.mult), s.out)
            done(dve, dve.scalar_tensor_tensor(G[ml, 3, :], l[ml], -1.0, G[ml, 2, :], ALU.mult, ALU.add), s.out)


def mlstm(core, Z, G):
    Y = core.Y
    with Stage(core, "mlstm") as st:
        conv = st.sb("conv", [P, 4, T])
        sig = st.sb("sig", [P, 4, T])
        vtok = st.sb("vtok", [P, 2, NT, P])
        gtok = st.sb("gtok", [P, NT, 4])
        E, PT = (st.sb(n, [P, 2, T]) for n in ("E", "PT"))
        low, den = st.sb("low", [P, T]), st.sb("den", [P, T])
        s = st.sems("conv sig silu vt vt_out gt gt_out scores weight weight_done heads_sum lows low_out den_out inv h_out")
        items = [(h, j) for h in range(4) for j in range(NT)]
        rows = lambda e: slice(64 * e, 64 * e + 64)
        block = st.block()

        @block.vector
        def _(dve):
            for c in range(4):
                tap = lambda j: core.param("conv", 4 * c + j)
                done(dve, dve.tensor_scalar(conv[:, c, :], Z[:, 16 + c, :], tap(3), None, ALU.mult), s.conv)
                for back in (1, 2, 3):
                    done(dve, dve.scalar_tensor_tensor(conv[:, c, back:], Z[:, 16 + c, 0:T - back], tap(3 - back), conv[:, c, back:],
                                                       ALU.mult, ALU.add), s.conv)
            for c in range(4):
                dve.wait_ge(s.sig, c + 1)
                scale = 1.0 if c < 2 else 64 ** -0.5
                done(dve, dve.scalar_tensor_tensor(conv[:, c, :], conv[:, c, :], scale, sig[:, c, :], ALU.mult, ALU.mult), s.silu)
            for i, (h, j) in enumerate(items):
                n = T - j * P
                dve.wait_ge(s.weight, i + 1)
                dve.wait_ge(s.scores, i + 1)
                if i >= 2:
                    dve.wait_ge(s.heads_sum, i - 1)
                done(dve, dve.tensor_tensor(PT[:, i % 2, 0:n], E[:, i % 2, 0:n], core.psum[i % 2][:, 0:n], ALU.mult), s.weight_done)
                if i % 8 == 7:
                    c = h // 2
                    dve.wait_ge(s.heads_sum, i + 1)
                    dve.wait_ge(s.low_out, 2 * c + 2)
                    done(dve, dve.tensor_tensor(den[:], den[:], low[:], ALU.max), s.den_out)
                    done(dve, dve.reciprocal(den[:], den[:]), s.inv)
                    done(dve, dve.tensor_tensor(Y[:, 6 + c, :], core.psum[4], den[:], ALU.mult), s.h_out)

        @block.scalar
        def _(act):
            for c in range(2):
                act.wait_ge(s.vt, c + 1)
                done(act, act.activation(vtok[:, c], core.psum[7].rearrange("p (b k) -> p b k", k=P), ACT.Copy), s.vt_out)
            act.wait_ge(s.gt, 1)
            done(act, act.activation(gtok[:], core.psum[6][:, 0:4 * NT].rearrange("p (b k) -> p b k", k=4), ACT.Copy), s.gt_out)
            for c in range(4):
                act.wait_ge(s.conv, 4 * c + 4)
                done(act, act.activation(sig[:, c, :], conv[:, c, :], ACT.Sigmoid), s.sig)
            for i, (h, j) in enumerate(items):
                n = T - j * P
                act.wait_ge(s.scores, i + 1)
                if i >= 2:
                    act.wait_ge(s.weight_done, i - 1)
                done(act, act.activation(E[:, i % 2, 0:n], core.psum[2 + i % 2][:, 0:n], ACT.Exp, bias=gtok[:, j, h:h + 1]), s.weight)
                if i % 8 == 7:
                    act.wait_ge(s.lows, h // 2 + 1)
                    if h > 1:
                        act.wait_ge(s.h_out, h // 2)
                    done(act, act.activation(low[:], core.psum[6], ACT.Exp), s.low_out)
                    act.wait_ge(s.heads_sum, i + 1)
                    done(act, act.activation(den[:], core.psum[5], ACT.Abs), s.low_out)

        @block.tensor
        def _(pe):
            ident = core.const("ident")
            for c in range(2):
                if c:
                    pe.wait_ge(s.vt_out, c)
                for b in range(NT):
                    mm = pe.transpose(core.psum[7][:, b * P:(b + 1) * P], Z[:, 20 + c, b * P:(b + 1) * P], ident)
                mm.then_inc(s.vt, 1)
            ml = slice(32, 36)
            for b in range(NT):
                mm = pe.matmul(core.psum[6][:, 4 * b:4 * b + 4], G[ml, 0, b * P:(b + 1) * P], ident[ml, 32:36], start=True, stop=True)
            mm.then_inc(s.gt, 1)
            pe.wait_ge(s.silu, 4)
            pe.wait_ge(s.gt_out, 1)
            pe.wait_ge(s.vt_out, 2)
            sel = core.const("sel").rearrange("p (h k) -> p h k", k=P)

            def score(i):
                h, j = items[i]
                c, e = h // 2, h % 2
                if i >= 2:
                    pe.wait_ge(s.weight_done, i - 1)
                n = T - j * P
                pe.matmul(core.psum[i % 2][:, 0:n], conv[rows(e), 2 + c, j * P:(j + 1) * P], conv[rows(e), c, j * P:T], start=True, stop=True)
                pe.matmul(core.psum[2 + i % 2][:, 0:n], sel[ml, h, :], G[ml, 2, j * P:T], start=True, stop=False)
                pe.matmul(core.psum[2 + i % 2][:, 0:P], core.mask("identb"), core.mask("prev"), start=False, stop=True).then_inc(s.scores, 1)

            score(0)
            for i, (h, j) in enumerate(items):
                c, e = h // 2, h % 2
                if i + 1 < len(items):
                    score(i + 1)
                if i % 8 == 0 and c:
                    pe.wait_ge(s.h_out, c)
                pe.wait_ge(s.weight_done, i + 1)
                n = T - j * P
                cols = slice(j * P, T)
                if i % 8 == 7:
                    for ee in range(2):
                        mm = pe.matmul(core.psum[6][rows(ee), :], sel[ml, 2 * c + ee, 0:64], G[ml, 3, :], start=True, stop=True)
                    mm.then_inc(s.lows, 1)
                pe.matmul(core.psum[4][rows(e), cols], vtok[:, c, j, rows(e)], PT[:, i % 2, 0:n], start=j == 0, stop=j == NT - 1)
                pe.matmul(core.psum[5][rows(e), cols], core.const("ones")[:, 0:64], PT[:, i % 2, 0:n], start=j == 0,
                          stop=j == NT - 1).then_inc(s.heads_sum, 1)


def hgrn2(core, Z):
    Y = core.Y
    with Stage(core, "hgrn") as st:
        b, kk, tmp, qe, ke = (st.sb(n, [P, 2, T]) for n in ("b", "k", "tmp", "qe", "ke"))
        W = [st.sb(f"W{i}", [P, 2, T]) for i in range(2)]
        S, part = st.sb("S", [P, 2, NCH, C]), st.sb("part", [P, 2, NCH, C])
        tokV, tokK = (st.sb(n, [P, 2, NCH, C]) for n in ("tokV", "tokK"))
        elast = st.sb("elast", [P, 2, NCH])
        H = [st.sb(f"H{i}", [P, 2, C]) for i in range(2)]
        Hd = st.sb("Hd", [P, 2, C])
        s = st.sems("part k ln logsig b eb ebdone rest eke ke_done qe_done last delta expd half w_ready pairs masked summed "
                    "tok tok_out h_ready h_decayed h_out o_ready o_out")
        q, f, v = Z[:, 2:4, :], Z[:, 4:6, :], Z[:, 6:8, :]
        half = lambda e: slice(64 * e, 64 * e + 64)
        levels = (1, 2, 4, 8, 16, 32)
        chunks = lambda ap: ap.rearrange("p c (n t) -> p c n t", t=C)
        blocks = lambda ap, m: ap.rearrange("p c (n u) -> p (c n) u", u=2 * m)
        block = st.block()
        ident = core.const("ident")

        @block.scalar
        def _(act):
            done(act, act.activation(kk[:], f, ACT.Sigmoid, scale=-1.0), s.k)
            done(act, act.activation(tmp[:], f, ACT.Abs), s.part)
            done(act, act.activation(tmp[:], tmp[:], ACT.Exp, scale=-1.0), s.part)
            done(act, act.activation(tmp[:], tmp[:], ACT.Ln, bias=1.0), s.ln)
            act.wait_ge(s.b, 2)
            done(act, act.activation(qe[:], b[:], ACT.Exp), s.eb)
            act.wait_ge(s.rest, 1)
            done(act, act.activation(ke[:], ke[:], ACT.Exp), s.eke)
            for i, m in enumerate(levels):
                w, d = blocks(W[i % 2][:], m), blocks(tmp[:], m)
                act.wait_ge(s.delta, i + 1)
                if i >= 2:
                    act.wait_ge(s.pairs, i)
                done(act, act.activation(w[:, :, 0:m], d[:, :, 0:m], ACT.Exp, scale=-1.0), s.expd)
                done(act, act.activation(w[:, :, m:], d[:, :, m:], ACT.Exp), s.expd)
            for i in range(4):
                act.wait_ge(s.tok, i + 1)
                to = (tokV, tokK)[i // 2]
                done(act, act.activation(to[:, i % 2], core.psum[4 + i].rearrange("p (n t) -> p n t", t=C), ACT.Copy), s.tok_out)
            act.wait_ge(s.o_ready, NCH)
            for c in range(2):
                done(act, act.activation(Y[:, 2 + c, :], core.psum[4 + c], ACT.Copy), s.o_out)

        @block.vector
        def _(dve):
            dve.wait_ge(s.ln, 1)
            done(dve, dve.scalar_tensor_tensor(tmp[:], f, 0.0, tmp[:], ALU.min, ALU.subtract), s.logsig)
            for c in range(2):
                done(dve, dve.tensor_tensor_scan(b[:, c, :], core.const("chunk"), tmp[:, c, :], 0.0, ALU.mult, ALU.add), s.b)
            b64 = blocks(b[:], 32)
            done(dve, dve.tensor_tensor(blocks(ke[:], 32), b64[:, :, C - 1:C].broadcast_to([P, 2 * NCH, C]), b64, ALU.subtract), s.rest)
            dve.wait_ge(s.eb, 1)
            done(dve, dve.tensor_copy(elast[:], chunks(qe[:])[:, :, :, C - 1]), s.last)
            done(dve, dve.tensor_tensor(qe[:], qe[:], q, ALU.mult), s.qe_done)
            dve.wait_ge(s.eke, 1)
            done(dve, dve.tensor_tensor(ke[:], ke[:], kk[:], ALU.mult), s.ke_done)

            def gather(i):
                dve.wait_ge(s.pairs, i + 1)
                m = 6 if i == 0 else i - 1
                mask = core.const("lmask")[:, m * C:(m + 1) * C].rearrange("p (o t) -> p o t", o=1).broadcast_to([P, 2 * NCH, C])
                bank = core.banks[:, 2 * (i % 2):2 * (i % 2) + 2, :].rearrange("p c (n t) -> p (c n) t", t=C)
                to = S if i == 0 else part
                done(dve, dve.tensor_tensor(to[:].rearrange("p c n t -> p (c n) t"), bank, mask, ALU.mult), s.masked)
                if i:
                    done(dve, dve.tensor_tensor(S[:], S[:], part[:], ALU.add), s.summed)

            for i, m in enumerate(levels):
                w, d, bb = blocks(W[i % 2][:], m), blocks(tmp[:], m), blocks(b[:], m)
                if i:
                    dve.wait_ge(s.expd, 2 * i)
                done(dve, dve.tensor_tensor(d, bb, bb[:, :, m - 1:m].broadcast_to([P, T // m, 2 * m]), ALU.subtract), s.delta)
                dve.wait_ge(s.expd, 2 * i + 2)
                done(dve, dve.tensor_tensor(w[:, :, 0:m], w[:, :, 0:m], blocks(kk[:], m)[:, :, 0:m], ALU.mult), s.half)
                done(dve, dve.tensor_tensor(w[:, :, m:], w[:, :, m:], blocks(q, m)[:, :, m:], ALU.mult), s.w_ready)
                gather(i)
            gather(6)
            for n in range(NCH - 1):
                new, old = H[(n + 1) % 2], H[n % 2]
                bank = core.psum[6 + n % 2][:, 0:2 * C].rearrange("p (c t) -> p c t", t=C)
                if n:
                    done(dve, dve.tensor_tensor(Hd[:], old[:], elast[:, :, n:n + 1].broadcast_to([P, 2, C]), ALU.mult), s.h_decayed)
                dve.wait_ge(s.h_ready, n + 1)
                if n:
                    dve.wait_ge(s.o_ready, n)
                    done(dve, dve.tensor_tensor(new[:], bank, Hd[:], ALU.add), s.h_out)
                else:
                    done(dve, dve.tensor_copy(new[:], bank), s.h_out)

        @block.tensor
        def _(pe):
            def pairs(i, lhs, rhs):
                if i >= 2:
                    pe.wait_ge(s.masked, i - 1)
                for c in range(2):
                    for n in range(NCH):
                        for e in range(2):
                            cols = slice(n * C, (n + 1) * C)
                            mm = pe.matmul(core.psum[2 * (i % 2) + c][half(e), cols], lhs[half(e), c, cols], rhs[half(e), c, cols], start=True, stop=True)
                mm.then_inc(s.pairs, 1)

            def tok(i, src, c):
                for n in range(NCH):
                    for e in range(2):
                        mm = pe.matmul(core.psum[4 + i][half(e), n * C:(n + 1) * C], src[half(e), c, n * C:(n + 1) * C],
                                       ident[half(e), 64 * e:64 * e + 64], start=True, stop=True)
                mm.then_inc(s.tok, 1)

            tok(0, v, 0)
            tok(1, v, 1)
            pe.wait_ge(s.k, 1)
            pairs(0, kk, q)
            pe.wait_ge(s.ke_done, 1)
            tok(2, ke, 0)
            tok(3, ke, 1)
            for i in range(6):
                pe.wait_ge(s.w_ready, i + 1)
                pairs(i + 1, W[i % 2], W[i % 2])
            pe.wait_ge(s.summed, 6)
            pe.wait_ge(s.qe_done, 1)
            pe.wait_ge(s.tok_out, 4)
            for n in range(NCH):
                if n < NCH - 1:
                    for c in range(2):
                        for e in range(2):
                            mm = pe.matmul(core.psum[6 + n % 2][half(e), c * C:(c + 1) * C], tokK[half(e), c, n], tokV[half(e), c, n], start=True, stop=True)
                    mm.then_inc(s.h_ready, 1)
                if n:
                    pe.wait_ge(s.h_out, n)
                for c in range(2):
                    for e in range(2):
                        cols = slice(n * C, (n + 1) * C)
                        out = core.psum[4 + c][half(e), cols]
                        mm = pe.matmul(out, tokV[half(e), c, n], S[half(e), c, n], start=True, stop=n == 0)
                        if n:
                            mm = pe.matmul(out, H[n % 2][half(e), c, :], qe[half(e), c, cols], start=False, stop=True)
                mm.then_inc(s.o_ready, 1)


TWO_PI_HI = 6.28125
TWO_PI_LO = 2 * np.pi - TWO_PI_HI
ROUND = 1.5 * 2.0 ** 23
PI_BELOW = 3.1415925


def s5(core, Z):
    Y = core.Y
    with Stage(core, "s5") as st:
        cs, sn = st.sb("cos", [P, 8, T]), st.sb("sin", [P, 8, T])
        names = "lr dt mag th k r r2 co si den abr abi t1 t2 cfr cfi"
        v = {n: st.sb(n, [P, 8]) for n in names.split()}
        bbr, bbi, tb = (st.sb(n, [P, 8, 16]) for n in ("bbr", "bbi", "tb"))
        big = st.sb("big", [P, 8, P])
        BT = [st.sb(n, [P, 8, P]) for n in ("BTr", "BTi")]
        s = st.sems("wglu_in dt mag angle cossin spread spread_t bt_out bu_ready bu_out scan x_ready x_used u_out "
                    "damping steps tanh_in tanhed gelu glu sigm glued sq total root")
        m3 = lambda ap: ap.rearrange("p (j q) -> p j q", j=8)
        one = lambda t: v[t][:]
        block = st.block()
        u = Z[:, 0:2, :]
        smask = m3(core.const("s5mask"))
        wide = lambda ap: ap.rearrange("p j (g q) -> p j g q", q=16)
        ring = [st.sb(f"ring{i}", [P, 4, T]) for i in range(1)]
        C_spread = [st.sb(n, [P, 8, P]) for n in ("Cr", "Ci")]
        small = st.sb("wglu", [P, 512])

        @block.sync
        def _(sp):
            a, b = SMALL_AT["wglu"]
            sp.dma_start(small[:], core.io["small"][:, a:b]).then_inc(s.wglu_in, 16)

        @block.scalar
        def _(act):
            done(act, act.activation(one("dt"), core.param("ldt"), ACT.Exp), s.dt)
            act.wait_ge(s.damping, 1)
            done(act, act.activation(one("mag"), one("mag"), ACT.Exp), s.mag)
            act.wait_ge(s.angle, 1)
            done(act, act.activation(one("si"), one("r"), ACT.Sin), s.cossin)
            done(act, act.activation(one("co"), one("r2"), ACT.Sin), s.cossin)
            for i in range(2):
                for q in range(2):
                    act.wait_ge(s.spread_t, 2 * i + q + 1)
                    done(act, act.activation(BT[i][:, 4 * q:4 * q + 4, :], core.psum[q].rearrange("p (j k) -> p j k", k=P), ACT.Copy), s.bt_out)
            for j in range(2):
                act.wait_ge(s.tanh_in, j + 1)
                done(act, act.activation(sn[:, j, :], sn[:, j, :], ACT.Tanh, scale=float(np.sqrt(2 / np.pi))), s.tanhed)
            for j in range(2):
                act.wait_ge(s.glu, j + 1)
                done(act, act.activation(sn[:, j, :], core.psum[4 + j], ACT.Sigmoid), s.sigm)
            for j in range(2):
                act.wait_ge(s.glued, j + 1)
                done(act, act.activation(sn[:, 2 + j, :], Y[:, j, :], ACT.Square), s.sq)
            act.wait_ge(s.total, 1)
            done(act, act.activation(sn[:, 4, :], core.psum[6], ACT.Sqrt, bias=core.eps_rms[:], scale=1.0 / 256), s.root)

        @block.vector
        def _(dve):
            def tt(out, a, b, op, sem=s.steps):
                done(dve, dve.tensor_tensor(out, a, b, op), sem)

            def ts(out, a, x, y, op0, op1=None, sem=s.steps):
                done(dve, dve.tensor_scalar(out, a, x, y, op0, op1) if op1 is not None else dve.tensor_scalar(out, a, x, y, op0), sem)

            li = core.param("lim")
            ts(one("lr"), core.param("lre"), -1e-4, None, ALU.min)
            dve.wait_ge(s.dt, 1)
            tt(one("mag"), one("lr"), one("dt"), ALU.mult, s.damping)
            tt(one("th"), li, one("dt"), ALU.mult)
            ts(one("k"), one("th"), 1 / (2 * np.pi), ROUND, ALU.mult, ALU.add)
            ts(one("k"), one("k"), -ROUND, None, ALU.add)
            done(dve, dve.scalar_tensor_tensor(one("r"), one("k"), -TWO_PI_HI, one("th"), ALU.mult, ALU.add), s.steps)
            done(dve, dve.scalar_tensor_tensor(one("r"), one("k"), -TWO_PI_LO, one("r"), ALU.mult, ALU.add), s.steps)
            ts(one("r"), one("r"), PI_BELOW, -PI_BELOW, ALU.min, ALU.max)
            ts(one("r2"), one("r"), float(np.pi / 2), None, ALU.add)
            ts(one("k"), one("r2"), PI_BELOW, -2 * np.pi, ALU.is_gt, ALU.mult)
            tt(one("r2"), one("r2"), one("k"), ALU.add)
            ts(one("r2"), one("r2"), PI_BELOW, -PI_BELOW, ALU.min, ALU.max, s.angle)
            dve.wait_ge(s.cossin, 2)
            dve.wait_ge(s.mag, 1)
            tt(one("abr"), one("mag"), one("co"), ALU.mult)
            tt(one("abi"), one("mag"), one("si"), ALU.mult)
            tt(one("t1"), one("lr"), one("lr"), ALU.mult)
            tt(one("t2"), li, li, ALU.mult)
            tt(one("den"), one("t1"), one("t2"), ALU.add)
            done(dve, dve.reciprocal(one("den"), one("den")), s.steps)
            ts(one("abr"), one("abr"), -1.0, None, ALU.add)
            tt(one("t1"), one("abr"), one("lr"), ALU.mult)
            tt(one("t2"), one("abi"), li, ALU.mult)
            tt(one("cfr"), one("t1"), one("t2"), ALU.add)
            tt(one("cfr"), one("cfr"), one("den"), ALU.mult)
            tt(one("t1"), one("abi"), one("lr"), ALU.mult)
            tt(one("t2"), one("abr"), li, ALU.mult)
            tt(one("cfi"), one("t1"), one("t2"), ALU.subtract)
            tt(one("cfi"), one("cfi"), one("den"), ALU.mult)
            cf = lambda n: v[n][:].rearrange("p (j o) -> p j o", o=1).broadcast_to([P, 8, 16])
            bre, bim = m3(core.param("bre")), m3(core.param("bim"))
            tt(bbr[:], bre, cf("cfr"), ALU.mult)
            tt(tb[:], bim, cf("cfi"), ALU.mult)
            tt(bbr[:], bbr[:], tb[:], ALU.subtract)
            tt(bbi[:], bim, cf("cfr"), ALU.mult)
            tt(tb[:], bre, cf("cfi"), ALU.mult)
            tt(bbi[:], bbi[:], tb[:], ALU.add)

            def spread(out, src, j, scale=1.0, sem=s.steps):
                o = out[:, j, :].rearrange("p (g q) -> p g q", q=16)
                done(dve, dve.scalar_tensor_tensor(o, src[:, j:j + 1, :].broadcast_to([P, 8, 16]), scale,
                                                   smask[:, j, :].rearrange("p (g q) -> p g q", q=16), ALU.mult, ALU.mult), sem)
            for i, src in enumerate((bbr, bbi)):
                if i:
                    dve.wait_ge(s.spread_t, 2)
                for j in range(8):
                    spread(big, src, j, 1.0, s.spread)
            for j in range(8):
                spread(C_spread[0], m3(core.param("cre")), j)
                spread(C_spread[1], m3(core.param("cim")), j, -1.0)
            done(dve, dve.memset(cs[:, :, 0:1], 1.0), s.steps)
            done(dve, dve.memset(sn[:, :, 0:1], 0.0), s.steps)
            done(dve, dve.tensor_copy(cs[:, :, 1], one("co")), s.steps)
            done(dve, dve.tensor_copy(sn[:, :, 1], one("si")), s.steps)
            n = 2
            while n < T:
                a, b2 = cs[:, :, n - 1], sn[:, :, n - 1]
                tt(one("t1"), a, one("co"), ALU.mult)
                tt(one("t2"), b2, one("si"), ALU.mult)
                tt(one("r"), one("t1"), one("t2"), ALU.subtract)
                tt(one("t1"), a, one("si"), ALU.mult)
                tt(one("t2"), b2, one("co"), ALU.mult)
                tt(one("r2"), one("t1"), one("t2"), ALU.add)
                pc = v["r"][:].rearrange("p (j o) -> p j o", o=1).broadcast_to([P, 8, n])
                ps = v["r2"][:].rearrange("p (j o) -> p j o", o=1).broadcast_to([P, 8, n])
                lo_, hi_ = slice(0, n), slice(n, 2 * n)
                t = ring[0][:].rearrange("p a t -> p (a t)")[:, 0:8 * n].rearrange("p (j t) -> p j t", j=8)
                tt(cs[:, :, hi_], cs[:, :, lo_], pc, ALU.mult)
                tt(t, sn[:, :, lo_], ps, ALU.mult)
                tt(cs[:, :, hi_], cs[:, :, hi_], t, ALU.subtract)
                tt(sn[:, :, hi_], cs[:, :, lo_], ps, ALU.mult)
                tt(t, sn[:, :, lo_], pc, ALU.mult)
                tt(sn[:, :, hi_], sn[:, :, hi_], t, ALU.add)
                n *= 2
            A, B, R, I = (ring[0][:, i, :] for i in range(4))
            for j in range(8):
                c, d = cs[:, j, :], sn[:, j, :]
                dve.wait_ge(s.bu_ready, j + 1)
                br, bi = core.psum[2 * (j % 2)], core.psum[2 * (j % 2) + 1]
                tt(A, br, c, ALU.mult)
                tt(B, bi, d, ALU.mult)
                tt(A, A, B, ALU.add)
                tt(B, bi, c, ALU.mult)
                tt(R, br, d, ALU.mult, s.bu_out)
                tt(B, B, R, ALU.subtract)
                mag = v["mag"][:, j:j + 1].broadcast_to([P, T])
                if j:
                    dve.wait_ge(s.x_used, j)
                done(dve, dve.tensor_tensor_scan(R, mag, A, 0.0, ALU.mult, ALU.add), s.scan)
                done(dve, dve.tensor_tensor_scan(I, mag, B, 0.0, ALU.mult, ALU.add), s.scan)
                tt(A, R, c, ALU.mult)
                tt(B, I, d, ALU.mult)
                tt(A, A, B, ALU.subtract)
                tt(B, I, c, ALU.mult)
                tt(R, R, d, ALU.mult)
                tt(sn[:, j, :], B, R, ALU.add)
                done(dve, dve.tensor_copy(cs[:, j, :], A), s.x_ready)
            for j in range(2):
                dve.wait_ge(s.x_used, 8)
                y = Y[:, j, :]
                done(dve, dve.scalar_tensor_tensor(y, u[:, j, :], core.param("s5d", j), core.psum[4 + j], ALU.mult, ALU.add), s.u_out)
                tt(A, y, y, ALU.mult)
                ts(A, A, 0.044715, 1.0, ALU.mult, ALU.add)
                tt(sn[:, j, :], A, y, ALU.mult, s.tanh_in)
            for j in range(2):
                y = Y[:, j, :]
                dve.wait_ge(s.tanhed, j + 1)
                ts(A, y, 0.5, None, ALU.mult)
                done(dve, dve.scalar_tensor_tensor(y, sn[:, j, :], 1.0, A, ALU.add, ALU.mult), s.gelu)
            for j in range(2):
                dve.wait_ge(s.sigm, j + 1)
                dve.wait_ge(s.glu, 2)
                tt(Y[:, j, :], Y[:, j, :], sn[:, j, :], ALU.mult, s.glued)
            dve.wait_ge(s.root, 1)
            done(dve, dve.reciprocal(A, sn[:, 4, :]), s.steps)
            for j in range(2):
                done(dve, dve.scalar_tensor_tensor(Y[:, j, :], Y[:, j, :], core.param("gain", j), A, ALU.mult, ALU.mult), s.steps)

        @block.tensor
        def _(pe):
            ident = core.const("ident")
            for i in range(2):
                pe.wait_ge(s.spread, 8 * i + 8)
                for q in range(2):
                    if i:
                        pe.wait_ge(s.bt_out, q + 1)
                    for j in range(4):
                        mm = pe.transpose(core.psum[q][:, j * P:(j + 1) * P], big[:, 4 * q + j, :], ident)
                    mm.then_inc(s.spread_t, 1)
            pe.wait_ge(s.bt_out, 4)

            def bu(j):
                if j >= 2:
                    pe.wait_ge(s.bu_out, j - 1)
                for i in range(2):
                    mm = pe.matmul(core.psum[2 * (j % 2) + i], BT[i][:, j, :], u[:, j // 4, :], start=True, stop=True)
                mm.then_inc(s.bu_ready, 1)

            bu(0)
            for j in range(8):
                if j < 7:
                    bu(j + 1)
                pe.wait_ge(s.x_ready, j + 1)
                bank = core.psum[4 + j // 4]
                pe.matmul(bank, C_spread[0][:, j, :], cs[:, j, :], start=j % 4 == 0, stop=False)
                mm = pe.matmul(bank, C_spread[1][:, j, :], sn[:, j, :], start=False, stop=j % 4 == 3)
                mm.then_inc(s.x_used, 1)
            pe.wait_ge(s.wglu_in, 16)
            pe.wait_ge(s.gelu, 2)
            wg = small[:].rearrange("p (k n) -> p k n", k=2)
            for j in range(2):
                for k in range(2):
                    mm = pe.matmul(core.psum[4 + j], wg[:, k, j * P:(j + 1) * P], Y[:, k, :], start=k == 0, stop=k == 1)
                mm.then_inc(s.glu, 1)
            for j in range(2):
                pe.wait_ge(s.sq, j + 1)
                mm = pe.matmul(core.psum[6], core.const("ones"), sn[:, 2 + j, :], start=j == 0, stop=j == 1)
            mm.then_inc(s.total, 1)


def head_norms(core, Z):
    Y = core.Y
    with Stage(core, "heads") as st:
        sq, sig = st.sb("sq", [P, 6, T]), st.sb("sig", [P, 4, T])
        s = st.sems("squared total root sig inv normed scaled gated")
        gates = {2: 8, 3: 9, 6: 22, 7: 23}
        block = st.block()

        @block.scalar
        def _(act):
            for i in range(6):
                done(act, act.activation(sq[:, i, :], Y[:, 2 + i, :], ACT.Square), s.squared)
            for i, z in enumerate(gates.values()):
                done(act, act.activation(sig[:, i, :], Z[:, z, :], ACT.Sigmoid), s.sig)
            for i in range(6):
                act.wait_ge(s.total, i + 1)
                done(act, act.activation(sq[:, i, :], core.psum[i], ACT.Sqrt, bias=core.eps_rms[:], scale=1.0 / 64), s.root)

        @block.tensor
        def _(pe):
            for i in range(6):
                pe.wait_ge(s.squared, i + 1)
                pe.matmul(core.psum[i], core.const("blk"), sq[:, i, :], start=True, stop=True).then_inc(s.total, 1)

        @block.vector
        def _(dve):
            dve.wait_ge(s.sig, 4)
            for i in range(6):
                y = Y[:, 2 + i, :]
                dve.wait_ge(s.root, i + 1)
                done(dve, dve.reciprocal(sq[:, i, :], sq[:, i, :]), s.inv)
                done(dve, dve.scalar_tensor_tensor(y, y, core.param("gain", 2 + i), sq[:, i, :], ALU.mult, ALU.mult), s.normed)
                if 2 + i in gates:
                    g = list(gates).index(2 + i)
                    done(dve, dve.tensor_tensor(y, y, sig[:, g, :], ALU.mult), s.scaled)
                    if i < 2:
                        done(dve, dve.tensor_tensor(y, y, Z[:, gates[2 + i], :], ALU.mult), s.gated)


def second_mixer(core):
    rms_norm(core, core.X, "pre", core.Y)
    with Stage(core, "second") as st:
        Z = st.sb("Zs", [P, 25, T])
        dense(core, [(10, Plain(Z)), (2, Plain(Z, 10, 64 ** -0.5)), (13, Plain(Z, 12))], core.Y)
        core.hook("Zs", Z)
        G = st.sb("G", [P, 4, T])
        gate_rows(core, Z, G)
        rows = lambda e: slice(64 * e, 64 * e + 64)
        heads = [dict(q=[Z[rows(h % 2), 10 + h // 2, :]], k=Z[rows(h % 2), 12 + h // 2, :], v=Z[rows(h % 2), 14 + h // 2, :],
                      out=core.Y[rows(h % 2), 4 + h // 2, :], row=64 * (h % 2)) for h in range(4)]
        sel = core.const("sel").rearrange("p (h k) -> p h k", k=P)
        attention(core, "fox", heads, ["causal"], bias=lambda h: (sel[0:4, h, :], G[0:4, 1, :]))
        mlstm(core, Z, G)
        hgrn2(core, Z)
        s5(core, Z)
        core.hook("Yraw", core.Y)
        head_norms(core, Z)
        core.hook("Yn", core.Y)
        dense(core, [(KD, Plain(core.Y))], core.Y)
    rms_norm(core, core.Y, "post", core.X, add=True)


def feed_forward(core):
    rms_norm(core, core.X, "fpre", core.Y)
    with Stage(core, "ffn") as st:
        xh, xl = (st.sb(n, [P, KD, T], F32R) for n in ("xh", "xl"))
        hh, hl = (st.sb(n, [P, FT, T], F32R) for n in ("hh", "hl"))
        for half in range(2):
            with Stage(core, "gateup") as g:
                gemm(g, [(2 * FT, Gated(hh, hl))], core.Y, (xh, xl), split_src=half == 0)
            with Stage(core, "down") as g:
                gemm(g, [(KD, Plain(core.Y) if half == 0 else Accumulate(core.Y))], None, (hh, hl), split_src=False)
    rms_norm(core, core.Y, "fpost", core.X, add=True)


def store(core):
    with Stage(core, "store") as st:
        s = st.sems("stored")
        block = st.block()

        @block.sync
        def _(sp):
            sp.dma_start(core.io["out"].rearrange("p (k t) -> p k t", t=T), core.X[:]).then_inc(s.stored, 16)
            sp.wait_ge(s.stored, 16)


def load(core):
    with Stage(core, "load") as st:
        masks = st.sb("masks", [P, MASK_N])
        loads = (("masks", masks), ("consts", core.consts), ("params", core.params))
        s = st.sems("x_in rest_in set_eps cast")
        block = st.block()

        @block.sync
        def _(sp):
            sp.dma_start(core.X[:], core.io["x"].rearrange("p (k t) -> p k t", t=T)).then_inc(s.x_in, 16)
            stream_weights(core, sp, 0, hi=RING)
            sp.wait_ge(s.x_in, 16)

        @block.scalar
        def _(act):
            for name, to in loads:
                act.dma_start(to[:], core.io[name]).then_inc(s.rest_in, 16)
            act.wait_ge(s.rest_in, 16 * len(loads))

        @block.vector
        def _(dve):
            for t, v in ((core.eps_ln, LN_EPS), (core.eps_gn, GN_EPS), (core.eps_rms, RMS_EPS)):
                dve.memset(t[:], v).then_inc(s.set_eps, 1)
            dve.wait_ge(s.set_eps, 3)
            dve.wait_ge(s.rest_in, 16 * len(loads))
            dve.tensor_copy(core.masks[:], masks[:]).then_inc(s.cast, 1)


def mlp(core, layer):
    with Stage(core, "mlp") as st:
        xh, xl = (st.sb(n, [P, KD, T], F32R) for n in ("xh", "xl"))
        hh, hl = (st.sb(n, [P, HALF, T], F32R) for n in ("hh", "hl"))
        for half in range(2):
            with Stage(core, "up") as g:
                gemm(g, [(HALF, SquaredRelu(hh, hl))], core.X, (xh, xl), split_src=half == 0)
            with Stage(core, "down") as g:
                gemm(g, [(KD, Residual(core.Y, core.X) if half == 0 else Accumulate(core.Y))], None, (hh, hl), U=2, split_src=False)


def dense(core, segments, src):
    with Stage(core, "dense") as st:
        xh, xl = (st.sb(n, [P, KD, T], F32R) for n in ("xh", "xl"))
        gemm(st, segments, src, (xh, xl))


def first_mixer(core):
    with Stage(core, "mixer") as st:
        Z = st.sb("Z", [P, 27, T])
        scale = P ** -0.5
        dense(core, [(15, Shift(Z)), (4, Rope(Z, 15, scale)), (4, Rope(Z, 19)), (4, Plain(Z, 23))], core.X)
        O = st.sb("O", [P, KD, T])
        core.hook("Z", Z)
        heads = [dict(q=[Z[:, 15 + h, :]], k=Z[:, 19 + h, :], v=Z[:, 23 + h, :], out=O[:, 4 + h, :], row=0) for h in range(4)]
        attention(core, "moba", heads, ["causal"])
        core.hook("O4", O)
        rwkv(core, Z, O)
        core.hook("O", O)
        dense(core, [(KD, Residual(core.Y, core.X))], O)


def dilated_mixer(core):
    with Stage(core, "dilated") as st:
        Z = st.sb("Z", [P, 40, T])
        dense(core, [(24, Rope(Z, 0, P ** -0.5)), (8, Rope(Z, 24)), (8, Plain(Z, 32))], core.X)
        core.hook("Z2", Z)
        heads = [dict(q=[Z[:, 8 * g + h, :] for g in range(3)], k=Z[:, 24 + h, :], v=Z[:, 32 + h, :], out=Z[:, 32 + h, :], row=0) for h in range(8)]
        attention(core, "dil", heads, ["band", "mod4", "mod16"])
        core.hook("O2", Z)
        dense(core, [(KD, Residual(core.Y, core.X))], Z[:, 32:40, :])


def program(nc, io, hook=None, upto=99):
    core_hook = hook or (lambda core, name, t: None)
    with ExitStack() as ctx:
        core = Core(nc, io, ctx)
        core.hook = lambda name, t: core_hook(core, name, t)
        core.gemms = [(io[n], kt, u) for n, kt, u in STREAMS]
        load(core)
        first_mixer(core)
        core.hook("Y0", core.Y)
        if upto < 1: return
        layer_norm(core, "ln1g0", "ln1b0")
        core.hook("X1", core.X)
        mlp(core, 0)
        layer_norm(core, "ln2g0", "ln2b0")
        core.hook("X2", core.X)
        if upto < 2: return
        dilated_mixer(core)
        layer_norm(core, "ln1g1", "ln1b1")
        core.hook("X3", core.X)
        mlp(core, 1)
        layer_norm(core, "ln2g1", "ln2b1")
        core.hook("X4", core.X)
        if upto < 3: return
        second_mixer(core)
        core.hook("X5", core.X)
        feed_forward(core)
        store(core)


STREAMS = [("w_ab_in", 8, 27), ("w_ab_out", 8, 8),
           ("w1_0_0", 8, HALF), ("w2_0_0", 8, 16), ("w1_0_1", 8, HALF), ("w2_0_1", 8, 16),
           ("w_c_in", 8, 40), ("w_c_out", 8, 8),
           ("w1_1_0", 8, HALF), ("w2_1_0", 8, 16), ("w1_1_1", 8, HALF), ("w2_1_1", 8, 16),
           ("w_in2", 8, 25), ("w_out2", 8, 8),
           ("w_gu_0", 8, 2 * FT), ("w_down_0", FT, 8), ("w_gu_1", 8, 2 * FT), ("w_down_1", FT, 8)]


def weight_units(w, kt, pair=None):
    K, N = w.shape
    w = w.reshape(K // (kt * P), kt, P, N // P, P)
    return np.ascontiguousarray(w.transpose(3, 0, 2, 1, 4)).reshape(-1, P, kt * P)


def padded(w, cols):
    return np.concatenate([w, np.zeros((w.shape[0], cols - w.shape[1]), w.dtype)], 1)


def columns(v):
    return np.asarray(v).reshape(-1, P).T


def layout(i):
    a = {k: np.asarray(v) for k, v in i.items()}
    io = {"x": a["x"][0].reshape(T, KD, P).transpose(2, 1, 0).reshape(P, KD * T), "consts": const_array(), "masks": mask_array()}
    w = a["ab_w_in"][0]
    io["w_ab_in"] = weight_units(np.concatenate([padded(w[:, :1824], 15 * P), w[:, 1824:]], 1), 8)
    io["w_ab_out"] = weight_units(a["ab_w_out"][0], 8)
    io["w_c_in"] = weight_units(a["c_w_in"][0], 8)
    io["w_c_out"] = weight_units(a["c_w_out"][0], 8)
    hid = HALF * P
    for layer in range(2):
        for h in range(2):
            io[f"w1_{layer}_{h}"] = weight_units(a["mlp_w1"][layer][:, h * hid:(h + 1) * hid], 8)
            io[f"w2_{layer}_{h}"] = weight_units(a["mlp_w2"][layer][h * hid:(h + 1) * hid], 8)
    w = a["w_in_2"][0]
    W = 256
    gates = np.zeros((D, P), w.dtype)
    gates[:, 0:4] = w[:, 8 * W:8 * W + 4]
    gates[:, 32:36] = w[:, 12 * W + 4:12 * W + 8]
    gates[:, 64:68] = w[:, 12 * W + 8:12 * W + 12]
    io["w_in2"] = weight_units(np.concatenate([w[:, :8 * W], w[:, 8 * W + 4:12 * W + 4], gates], 1), 8)
    io["w_out2"] = weight_units(a["w_out_2"][0], 8)
    gate, up, down = a["w_ffn_gate_2"][0], a["w_ffn_up_2"][0], a["w_ffn_down_2"][0]
    fh = FT * P
    for h in range(2):
        both = np.stack([m[:, h * fh:(h + 1) * fh].reshape(D, FT, P) for m in (gate, up)], 2)
        io[f"w_gu_{h}"] = weight_units(both.reshape(D, 2 * fh), 8)
        io[f"w_down_{h}"] = weight_units(down[h * fh:(h + 1) * fh], FT)
    small = {n: np.zeros((P, c), np.float32) for n, c in SMALL_COLS.items()}
    small["lora"][0:64], small["lora"][64:128] = a["ab_w_up"][0], a["ab_a_up"][0]
    small["gup0"][:], small["gup1"][0:32] = a["ab_g_up"][0][0:P], a["ab_g_up"][0][P:160]
    small["wglu"][:] = a["s5_w_glu_2"][0].reshape(2, P, 256).transpose(1, 0, 2).reshape(P, 512)
    io["small"] = np.concatenate([small[n] for n in SMALL_COLS], 1)

    p = {}
    mix = a["ab_shift_mix"][0]
    p["mix"] = columns(np.concatenate([mix, np.zeros(15 * P - 1824, mix.dtype)]))
    for n, key in (("w0", "ab_w0"), ("a0", "ab_a0"), ("kk", "ab_k_k"), ("ka", "ab_k_a"), ("gng", "ab_lnx_g"), ("gnb", "ab_lnx_b"),
                   ("pre", "ln_mix_pre_2"), ("post", "ln_mix_post_2"), ("fpre", "ln_ffn_pre_2"), ("fpost", "ln_ffn_post_2"),
                   ("gain", "mix_gain_2"), ("s5d", "s5_d_2")):
        p[n] = columns(a[key][0])
    p["rk"] = columns(a["ab_r_k"][0].reshape(-1))
    for layer in range(2):
        for n in ("ln1", "ln2"):
            for m in "gb":
                p[f"{n}{m}{layer}"] = columns(a[f"{n}_{m}"][layer])
    gb = a["gate_bias_2"][0]
    p["gateb"] = np.zeros((P, 1), np.float32)
    p["gateb"][0:4, 0], p["gateb"][32:36, 0], p["gateb"][64:68, 0] = gb[0:4], gb[4:8], gb[8:12]
    states = lambda v: v.reshape(8, P, *v.shape[2:])
    p["lre"], p["lim"] = states(a["s5_lambda_re_2"][0]).T, states(a["s5_lambda_im_2"][0]).T
    p["ldt"] = np.repeat(a["s5_log_dt_2"][0].reshape(8, 2), 64, axis=1).T
    p["bre"], p["bim"] = (states(a[k][0]).transpose(1, 0, 2).reshape(P, 128) for k in ("s5_b_re_2", "s5_b_im_2"))
    p["cre"], p["cim"] = (states(a[k][0].transpose(0, 2, 1)).transpose(1, 0, 2).reshape(P, 128) for k in ("s5_c_re_2", "s5_c_im_2"))
    p["conv"] = a["mlstm_conv_w_2"][0].reshape(4, 4, P).transpose(2, 1, 0).reshape(P, 16)
    io["params"] = np.concatenate([np.asarray(p[n], np.float32).reshape(P, -1) for n in PARAM_COLS], 1)
    return {n: np.ascontiguousarray(v) for n, v in io.items()}


def kernel(**inputs):
    import concourse.bacc as bacc
    from concourse.bass_utils import run_bass_kernel_spmd

    nc = bacc.Bacc("TRN2", target_bir_lowering=False, num_devices=1)
    arrays = layout(inputs)
    io = {n: nc.dram_tensor(f"in_{n}", v.shape, mybir.dt.from_np(v.dtype), kind="ExternalInput").ap() for n, v in arrays.items()}
    io["out"] = nc.dram_tensor("out_x", (P, KD * T), F32, kind="ExternalOutput").ap()
    program(nc, io)
    r = run_bass_kernel_spmd(nc, [{f"in_{n}": v for n, v in arrays.items()}], core_ids=[0])
    out = r.results[0]["out_x"].reshape(P, KD, T)
    return np.ascontiguousarray(out.transpose(2, 1, 0)).reshape(1, T, D)
```

```python
from collections import namedtuple
from contextlib import ExitStack

import numpy as np
import concourse.bass as bass
from concourse import mybir

F32 = mybir.dt.float32
F32R = mybir.dt.float32r
BF16 = mybir.dt.bfloat16
ALU = mybir.AluOpType
ACT = mybir.ActivationFunctionType
AX = mybir.AxisListType

P = 128
T = 512
D = 1024
KD = D // P
ALPHA = 4 ** 0.25
LN_EPS = 1e-5
GN_EPS = 64e-5
RMS_EPS = 1e-6
NEG = -1e30
C = 64
NCH = T // C
NT = T // P
HALF = 4096 // P // 2
FT = 2816 // P // 2
RING = 4
BANKS = 4
KT_MAX = 11

CONST_COLS = {"ident": P, "ones": P, "blk": P, "ropec": T, "ropes": T, "chunk": T, "rmask": 4 * C,
              "lmask": 7 * C, "lmaskt": 6 * C, "s5mask": 8 * P, "sel": 4 * P}
MASK_COLS = {"identb": P, "causal": P, "prev": P, "mod4": 4 * P, "mod16": 4 * P}


def offsets(cols):
    at, out = 0, {}
    for name, n in cols.items():
        out[name] = (at, at + n)
        at += n
    return out, at


CONST_AT, CONST_N = offsets(CONST_COLS)
MASK_AT, MASK_N = offsets(MASK_COLS)

PARAM_COLS = {"mix": 15, "w0": 4, "a0": 4, "kk": 4, "ka": 4, "rk": 4, "gng": 4, "gnb": 4,
              "ln1g0": 8, "ln1b0": 8, "ln2g0": 8, "ln2b0": 8, "ln1g1": 8, "ln1b1": 8,
              "ln2g1": 8, "ln2b1": 8, "pre": 8, "post": 8, "fpre": 8, "fpost": 8,
              "gain": 8, "gateb": 1, "s5d": 2, "lre": 8, "lim": 8, "ldt": 8, "conv": 16,
              "cre": 128, "cim": 128}
PARAM_AT, PARAM_N = offsets(PARAM_COLS)

SMALL_COLS = {"lora": 512, "gup0": 512, "gup1": 512, "wglu": 512}
SMALL_AT, SMALL_N = offsets(SMALL_COLS)


def const_array():
    a = {k: np.zeros((P, n), np.float32) for k, n in CONST_COLS.items()}
    p = np.arange(P)
    a["ident"][:] = np.eye(P)
    a["ones"][:] = 1
    a["blk"][:] = (p[:, None] // 64 == p[None, :] // 64)
    inv = np.float32(500000.0) ** (-np.arange(16, dtype=np.float32) / np.float32(16))
    ang = inv[:, None] * np.arange(T, dtype=np.float32)[None]
    a["ropec"][0:16] = a["ropec"][16:32] = np.cos(ang)
    a["ropes"][0:16] = -np.sin(ang)
    a["ropes"][16:32] = np.sin(ang)
    a["chunk"][:] = (np.arange(T) % C != 0)
    s, t = np.arange(C)[:, None], np.arange(C)[None]
    both = lambda m: np.concatenate([m, m], 0)
    a["rmask"][:] = both(np.concatenate([s < t, s <= t, s < t, s <= t], 1))
    level = lambda m: (s // (2 * m) == t // (2 * m)) & (s % (2 * m) < m) & (t % (2 * m) >= m)
    levels = [level(m) for m in (1, 2, 4, 8, 16, 32)]
    a["lmask"][:] = both(np.concatenate(levels + [s == t], 1))
    a["lmaskt"][:] = both(np.concatenate([m.T for m in levels], 1))
    m = a["s5mask"].reshape(P, 8, P)
    for j in range(8):
        m[:, j] = ((2 * j + p[:, None] // 64) % 8 == p[None, :] // 16)
    m = a["sel"].reshape(P, 4, P)
    for h in range(4):
        m[:, h] = (p[:, None] % 32 == h)
    return np.concatenate([a[k] for k in CONST_COLS], 1)


def mask_array():
    q, k = np.arange(P)[:, None], np.arange(P)[None]
    bias = lambda ok: np.where(ok, 0.0, NEG)
    mod = lambda n: np.concatenate([bias((q - k) % n == 0)] * 3 + [bias(((q - k) % n == 0) & (k <= q))], 1)
    parts = {"identb": np.eye(P), "causal": bias(k <= q), "prev": bias(k >= q), "mod4": mod(4), "mod16": mod(16)}
    return np.concatenate([parts[n] for n in MASK_COLS], 1).astype(np.float32)


class Core:

    def __init__(self, nc, io, ctx):
        self.nc, self.io = nc, io
        COUNTS.clear()
        sb = lambda n, s, d=F32: ctx.enter_context(nc.sbuf_tensor(n, s, d))
        sem = lambda n: ctx.enter_context(nc.semaphore(n))
        self.consts = sb("consts", [P, CONST_N])
        self.masks = sb("masks", [P, MASK_N], BF16)
        self.params = sb("params", [P, PARAM_N])
        self.X = sb("X", [P, KD, T])
        self.Y = sb("Y", [P, KD, T])
        self.eps_ln, self.eps_gn, self.eps_rms = sb("eps_ln", [P, 1]), sb("eps_gn", [P, 1]), sb("eps_rms", [P, 1])
        self.line = sb("line", [P, T])
        steps = sb("s5_steps", [P, 5, 8])
        self.s5 = {n: steps[:, i, :] for i, n in enumerate(("mag", "co", "si", "cfr", "cfi"))}
        self.raw = [sb(f"w_raw{i}", [P, KT_MAX * P]) for i in range(RING)]
        self.banks = ctx.enter_context(nc.psum_tensor("banks", [P, 8, T], F32))
        self.psum = [self.banks[:, i, :] for i in range(8)]
        self.w_landed = [sem(f"w_landed{i}") for i in range(RING)]
        self.consts_in = sem("consts_in")
        self.hi_ready = sem("hi_ready")
        self.split_ready = sem("split_ready")
        self.unit_used = sem("unit_used")
        self.block_out = sem("block_out")
        self.units = self.blocks = 0
        self.gemms = []
        self.n_gemm = 0
        self.to_clear = []
        self.stage = 0

    def const(self, name, rows=slice(None)):
        a, b = CONST_AT[name]
        return self.consts[rows, a:b]

    def mask(self, name):
        a, b = MASK_AT[name]
        return self.masks[:, a:b]

    def param(self, name, j=None):
        a, b = PARAM_AT[name]
        return self.params[:, a:b] if j is None else self.params[:, a + j:a + j + 1]


class Stage:

    def __init__(self, core, name):
        core.stage += 1
        self.core, self.nc, self.tag = core, core.nc, f"{name}{core.stage}_"
        self.ctx = ExitStack()
        self.own, self.cleared = [], []

    def __enter__(self):
        return self

    def __exit__(self, *e):
        self.ctx.close()
        for h in self.cleared:
            self.nc.release_semaphore(h)
        self.core.to_clear += self.own

    def sb(self, name, shape, dt=F32):
        return self.ctx.enter_context(self.nc.sbuf_tensor(self.tag + name, shape, dt))

    def sems(self, names, prefix=""):
        made = [self.nc.alloc_semaphore(self.tag + prefix + n) for n in names.split()]
        self.own += made
        return namedtuple("Semaphores", names)(*made)

    def block(self, pool=None):
        block = self.ctx.enter_context(self.nc.Block(no_gpsimd_drain=True))
        self.cleared, self.core.to_clear = self.core.to_clear, []

        @block.gpsimd
        def _(eng):
            nums = sorted(h.num for h in self.cleared)
            while nums:
                n = 1
                while n < len(nums) and nums[n] == nums[0] + n:
                    n += 1
                eng.sem_clear(range(nums[0], nums[0] + n))
                nums = nums[n:]
            if pool:
                pool(eng)
        return block


def done(eng, ins, sem):
    ins.then_inc(sem, 1)
    COUNTS[sem.name] = COUNTS.get(sem.name, 0) + 1
    eng.wait_ge(sem, COUNTS[sem.name])


COUNTS = {}


def inv_root(act, out, src, sem, bias=0.0, scale=1.0):
    done(act, act.activation(out, src, ACT.Ln, bias=bias, scale=scale), sem)
    done(act, act.activation(out, out, ACT.Exp, scale=-0.5), sem)


def in_groups(eng, n, group, body, lo=0):
    whole = n // group
    for j in range(lo, min(group, n)):
        body(0, j)
    if whole > 2:
        with eng.Fori(1, whole, 1) as it:
            for j in range(group):
                body(it, j)
    elif whole == 2:
        for j in range(group):
            body(1, j)
    if whole:
        for j in range(n - whole * group):
            body(whole, j)


def at_start(it):
    return isinstance(it, int) and it == 0


def stream_weights(core, sp, g, lo=0, hi=None, base=None):
    w, kt, n = core.gemms[g]
    base = core.units if base is None else base
    n = n if hi is None else min(hi, n)

    def body(it, j):
        at = base + j
        if at >= RING or not at_start(it):
            sp.wait_ge(core.split_ready, at - RING + 1 + it * RING)
        sp.dma_start(core.raw[at % RING][:, 0:kt * P], w[it * RING + j]).then_inc(core.w_landed[at % RING], 16)

    in_groups(sp, n, RING, body, lo)


class Evac:
    pair = 1
    act = dve = None

    def setup(self, st, tag):
        pass

    def start(self, dve):
        pass


class Summed(Evac):

    def setup(self, st, tag):
        self.line, self.s = st.core.line, st.sems("summed", tag)

    def start(self, dve):
        if self.sum:
            dve.memset(self.line[:], 0.0).then_inc(self.s.summed, 1)

    def add(self, dve, y, nth, left):
        if self.sum:
            dve.wait_ge(left[0], left[1])
            dve.wait_ge(self.s.summed, nth)
            dve.tensor_tensor(self.line[:], self.line[:], y, ALU.add).then_inc(self.s.summed, 1)


class Plain(Evac):

    def __init__(self, Z, off=0, scale=1.0):
        self.Z, self.off, self.scale = Z, off, scale

    def act(self, act, b, nth, banks, core, b0):
        act.activation(self.Z[:, bass.ds(b + self.off, 1), :], banks[0], ACT.Copy, scale=self.scale).then_inc(core.block_out, 1)


class Residual(Summed):

    def __init__(self, Y, X, sum=False):
        self.Y, self.X, self.sum = Y, X, sum

    def dve(self, dve, b, nth, banks, core, b0):
        y = self.Y[:, bass.ds(b, 1), :]
        dve.scalar_tensor_tensor(y, self.X[:, bass.ds(b, 1), :], ALPHA, banks[0], ALU.mult, ALU.add).then_inc(core.block_out, 1)
        self.add(dve, self.Y[:, b, :] if isinstance(b, int) else y, nth, (core.block_out, b0 + nth))


class Accumulate(Summed):

    def __init__(self, Y, sum=False):
        self.Y, self.sum = Y, sum

    def dve(self, dve, b, nth, banks, core, b0):
        y = self.Y[:, bass.ds(b, 1), :]
        dve.tensor_tensor(y, y, banks[0], ALU.add).then_inc(core.block_out, 1)
        self.add(dve, self.Y[:, b, :] if isinstance(b, int) else y, nth, (core.block_out, b0 + nth))


class SquaredRelu(Evac):

    def __init__(self, hh, hl):
        self.hh, self.hl = hh, hl

    def setup(self, st, tag):
        self.relu, self.sq = st.sb(tag + "relu", [P, T]), st.sb(tag + "sq", [P, T])
        self.s = st.sems("squared hidden_hi hidden_lo", tag)

    def act(self, act, b, nth, banks, core, b0):
        if not (isinstance(b, int) and b == 0):
            act.wait_ge(self.s.squared, nth - 1)
        act.activation(self.relu[:], banks[0], ACT.Relu).then_inc(core.block_out, 1)
        act.wait_ge(core.block_out, b0 + nth)
        act.activation(self.hh[:, bass.ds(b, 1), :], self.relu[:], ACT.Square).then_inc(self.s.hidden_hi, 1)
        act.wait_ge(self.s.hidden_hi, nth)

    def dve(self, dve, b, nth, banks, core, b0):
        if not (isinstance(b, int) and b == 0):
            dve.wait_ge(self.s.hidden_lo, nth - 1)
        dve.wait_ge(core.block_out, b0 + nth)
        dve.tensor_tensor(self.sq[:], self.relu[:], self.relu[:], ALU.mult).then_inc(self.s.squared, 1)
        dve.wait_ge(self.s.squared, nth)
        dve.wait_ge(self.s.hidden_hi, nth)
        dve.tensor_tensor(self.hl[:, bass.ds(b, 1), :], self.sq[:], self.hh[:, bass.ds(b, 1), :].bitcast(F32),
                          ALU.subtract).then_inc(self.s.hidden_lo, 1)


class Gated(Evac):
    pair = 2

    def __init__(self, hh, hl):
        self.hh, self.hl = hh, hl

    def setup(self, st, tag):
        self.sg, self.gs, self.prod = (st.sb(tag + n, [P, T]) for n in ("sg", "gs", "prod"))
        self.s = st.sems("sig gated hidden_hi hidden_lo", tag)

    def act(self, act, b, nth, banks, core, b0):
        act.activation(self.sg[:], banks[0], ACT.Sigmoid).then_inc(self.s.sig, 1)
        act.wait_ge(core.block_out, b0 + 2 * nth)
        act.activation(self.hh[:, bass.ds(nth - 1, 1), :], self.prod[:], ACT.Copy).then_inc(self.s.hidden_hi, 1)

    def dve(self, dve, b, nth, banks, core, b0):
        dve.wait_ge(self.s.sig, nth)
        if not (isinstance(b, int) and b == 1):
            dve.wait_ge(self.s.hidden_lo, nth - 1)
        dve.tensor_tensor(self.gs[:], self.sg[:], banks[0], ALU.mult).then_inc(self.s.gated, 1)
        dve.wait_ge(self.s.gated, nth)
        dve.tensor_tensor(self.prod[:], self.gs[:], banks[1], ALU.mult).then_inc(core.block_out, 2)
        dve.wait_ge(self.s.hidden_hi, nth)
        h = bass.ds(nth - 1, 1)
        dve.tensor_tensor(self.hl[:, h, :], self.prod[:], self.hh[:, h, :].bitcast(F32), ALU.subtract).then_inc(self.s.hidden_lo, 1)


class Shift(Evac):

    def __init__(self, Z):
        self.Z = Z

    def setup(self, st, tag):
        self.tmp = [st.sb(f"{tag}tmp{i}", [P, T + 1]) for i in range(2)]
        self.diff = st.sb(tag + "diff", [P, T])
        self.s = st.sems("zeroed copied diffed", tag)

    def start(self, dve):
        for t in self.tmp:
            dve.memset(t[:, 0:1], 0.0).then_inc(self.s.zeroed, 1)

    def act(self, act, b, nth, banks, core, b0):
        jb = self.jb
        if not (isinstance(b, int) and b < 2):
            act.wait_ge(core.block_out, b0 + nth - 2)
        act.activation(self.tmp[jb % 2][:, 1:T + 1], banks[0], ACT.Copy).then_inc(self.s.copied, 1)

    def dve(self, dve, b, nth, banks, core, b0):
        tmp = self.tmp[self.jb % 2]
        if isinstance(b, int) and b == 0:
            dve.wait_ge(self.s.zeroed, 2)
        dve.wait_ge(self.s.copied, nth)
        if not (isinstance(b, int) and b == 0):
            dve.wait_ge(core.block_out, b0 + nth - 1)
        dve.tensor_tensor(self.diff[:], tmp[:, 0:T], banks[0], ALU.subtract).then_inc(self.s.diffed, 1)
        dve.wait_ge(self.s.diffed, nth)
        a, _ = PARAM_AT["mix"]
        dve.scalar_tensor_tensor(self.Z[:, bass.ds(b, 1), :], self.diff[:], core.params[:, bass.ds(b + a, 1)],
                                 tmp[:, 1:T + 1], ALU.mult, ALU.add).then_inc(core.block_out, 1)


SWAP = list(range(16, 32)) + list(range(16))


class Rope(Evac):

    def __init__(self, Z, off, scale=1.0):
        self.Z, self.off, self.scale = Z, off, scale

    def setup(self, st, tag):
        self.sw, self.sn, self.cs = (st.core.Y[0:32, i, :] for i in range(3))
        self.s = st.sems("copied swapped turned", tag)

    def act(self, act, b, nth, banks, core, b0):
        act.activation(self.Z[:, bass.ds(b + self.off, 1), :], banks[0], ACT.Copy, scale=self.scale).then_inc(self.s.copied, 1)

    def dve(self, dve, b, nth, banks, core, b0):
        r = slice(0, 32)
        if isinstance(b, int) and b == 0:
            dve.wait_ge(core.consts_in, 32)
        if b0 or not isinstance(b, int) or b:
            dve.wait_ge(core.block_out, b0 + nth - 1)
        dve.wait_ge(self.s.copied, nth)
        dve.scalar_tensor_tensor(self.cs, banks[0][r], self.scale, core.const("ropec", r), ALU.mult, ALU.mult).then_inc(self.s.turned, 1)
        dve.stream_shuffle(self.sw, banks[0][r], SWAP).then_inc(self.s.swapped, 1)
        dve.wait_ge(self.s.swapped, nth)
        dve.scalar_tensor_tensor(self.sn, self.sw, self.scale, core.const("ropes", r), ALU.mult, ALU.mult).then_inc(self.s.turned, 1)
        dve.wait_ge(self.s.turned, 2 * nth)
        dve.tensor_tensor(self.Z[r, bass.ds(b + self.off, 1), :], self.cs, self.sn, ALU.add).then_inc(core.block_out, 1)


def gemms(st, parts, pool=None):
    block = st.block(pool or parts[0]["pool"])

    @block.sync
    def _(sp):
        for part in parts:
            part["sp"](sp)

    @block.scalar
    def _(act):
        held = None
        for part in parts:
            held = part["act"](act, held, part is parts[-1])

    @block.vector
    def _(dve):
        held = None
        for part in parts:
            held = part["dve"](dve, held, part is parts[-1])

    @block.tensor
    def _(pe):
        for part in parts:
            part["pe"](pe)


def weight_slots(st, kt):
    return [[st.sb(f"w_{n}{i}", [P, kt * P], F32R) for i in range(2)] for n in ("hi", "lo")]


def gemm(st, tag, slots, segments, src, src_parts, U=1, split_src=True, pool=None, norm=None, src_sem=None):
    core = st.core
    g = core.n_gemm
    w, kt, n_units = core.gemms[g]
    assert n_units == U * sum(n for n, _ in segments)
    u0, b0 = core.units, core.blocks
    group = 4 * U
    hi, lo = ([slot[:, 0:kt * P] for slot in part] for part in slots)
    if split_src:
        s = st.sems("mean centred squared var inv scaled src_hi x_ready src_ready", tag)
    ln = norm and norm[0] == "ln"
    centre, mean, var = core.Y if ln else core.X, core.psum[4], core.psum[5]
    squares = core.X if ln else core.Y
    src_hi, src_lo = src_parts
    for i, (_, e) in enumerate(segments):
        e.setup(st, f"{tag}seg{i}_")
    KT = kt * U

    def beside(gp):
        gp.wait_ge(s.src_ready, KT)
        pool(gp)


    def walk(unit, out, eng, held=None, last=True):
        ub = 0
        for n, e in segments:
            def leave(it, jn, e=e, ub=ub):
                if out and jn % e.pair == 0:
                    nth = it * (4 // e.pair) + jn // e.pair
                    e.jb = (jn - 1) % 4
                    banks = [core.psum[(b0 + ub // U + jn - 1 - i) % 4] for i in range(e.pair)][::-1]
                    out(e, it * 4 + jn - 1, nth, banks, ub)

            def body(it, j, ub=ub, leave=leave, held=held):
                unit(it, j, ub)
                if held and at_start(it) and j == 0:
                    held()
                if j % U == 0 and not (at_start(it) and j == 0):
                    leave(it, j // U)
            in_groups(eng, n * U, group, body)
            held = lambda leave=leave, n=n: leave((n - 1) // 4, (n - 1) % 4 + 1)
            ub += n * U
        if last:
            held()
        return held

    def sp_part(sp):
        stream_weights(core, sp, g, lo=min(RING, n_units), base=u0)
        if g + 1 < len(core.gemms):
            stream_weights(core, sp, g + 1, hi=RING, base=u0 + n_units)

    def leaving(eng, part):
        def out(e, b, nth, banks, ub):
            f = e.act if part == "act" else e.dve
            if f:
                eng.wait_ge(core.unit_used, u0 + ub + nth * e.pair * U)
                f(eng, b, nth, banks, core, b0 + ub // U)
        return out

    def last_before_src(it, j, ub):
        return split_src and at_start(it) and ub + j == 1

    def act_part(act, held, last):
        def split():
            if norm:
                for k in range(KD):
                    if ln:
                        act.wait_ge(s.centred, k + 1)
                    act.activation(squares[:, k, :], centre[:, k, :], ACT.Square).then_inc(s.squared, 1)
                act.wait_ge(s.var, 1)
                inv_root(act, core.line[:], var, s.inv, (core.eps_ln if ln else core.eps_rms)[:], 1.0 / D)
            for k in range(KT):
                if norm:
                    act.wait_ge(s.scaled, k + 1)
                if ln:
                    gain, bias = core.param(norm[1], k), core.param(norm[2], k)
                    act.activation(src_hi[:, k, :], core.Y[:, k, :], ACT.Identity, bias=bias, scale=gain).then_inc(s.src_hi, 1)
                    act.activation(core.X[:, k, :], core.Y[:, k, :], ACT.Identity, bias=bias, scale=gain).then_inc(s.x_ready, 1)
                else:
                    act.activation(src_hi[:, k, :], src[:, k, :], ACT.Copy).then_inc(s.src_hi, 1)

        def unit(it, j, ub):
            at = u0 + ub + j
            act.wait_ge(core.w_landed[at % RING], 16 * (at // RING + 1) + it * (16 * group // RING))
            if at >= 2 or not at_start(it):
                act.wait_ge(core.unit_used, at - 1 + it * group)
            act.activation(hi[at % 2], core.raw[at % RING][:, 0:kt * P], ACT.Copy).then_inc(core.hi_ready, 1)
            if last_before_src(it, j, ub):
                split()
        return walk(unit, leaving(act, "act"), act, held, last)

    def dve_part(dve, held, last):
        for _, e in segments:
            e.start(dve)

        def scale(k):
            if ln:
                dve.tensor_tensor(core.Y[:, k, :], core.Y[:, k, :], core.line[:], ALU.mult).then_inc(s.scaled, 1)
            elif norm:
                dve.scalar_tensor_tensor(core.Y[:, k, :], core.X[:, k, :], core.param(norm[1], k), core.line[:],
                                         ALU.mult, ALU.mult).then_inc(s.scaled, 1)

        def centre_tiles():
            dve.wait_ge(s.mean, 1)
            for k in range(KD):
                dve.scalar_tensor_tensor(core.Y[:, k, :], mean, -1.0 / D, core.Y[:, k, :], ALU.mult, ALU.add).then_inc(s.centred, 1)

        def split():
            if norm:
                dve.wait_ge(s.inv, 2)
            scale(0)
            for k in range(KT):
                if k + 1 < KT:
                    scale(k + 1)
                dve.wait_ge(s.src_hi, k + 1)
                if ln:
                    dve.wait_ge(s.x_ready, k + 1)
                dve.tensor_tensor(src_lo[:, k, :], src[:, k, :], src_hi[:, k, :].bitcast(F32),
                                  ALU.subtract).then_inc(s.src_ready, 1)

        def unit(it, j, ub):
            at = u0 + ub + j
            dve.wait_ge(core.hi_ready, at + 1 + it * group)
            dve.tensor_tensor(lo[at % 2], core.raw[at % RING][:, 0:kt * P], hi[at % 2].bitcast(F32),
                              ALU.subtract).then_inc(core.split_ready, 1)
            if ln and at_start(it) and ub + j == 0:
                centre_tiles()
            if last_before_src(it, j, ub):
                split()
        return walk(unit, leaving(dve, "dve"), dve, held, last)

    def pe_part(pe):
        def first_two():
            banks = [core.psum[(b0 + i) % 4] for i in range(2)]
            if ln:
                pe.matmul(mean, core.const("ones"), core.line[:], start=True, stop=True).then_inc(s.mean, 1)
            if norm:
                for k in range(KD):
                    pe.wait_ge(s.squared, k + 1)
                    mm = pe.matmul(var, core.const("ones"), squares[:, k, :], start=k == 0, stop=k == KD - 1)
                mm.then_inc(s.var, 1)
            pe.wait_ge(core.split_ready, u0 + 2)
            if b0 + 1 >= BANKS:
                pe.wait_ge(core.block_out, b0 + 2 - BANKS)
            for k in range(kt):
                pe.wait_ge(s.src_ready, k + 1)
                for i, bank in enumerate(banks):
                    wh, wl = (w[(u0 + i) % 2][:, k * P:(k + 1) * P] for w in (hi, lo))
                    pe.matmul(bank, wh, src_hi[:, k, :], start=k == 0, stop=False)
                    pe.matmul(bank, wh, src_lo[:, k, :], start=False, stop=False)
                    mm = pe.matmul(bank, wl, src_hi[:, k, :], start=False, stop=k == kt - 1)
                    if k == kt - 1:
                        mm.then_inc(core.unit_used, 1)

        def unit(it, j, ub):
            if split_src and at_start(it) and ub + j < 2:
                if ub + j == 0:
                    first_two()
                return
            at = u0 + ub + j
            pe.wait_ge(core.split_ready, at + 1 + it * group)
            gb = b0 + (ub + j) // U
            bank = core.psum[gb % 4]
            if j % U == 0 and (gb >= BANKS or not at_start(it)):
                pe.wait_ge(core.block_out, gb - BANKS + 1 + it * 4)
            for k in range(kt):
                kk = (j % U) * kt + k
                if src_sem and at_start(it) and ub + j < U:
                    pe.wait_ge(src_sem, kk + 1)
                wh, wl = hi[at % 2][:, k * P:(k + 1) * P], lo[at % 2][:, k * P:(k + 1) * P]
                pe.matmul(bank, wh, src_hi[:, kk, :], start=kk == 0, stop=False)
                pe.matmul(bank, wh, src_lo[:, kk, :], start=False, stop=False)
                mm = pe.matmul(bank, wl, src_hi[:, kk, :], start=False, stop=kk == KT - 1)
            mm.then_inc(core.unit_used, 1)
        walk(unit, None, pe)

    core.units += n_units
    core.blocks += n_units // U
    core.n_gemm += 1
    return dict(sp=sp_part, act=act_part, dve=dve_part, pe=pe_part, pool=beside if pool else None)


def layer_norm(core, gain, bias):
    X, Y, line = core.X, core.Y, core.line
    with Stage(core, "ln") as st:
        sq = st.sb("sq", [P, KD, T])
        s = st.sems("mean centred squared var inv scaled")
        mean, var = core.psum[4], core.psum[5]
        ones = core.const("ones")
        block = st.block()

        @block.tensor
        def _(pe):
            pe.matmul(mean, ones, line[:], start=True, stop=True).then_inc(s.mean, 1)
            for k in range(KD):
                pe.wait_ge(s.squared, k + 1)
                mm = pe.matmul(var, ones, sq[:, k, :], start=k == 0, stop=k == KD - 1)
            mm.then_inc(s.var, 1)

        @block.vector
        def _(dve):
            dve.wait_ge(s.mean, 1)
            for k in range(KD):
                dve.scalar_tensor_tensor(Y[:, k, :], mean, -1.0 / D, Y[:, k, :], ALU.mult, ALU.add).then_inc(s.centred, 1)
            dve.wait_ge(s.inv, 2)
            for k in range(KD):
                dve.wait_ge(s.centred, k + 1)
                dve.tensor_tensor(X[:, k, :], Y[:, k, :], line[:], ALU.mult).then_inc(s.scaled, 1)

        @block.scalar
        def _(act):
            for k in range(KD):
                act.wait_ge(s.centred, k + 1)
                act.activation(sq[:, k, :], Y[:, k, :], ACT.Square).then_inc(s.squared, 1)
            act.wait_ge(s.var, 1)
            inv_root(act, line[:], var, s.inv, core.eps_ln[:], 1.0 / D)
            for k in range(KD):
                act.wait_ge(s.scaled, k + 1)
                act.activation(X[:, k, :], X[:, k, :], ACT.Identity, bias=core.param(bias, k), scale=core.param(gain, k))


def rms_norm(core, src, gain, dst):
    line = core.line
    with Stage(core, "rms") as st:
        sq = st.sb("sq", [P, KD, T])
        s = st.sems("squared total inv normed")
        total = core.psum[4]
        block = st.block()

        @block.tensor
        def _(pe):
            for k in range(KD):
                pe.wait_ge(s.squared, k + 1)
                mm = pe.matmul(total, core.const("ones"), sq[:, k, :], start=k == 0, stop=k == KD - 1)
            mm.then_inc(s.total, 1)

        @block.scalar
        def _(act):
            for k in range(KD):
                act.activation(sq[:, k, :], src[:, k, :], ACT.Square).then_inc(s.squared, 1)
            act.wait_ge(s.total, 1)
            inv_root(act, line[:], total, s.inv, core.eps_rms[:], 1.0 / D)

        @block.vector
        def _(dve):
            dve.wait_ge(s.inv, 2)
            for k in range(KD):
                dve.scalar_tensor_tensor(sq[:, k, :], src[:, k, :], core.param(gain, k), line[:], ALU.mult, ALU.mult).then_inc(s.normed, 1)
            for k in range(KD):
                dve.wait_ge(s.normed, k + 1)
                dve.tensor_tensor(dst[:, k, :], dst[:, k, :], sq[:, k, :], ALU.add)


def attention(core, name, heads, kinds, bias=None):
    nc = core.nc
    G = len(kinds)
    H = len(heads)
    K = heads[0]["k"].shape[0]
    tiles = [(h, qb) for h in range(H) for qb in range(NT)]

    def span(kind, qb):
        return (max(0, qb - 1), qb + 1) if kind == "band" else (0, qb + 1)

    with Stage(core, name) as st:
        prob = st.sb("prob", [P, 2, G, T])
        probt = st.sb("probt", [P, 2, NT, T])
        vtok = st.sb("vtok", [P, 2, NT, K])
        mx, nm = st.sb("mx", [P, 2, 2]), st.sb("nm", [P, 2, 1])
        ssum, tot, inv = st.sb("ssum", [P, 2, 4]), st.sb("tot", [P, 2, 1]), st.sb("inv", [P, 2, 1])
        s = st.sems("scored maxed negmax expd summed inverted added prob_ready turned turned_out mixed mixed_out")
        turn, mix = core.psum[6], core.psum[7]
        block = st.block()
        ident = core.const("ident")

        def sbank(i, g):
            return core.psum[3 * (i % 2) + g]

        def turn_of(i):
            return i + i // NT + 2

        @block.tensor
        def _(pe):
            def score(i):
                h, qb = tiles[i]
                hd = heads[h]
                if i >= 2:
                    pe.wait_ge(s.expd, i - 1)
                for g, kind in enumerate(kinds):
                    a, b = span(kind, qb)
                    n = (b - a) * P
                    out = sbank(i, g)[:, 0:n]
                    pe.matmul(out, hd["q"][g][:, qb * P:(qb + 1) * P], hd["k"][:, a * P:b * P], start=True, stop=False)
                    if bias:
                        lhs, rhs = bias(h)
                        pe.matmul(out, lhs, rhs[:, a * P:b * P], start=False, stop=False)
                    idb = core.mask("identb")
                    if kind == "causal":
                        mm = pe.matmul(sbank(i, g)[:, n - P:n], idb, core.mask("causal"), start=False, stop=True)
                    elif kind == "band":
                        if qb:
                            pe.matmul(sbank(i, g)[:, 0:P], idb, core.mask("prev"), start=False, stop=False)
                        mm = pe.matmul(sbank(i, g)[:, n - P:n], idb, core.mask("causal"), start=False, stop=True)
                    else:
                        mm = pe.matmul(out, idb, core.mask(kind)[:, NT * P - n:], start=False, stop=True)
                mm.then_inc(s.scored, 1)

            score(0)
            score(1)
            for i, (h, qb) in enumerate(tiles):
                v = heads[h]["v"]
                row = heads[h]["row"]
                rows = slice(row, row + K)
                if qb == 0:
                    if i:
                        pe.wait_ge(s.turned_out, turn_of(i) - 2)
                    for b in range(NT):
                        mm = pe.transpose(turn[:, b * K:(b + 1) * K], v[:, b * P:(b + 1) * P], ident[rows, row:row + K])
                    mm.then_inc(s.turned, 1)
                if i + 2 < len(tiles):
                    score(i + 2)
                pe.wait_ge(s.turned_out, turn_of(i) - 1)
                pe.wait_ge(s.prob_ready, i + 1)
                for b in range(qb + 1):
                    mm = pe.transpose(turn[:, b * P:(b + 1) * P], prob[:, i % 2, G - 1, b * P:(b + 1) * P], ident)
                mm.then_inc(s.turned, 1)
                if qb == NT - 1:
                    pe.wait_ge(s.turned_out, turn_of(i))
                    if h:
                        pe.wait_ge(s.mixed_out, h)
                    for b in range(NT):
                        mm = pe.matmul(mix[rows, b * P:T], vtok[:, h % 2, b, :], probt[:, h % 2, b, b * P:T],
                                       start=b == 0, stop=b == NT - 1)
                    mm.then_inc(s.mixed, 1)

        @block.vector
        def _(dve):
            def top(i):
                h, qb = tiles[i]
                p = i % 2
                dve.wait_ge(s.scored, i + 1)
                if i >= 2:
                    dve.wait_ge(s.expd, i - 1)
                n = (qb + 1) * P
                if G == 1:
                    done(dve, dve.tensor_reduce(nm[:, p, :], sbank(i, 0)[:, 0:n], AX.X, ALU.max, negate=True), s.negmax)
                    return
                a, b = span(kinds[0], qb)
                done(dve, dve.tensor_reduce(mx[:, p, 0:1], sbank(i, 0)[:, 0:(b - a) * P], AX.X, ALU.max), s.maxed)
                done(dve, dve.tensor_reduce(mx[:, p, 1:2], core.banks[:, 3 * p + 1:3 * p + 3, 0:n], AX.XY, ALU.max), s.maxed)
                dve.wait_ge(s.maxed, 2 * i + 2)
                done(dve, dve.tensor_reduce(nm[:, p, :], mx[:, p, :], AX.X, ALU.max, negate=True), s.negmax)

            top(0)
            top(1)
            for i, (h, qb) in enumerate(tiles):
                p = i % 2
                n = (qb + 1) * P
                dve.wait_ge(s.expd, i + 1)
                total = ssum[:, p, 0:1]
                last = prob[:, p, G - 1, 0:n]
                if G > 1:
                    total = tot[:, p, :]
                    done(dve, dve.tensor_reduce(total, ssum[:, p, 0:G], AX.X, ALU.add), s.summed)
                    done(dve, dve.tensor_tensor(last, last, prob[:, p, 1, 0:n], ALU.add), s.added)
                    dve.wait_ge(s.summed, i + 1)
                done(dve, dve.reciprocal(inv[:, p, :], total), s.inverted)
                if G > 1:
                    a, b = span(kinds[0], qb)
                    dve.wait_ge(s.added, 2 * i + 1)
                    part = prob[:, p, G - 1, a * P:b * P]
                    done(dve, dve.tensor_tensor(part, part, prob[:, p, 0, 0:(b - a) * P], ALU.add), s.added)
                    dve.wait_ge(s.added, 2 * i + 2)
                dve.wait_ge(s.inverted, i + 1)
                done(dve, dve.tensor_scalar(last, last, inv[:, p, :], None, ALU.mult), s.prob_ready)
                if i + 2 < len(tiles):
                    top(i + 2)

        @block.scalar
        def _(act):
            def expo(i):
                h, qb = tiles[i]
                p = i % 2
                act.wait_ge(s.negmax, i + 1)
                if i >= 2:
                    act.wait_ge(s.turned, turn_of(i - 2))
                for g, kind in enumerate(kinds):
                    a, b = span(kind, qb)
                    n = (b - a) * P
                    e = act.activation(prob[:, p, g, 0:n], sbank(i, g)[:, 0:n], ACT.Exp, bias=nm[:, p, :],
                                       accum_out=ssum[:, p, g:g + 1])
                e.then_inc(s.expd, 1)

            expo(0)
            expo(1)
            for i, (h, qb) in enumerate(tiles):
                if qb == 0:
                    act.wait_ge(s.turned, turn_of(i) - 1)
                    done(act, act.activation(vtok[:, h % 2, :, :], turn[:, 0:NT * K].rearrange("p (b k) -> p b k", k=K), ACT.Copy), s.turned_out)
                act.wait_ge(s.turned, turn_of(i))
                done(act, act.activation(probt[:, h % 2, 0:qb + 1, qb * P:(qb + 1) * P],
                               turn[:, 0:(qb + 1) * P].rearrange("p (b k) -> p b k", k=P), ACT.Copy), s.turned_out)
                if i + 2 < len(tiles):
                    expo(i + 2)
                if qb == NT - 1:
                    act.wait_ge(s.mixed, h + 1)
                    out = heads[h]["out"]
                    row = heads[h]["row"]
                    rows = slice(row, row + K)
                    done(act, act.activation(out, mix[rows, :], ACT.Copy), s.mixed_out)


DECAY = float(np.exp(-0.5))


def rwkv(core, Z, O):
    nc, Y = core.nc, core.Y
    heads = [(c, e) for c in range(4) for e in range(2)]
    half = lambda e: slice(64 * e, 64 * e + 64)
    chunked = lambda ap: ap.rearrange("p c (n t) -> p c n t", t=C)
    with Stage(core, "rwkv") as st:
        AR = st.sb("AR", [P, 4, NCH, 2, C])
        tokB, tokK, tokV = (st.sb(n, [P, 4, NCH, C]) for n in ("tokB", "tokK", "tokV"))
        Q = st.sb("Q", [P, 2, NCH, C])
        diag = [st.sb(f"diag{i}", [P, NCH, P]) for i in range(2)]
        prod = [Y[:, 7, :].rearrange("p (n t) -> p n t", t=C), Z[:, 12, :].rearrange("p (n t) -> p n t", t=C)]
        elast = st.sb("elast", [P, 4, NCH])
        Hs = [Q[:, 0, 0:4], Q[:, 0, 4:8]]
        Dsb, SA = Q[:, 1, 0:4], Q[:, 1, 4:8]
        small = Y[:, 4:7, :]
        lora = lambda rows, c: small[rows, 0, c * P:(c + 1) * P]
        r, k, v = Z[:, 0:4, :], Z[:, 4:8, :], Z[:, 8:12, :]
        lw, a, kk = Z[:, 15:19, :], Z[:, 19:23, :], Z[:, 23:27, :]
        flat = lambda ap: ap[:].rearrange("p c n t -> p c (n t)")
        cum, norm, temp = flat(tokB), flat(tokK), flat(tokV)
        at, rt = AR[:, :, :, 0, :], AR[:, :, :, 1, :]
        bt, kt, bonus = kk, k, O[:, 0:4, :]
        Nt, X = chunked(kk), chunked(k)
        Arb, Aak, Ark = chunked(lw), chunked(a), chunked(r)
        XT = chunked(Y[:, 0:4, :])
        s = st.sems("small_in tanhed decay_in rate_in rate decay cum before e_before e_in e_neg elast_kept "
                    "kk_raw kk_squared kk_sum kk_clamped kk_inv kk_unit at_ready rate_less k_new rk rk_sum bonus_ready "
                    "b_ready bt_ready kt_ready rt_ready tok tok_out zeroed b_diag k_diag b_pairs a_pairs k_pairs masked x_first "
                    "q_ready q_out x_prod xt_prod x_next "
                    "d_ready d_out sa_ready sa_out h_ready h_sum h_out y_ready y_out "
                    "gate_sig gate mean centred squared var log inv y_scaled y_affine y_bonus")
        def wide(g):
            b = (0, 3, 5)[g % 3]
            return core.banks[:, b:b + 2, :].rearrange("p b (n m) -> p (b n) m", m=P)

        def narrow(c):
            return core.psum[(2, 7)[c % 2]].rearrange("p (n t) -> p n t", t=C)

        def xt_prods(n):
            return 2 * n if n <= 16 else 16 + n

        def diagonal(act, to, src, sem):
            for e in range(2):
                act.activation(to[half(e), :, 64 * e:64 * e + 64], src[half(e)], ACT.Copy).then_inc(sem, 1)

        def pool(gp):
            for i in range(2):
                gp.memset(diag[i][:], 0.0).then_inc(s.zeroed, 1)

        block = st.block(pool)
        ident = core.const("ident")

        def level_products(pe, n, c):
            last = n > 16
            pe.wait_ge(s.q_out, n)
            if n > 2:
                pe.wait_ge(s.xt_prod, xt_prods(n - 2))
            for i in range(NCH):
                cols = slice(i * C, (i + 1) * C)
                if not last:
                    for e in range(2):
                        pe.matmul(core.psum[2 + c % 2][half(e), cols], XT[half(e), c, i], Q[half(e), c % 2, i], start=True, stop=True)
                for e in range(2):
                    mm = pe.matmul(core.psum[4 + c % 2][half(e), cols], Q[half(e), c % 2, i], XT[half(e), c, i], start=True, stop=True)
            mm.then_inc(s.x_prod, 1)

        @block.sync
        def _(sp):
            sp.dma_start(small, core.io["small"].rearrange("p (j t) -> p j t", t=T)[:, 0:3, :]).then_inc(s.small_in, 16)

        def lvl(name, i, n=NCH):
            m = core.const(name)[:, i * C:(i + 1) * C]
            return m.rearrange("p (o t) -> p o t", o=1).broadcast_to([P, n, C])

        @block.scalar
        def _(act):
            done(act, act.activation(Z[0:64, 12, :], Z[0:64, 12, :], ACT.Tanh), s.tanhed)
            for c in range(4):
                act.wait_ge(s.rate_in, c + 1)
                done(act, act.activation(a[:, c, :], core.psum[4 + c], ACT.Sigmoid, bias=core.param("a0", c)), s.rate)
            for c in range(4):
                act.wait_ge(s.decay_in, c + 1)
                done(act, act.activation(lw[:, c, :], core.psum[c], ACT.Sigmoid, bias=core.param("w0", c)), s.decay)
            act.wait_ge(s.kk_raw, 4)
            done(act, act.activation(norm, kk, ACT.Square), s.kk_squared)
            act.wait_ge(s.kk_clamped, 1)
            inv_root(act, norm, norm, s.kk_inv)
            for c in range(4):
                act.wait_ge(s.cum, c + 1)
                done(act, act.activation(rt[:, c], tokB[:, c], ACT.Exp, scale=-DECAY), s.e_in)
            act.wait_ge(s.before, 1)
            for c in range(4):
                done(act, act.activation(at[:, c], chunked(lw)[:, c], ACT.Exp, scale=-DECAY), s.e_before)
            act.wait_ge(s.e_before, 4)
            done(act, act.activation(lw, cum, ACT.Exp, scale=DECAY), s.e_neg)
            for i, to in enumerate((tokV, tokB, tokK)):
                for c in range(4):
                    act.wait_ge(s.tok, 4 * i + c + 1)
                    done(act, act.activation(to[:, c], core.psum[4 + (4 * i + c) % 4].rearrange("p (n t) -> p n t", t=C), ACT.Copy), s.tok_out)
            act.wait_ge(s.zeroed, 2)
            for c in range(4):
                if c:
                    act.wait_ge(s.b_pairs, c)
                else:
                    act.wait_ge(s.bt_ready, 1)
                diagonal(act, diag[0], chunked(bt)[:, c], s.b_diag)
                if c:
                    act.wait_ge(s.k_pairs, c)
                else:
                    act.wait_ge(s.kt_ready, 1)
                diagonal(act, diag[1], chunked(kt)[:, c], s.k_diag)
            for n in range(1, 21):
                c = (n - 1) % 4
                bank = core.psum[c % 2].rearrange("p (n t) -> p n t", t=C)
                act.wait_ge(s.q_ready, n)
                if n > 2:
                    act.wait_ge(s.x_prod, n - 2)
                done(act, act.activation(Q[:, c % 2], bank, ACT.Copy), s.q_out)
            for n in range(NCH):
                act.wait_ge(s.d_ready, n + 1)
                done(act, act.activation(Dsb[:], core.psum[0][:, 0:4 * C].rearrange("p (c t) -> p c t", t=C), ACT.Copy), s.d_out)
                act.wait_ge(s.sa_ready, n + 1)
                done(act, act.activation(SA[:], core.psum[1][:, 0:4 * C].rearrange("p (c t) -> p c t", t=C), ACT.Copy), s.sa_out)
                act.wait_ge(s.y_ready, n + 1)
                done(act, act.activation(at[:, :, n, :], core.psum[3][:, 0:4 * C].rearrange("p (c t) -> p c t", t=C), ACT.Copy), s.y_out)
            done(act, act.activation(Z[:, 13, :], Z[:, 13, :], ACT.Sigmoid), s.gate_sig)
            done(act, act.activation(Z[0:32, 14, :], Z[0:32, 14, :], ACT.Sigmoid), s.gate_sig)
            for c in range(4):
                act.wait_ge(s.centred, c + 1)
                done(act, act.activation(rt[:, c], at[:, c], ACT.Square), s.squared)
            for c in range(4):
                act.wait_ge(s.var, c + 1)
                done(act, act.activation(r[:, c, :], core.psum[c], ACT.Ln, bias=core.eps_gn[:], scale=1.0 / 64), s.log)
            for c in range(4):
                act.activation(r[:, c, :], r[:, c, :], ACT.Exp, scale=-0.5).then_inc(s.inv, 1)

        @block.vector
        def _(dve):
            for c in range(4):
                done(dve, dve.tensor_scalar(kk[:, c, :], k[:, c, :], core.param("kk", c), None, ALU.mult), s.kk_raw)
            for c in range(4):
                dve.wait_ge(s.rate, c + 1)
                done(dve, dve.tensor_scalar(temp[:, c, :], a[:, c, :], -1.0, core.param("ka", c), ALU.add, ALU.mult), s.rate_less)
            dve.wait_ge(s.kk_squared, 1)
            dve.wait_ge(s.rate_less, 4)
            done(dve, dve.scalar_tensor_tensor(k, temp, 1.0, k, ALU.add, ALU.mult), s.k_new)
            for c in range(4):
                dve.wait_ge(s.decay, c + 1)
                done(dve, dve.tensor_tensor_scan(cum[:, c, :], core.const("chunk"), lw[:, c, :], 0.0, ALU.mult, ALU.add), s.cum)
            dve.wait_ge(s.cum, 4)
            done(dve, dve.tensor_tensor(lw, cum, lw, ALU.subtract), s.before)
            dve.wait_ge(s.kk_sum, 4)
            done(dve, dve.tensor_scalar(norm, core.banks[:, 4:8, :], 1e-24, None, ALU.max), s.kk_clamped)
            dve.wait_ge(s.k_new, 1)
            for c in range(4):
                done(dve, dve.scalar_tensor_tensor(temp[:, c, :], r[:, c, :], core.param("rk", c), k[:, c, :], ALU.mult, ALU.mult), s.rk)
            dve.wait_ge(s.kk_inv, 2)
            done(dve, dve.tensor_tensor(kk, kk, norm, ALU.mult), s.kk_unit)
            dve.wait_ge(s.e_before, 4)
            done(dve, dve.scalar_tensor_tensor(at, chunked(kk), -1.0, at, ALU.mult, ALU.mult), s.at_ready)
            dve.wait_ge(s.e_in, 4)
            done(dve, dve.tensor_copy(elast[:], rt[:, :, :, C - 1]), s.elast_kept)
            done(dve, dve.tensor_tensor(rt, rt, chunked(r), ALU.mult), s.rt_ready)
            done(dve, dve.tensor_tensor(kk, kk, a, ALU.mult), s.b_ready)
            dve.wait_ge(s.e_neg, 1)
            done(dve, dve.tensor_tensor(bt, kk, lw, ALU.mult), s.bt_ready)
            done(dve, dve.tensor_tensor(kt, k, lw, ALU.mult), s.kt_ready)
            dve.wait_ge(s.rk_sum, 4)
            done(dve, dve.tensor_tensor(bonus, core.banks[:, 0:4, :], v, ALU.mult), s.bonus_ready)
            dve.wait_ge(s.tok_out, 12)
            for c in range(4):
                bb, kb = wide(2 * c), wide(2 * c + 1)
                m = lambda i: core.const("rmask")[:, i * C:(i + 1) * C].rearrange("p (o t) -> p o t", o=1).broadcast_to([P, NCH, C])
                dve.wait_ge(s.b_pairs, c + 1)
                done(dve, dve.tensor_tensor(XT[:, c], bb[:, :, 0:C], lvl("lmask", 0), ALU.mult), s.masked)
                done(dve, dve.tensor_tensor(Arb[:, c], bb[:, :, C:P], m(1), ALU.mult), s.masked)
                dve.wait_ge(s.a_pairs, c + 1)
                done(dve, dve.tensor_tensor(Nt[:, c], bb[:, :, 0:C], m(0), ALU.mult), s.masked)
                dve.wait_ge(s.k_pairs, c + 1)
                done(dve, dve.tensor_tensor(Aak[:, c], kb[:, :, 0:C], m(2), ALU.mult), s.masked)
                done(dve, dve.tensor_tensor(Ark[:, c], kb[:, :, C:P], m(3), ALU.mult), s.masked)
                done(dve, dve.tensor_tensor(X[:, c], narrow(c), lvl("lmaskt", 0), ALU.mult), s.masked)
                done(dve, dve.tensor_tensor(X[:, c], X[:, c], lvl("lmask", 6), ALU.add), s.x_first)
                done(dve, dve.tensor_tensor(XT[:, c], XT[:, c], lvl("lmask", 6), ALU.add), s.x_first)
            n = 0
            for l in range(1, 6):
                for c in range(4):
                    n += 1
                    view = lambda i: core.psum[i].rearrange("p (n t) -> p n t", t=C)
                    dve.wait_ge(s.x_prod, n)
                    if l < 5:
                        dve.tensor_tensor(prod[0][:], view(2 + c % 2), lvl("lmaskt", l), ALU.mult).then_inc(s.xt_prod, 1)
                    dve.tensor_tensor(prod[1][:], view(4 + c % 2), lvl("lmask", l), ALU.mult).then_inc(s.xt_prod, 1)
                    dve.wait_ge(s.xt_prod, xt_prods(n))
                    if l < 5:
                        dve.tensor_tensor(X[:, c], X[:, c], prod[0][:], ALU.add).then_inc(s.x_next, 1)
                    dve.tensor_tensor(XT[:, c], XT[:, c], prod[1][:], ALU.add).then_inc(s.x_next, 1)
                    dve.wait_ge(s.x_next, xt_prods(n))
            for n in range(NCH - 1):
                new, old = Hs[(n + 1) % 2], Hs[n % 2]
                dve.wait_ge(s.h_ready, n + 1)
                bank = core.psum[2][:, 0:4 * C].rearrange("p (c t) -> p c t", t=C)
                last = elast[:, :, n:n + 1].broadcast_to([P, 4, C])
                if n:
                    dve.wait_ge(s.y_ready, n)
                    done(dve, dve.tensor_tensor(new[:], bank, old[:], ALU.add), s.h_sum)
                    dve.wait_ge(s.h_sum, n)
                    done(dve, dve.tensor_tensor(new[:], new[:], last, ALU.mult), s.h_out)
                    dve.wait_ge(s.h_out, n + 1)
                else:
                    done(dve, dve.tensor_tensor(new[:], bank, last, ALU.mult), s.h_out)
                    dve.wait_ge(s.h_out, 1)
            for c in range(4):
                dve.wait_ge(s.mean, c + 1)
                bank = core.psum[c].rearrange("p (n t) -> p n t", t=C)
                done(dve, dve.scalar_tensor_tensor(at[:, c], bank, -1.0 / 64, at[:, c], ALU.mult, ALU.add), s.centred)
            for c in range(4):
                dve.wait_ge(s.inv, c + 1)
                done(dve, dve.tensor_tensor(at[:, c], at[:, c], chunked(r)[:, c], ALU.mult), s.y_scaled)
                done(dve, dve.tensor_scalar(at[:, c], at[:, c], core.param("gng", c), core.param("gnb", c), ALU.mult, ALU.add), s.y_affine)
                o = chunked(O[:, 0:4, :])[:, c]
                done(dve, dve.tensor_tensor(o, o, at[:, c], ALU.add), s.y_bonus)
                dve.wait_ge(s.gate, c + 1)
                dve.tensor_tensor(O[:, c, :], O[:, c, :], core.psum[4 + c], ALU.mult)

        @block.tensor
        def _(pe):
            pe.wait_ge(s.small_in, 16)
            for c in range(4):
                pe.matmul(core.psum[4 + c], lora(slice(64, 128), c), Z[64:128, 12, :], start=True, stop=True).then_inc(s.rate_in, 1)
            pe.wait_ge(s.tanhed, 1)
            for c in range(4):
                pe.matmul(core.psum[c], lora(slice(0, 64), c), Z[0:64, 12, :], start=True, stop=True).then_inc(s.decay_in, 1)
            pe.wait_ge(s.kk_squared, 1)
            pe.wait_ge(s.rate, 4)
            for c in range(4):
                pe.matmul(core.psum[4 + c], core.const("blk"), norm[:, c, :], start=True, stop=True).then_inc(s.kk_sum, 1)
            pe.wait_ge(s.decay, 4)
            for c in range(4):
                pe.wait_ge(s.rk, c + 1)
                pe.matmul(core.psum[c], core.const("blk"), temp[:, c, :], start=True, stop=True).then_inc(s.rk_sum, 1)

            def tok(i, src):
                for c in range(4):
                    if i + c:
                        pe.wait_ge(s.tok_out, max(1, 4 * i + c - 3))
                    for n in range(NCH):
                        for e in range(2):
                            mm = pe.matmul(core.psum[4 + (4 * i + c) % 4][half(e), n * C:(n + 1) * C],
                                           src[half(e), c, n * C:(n + 1) * C], ident[half(e), 64 * e:64 * e + 64], start=True, stop=True)
                    mm.then_inc(s.tok, 1)

            pe.wait_ge(s.kk_clamped, 1)
            tok(0, v)
            pe.wait_ge(s.bt_ready, 1)
            tok(1, bt)
            pe.wait_ge(s.kt_ready, 1)
            tok(2, kt)
            pe.wait_ge(s.at_ready, 1)
            pe.wait_ge(s.rt_ready, 1)
            pe.wait_ge(s.bonus_ready, 1)
            pe.wait_ge(s.tok_out, 12)
            for c in range(4):
                def group(diag_, rhs, out, ready, sem):
                    pe.wait_ge(ready, 2 * c + 2)
                    for n in range(NCH):
                        mm = pe.matmul(out(n), diag_[:, n, :], rhs(n), start=True, stop=True)
                    mm.then_inc(sem, 1)

                both = lambda n: AR[:, c, n].rearrange("p a t -> p (a t)")
                if c > 1:
                    pe.wait_ge(s.masked, 6 * (c - 2) + 5)
                group(diag[0], both, lambda n: wide(2 * c)[:, n, :], s.b_diag, s.b_pairs)
                if c > 1:
                    pe.wait_ge(s.masked, 6 * (c - 2) + 6)
                for n in range(NCH):
                    for e in range(2):
                        mm = pe.matmul(narrow(c)[half(e), n, :], AR[half(e), c, n, 0, :], bt[half(e), c, n * C:(n + 1) * C], start=True, stop=True)
                mm.then_inc(s.a_pairs, 1)
                if c > 0:
                    pe.wait_ge(s.masked, 6 * (c - 1) + 3)
                group(diag[1], both, lambda n: wide(2 * c + 1)[:, n, :], s.k_diag, s.k_pairs)
            n = 0
            pe.wait_ge(s.masked, 24)
            for l in range(1, 6):
                for c in range(4):
                    n += 1
                    pe.wait_ge(s.x_first, 2 * c + 2)
                    if l > 1:
                        pe.wait_ge(s.x_next, 2 * (n - 4))
                    if n > 2:
                        pe.wait_ge(s.q_out, n - 2)
                    for i in range(NCH):
                        for e in range(2):
                            mm = pe.matmul(core.psum[c % 2][half(e), i * C:(i + 1) * C], Nt[half(e), c, i], X[half(e), c, i], start=True, stop=True)
                    mm.then_inc(s.q_ready, 1)
                    if n > 1:
                        level_products(pe, n - 1, (c - 1) % 4)
            level_products(pe, n, 3)
            pe.wait_ge(s.x_next, xt_prods(20))
            for n in range(NCH):
                H = Hs[n % 2]
                if n:
                    pe.wait_ge(s.h_out, n)
                    pe.wait_ge(s.d_out, n)
                for c, e in heads:
                    out = core.psum[0][half(e), c * C:(c + 1) * C]
                    if n:
                        pe.matmul(out, AR[half(e), c, n, 0, :], H[half(e), c, :], start=True, stop=False)
                    mm = pe.matmul(out, Aak[half(e), c, n], tokV[half(e), c, n], start=n == 0, stop=True)
                mm.then_inc(s.d_ready, 1)
                pe.wait_ge(s.d_out, n + 1)
                if n:
                    pe.wait_ge(s.sa_out, n)
                for c, e in heads:
                    mm = pe.matmul(core.psum[1][half(e), c * C:(c + 1) * C], XT[half(e), c, n], Dsb[half(e), c, :], start=True, stop=True)
                mm.then_inc(s.sa_ready, 1)
                pe.wait_ge(s.sa_out, n + 1)
                if n < NCH - 1:
                    for c, e in heads:
                        out = core.psum[2][half(e), c * C:(c + 1) * C]
                        pe.matmul(out, tokK[half(e), c, n], tokV[half(e), c, n], start=True, stop=False)
                        mm = pe.matmul(out, tokB[half(e), c, n], SA[half(e), c, :], start=False, stop=True)
                    mm.then_inc(s.h_ready, 1)
                if n:
                    pe.wait_ge(s.y_out, n)
                for c, e in heads:
                    out = core.psum[3][half(e), c * C:(c + 1) * C]
                    pe.matmul(out, tokV[half(e), c, n], Ark[half(e), c, n], start=True, stop=False)
                    if n:
                        pe.matmul(out, H[half(e), c, :], AR[half(e), c, n, 1, :], start=False, stop=False)
                    mm = pe.matmul(out, SA[half(e), c, :], Arb[half(e), c, n], start=False, stop=True)
                mm.then_inc(s.y_ready, 1)
            pe.wait_ge(s.gate_sig, 2)
            for c in range(4):
                pe.matmul(core.psum[4 + c], small[:, 1, c * P:(c + 1) * P], Z[:, 13, :], start=True, stop=False)
                pe.matmul(core.psum[4 + c], small[0:32, 2, c * P:(c + 1) * P], Z[0:32, 14, :], start=False, stop=True).then_inc(s.gate, 1)
            for c in range(4):
                pe.wait_ge(s.y_out, NCH)
                pe.matmul(core.psum[c], core.const("blk"), at[:, c], start=True, stop=True).then_inc(s.mean, 1)
            for c in range(4):
                pe.wait_ge(s.squared, c + 1)
                pe.matmul(core.psum[c], core.const("blk"), rt[:, c], start=True, stop=True).then_inc(s.var, 1)




def gate_rows(core, Z, G):
    with Stage(core, "gates") as st:
        x, l = st.sb("x", [P, T]), st.sb("l", [P, T])
        s = st.sems("biased part ln logsig summed moved source maxed out")
        block = st.block()
        ml = slice(32, 36)

        @block.scalar
        def _(act):
            done(act, act.activation(x[:], Z[:, 24, :], ACT.Identity, bias=core.param("gateb")), s.biased)
            done(act, act.activation(l[:], x[:], ACT.Abs), s.part)
            done(act, act.activation(l[:], l[:], ACT.Exp, scale=-1.0), s.part)
            done(act, act.activation(l[:], l[:], ACT.Ln, bias=1.0), s.ln)

        @block.vector
        def _(dve):
            dve.wait_ge(s.ln, 1)
            done(dve, dve.scalar_tensor_tensor(l[:], x[:], 0.0, l[:], ALU.min, ALU.subtract), s.logsig)
            one = core.const("ones")[:, 0:1].broadcast_to([P, T])
            done(dve, dve.tensor_tensor_scan(G[:, 1, :], one, l[:], 0.0, ALU.mult, ALU.add), s.summed)
            done(dve, dve.tensor_copy(l[ml], G[64:68, 1, :]), s.moved)
            done(dve, dve.tensor_tensor(G[ml, 0, :], x[ml], l[ml], ALU.subtract), s.source)
            done(dve, dve.tensor_tensor_scan(x[ml], G[ml, 0, :], G[ml, 0, :], 0.0, ALU.max, ALU.max), s.maxed)
            done(dve, dve.tensor_scalar(G[0:4, 1, :], G[0:4, 1, :], -1.0, None, ALU.mult), s.out)
            done(dve, dve.tensor_scalar(G[ml, 2, :], x[ml], -1.0, None, ALU.mult), s.out)
            done(dve, dve.scalar_tensor_tensor(G[ml, 3, :], l[ml], -1.0, G[ml, 2, :], ALU.mult, ALU.add), s.out)


def mlstm(core, Z, G):
    Y = core.Y
    with Stage(core, "mlstm") as st:
        conv = st.sb("conv", [P, 4, T])
        sig = st.sb("sig", [P, 4, T])
        vtok = st.sb("vtok", [P, 2, NT, P])
        gtok = st.sb("gtok", [P, NT, 4])
        E, PT = (st.sb(n, [P, 2, T]) for n in ("E", "PT"))
        low, den = st.sb("low", [P, T]), st.sb("den", [P, T])
        s = st.sems("conv sig silu vt vt_out gt gt_out scores weight weight_done heads_sum lows low_out den_out inv h_out")
        items = [(h, j) for h in range(4) for j in range(NT)]
        rows = lambda e: slice(64 * e, 64 * e + 64)
        block = st.block()

        @block.vector
        def _(dve):
            for c in range(4):
                tap = lambda j: core.param("conv", 4 * c + j)
                done(dve, dve.tensor_scalar(conv[:, c, :], Z[:, 16 + c, :], tap(3), None, ALU.mult), s.conv)
                for back in (1, 2, 3):
                    done(dve, dve.scalar_tensor_tensor(conv[:, c, back:], Z[:, 16 + c, 0:T - back], tap(3 - back), conv[:, c, back:],
                                                       ALU.mult, ALU.add), s.conv)
            for c in range(4):
                dve.wait_ge(s.sig, c + 1)
                scale = 1.0 if c < 2 else 64 ** -0.5
                done(dve, dve.scalar_tensor_tensor(conv[:, c, :], conv[:, c, :], scale, sig[:, c, :], ALU.mult, ALU.mult), s.silu)
            for i, (h, j) in enumerate(items):
                n = T - j * P
                dve.wait_ge(s.weight, i + 1)
                dve.wait_ge(s.scores, i + 1)
                if i >= 2:
                    dve.wait_ge(s.heads_sum, i - 1)
                done(dve, dve.tensor_tensor(PT[:, i % 2, 0:n], E[:, i % 2, 0:n], core.psum[i % 2][:, 0:n], ALU.mult), s.weight_done)
                if i % 8 == 7:
                    c = h // 2
                    dve.wait_ge(s.heads_sum, i + 1)
                    dve.wait_ge(s.low_out, 2 * c + 2)
                    done(dve, dve.tensor_tensor(den[:], den[:], low[:], ALU.max), s.den_out)
                    done(dve, dve.reciprocal(den[:], den[:]), s.inv)
                    done(dve, dve.tensor_tensor(Y[:, 6 + c, :], core.psum[4], den[:], ALU.mult), s.h_out)

        @block.scalar
        def _(act):
            for c in range(2):
                act.wait_ge(s.vt, c + 1)
                done(act, act.activation(vtok[:, c], core.psum[7].rearrange("p (b k) -> p b k", k=P), ACT.Copy), s.vt_out)
            act.wait_ge(s.gt, 1)
            done(act, act.activation(gtok[:], core.psum[6][:, 0:4 * NT].rearrange("p (b k) -> p b k", k=4), ACT.Copy), s.gt_out)
            for c in range(4):
                act.wait_ge(s.conv, 4 * c + 4)
                done(act, act.activation(sig[:, c, :], conv[:, c, :], ACT.Sigmoid), s.sig)
            for i, (h, j) in enumerate(items):
                n = T - j * P
                act.wait_ge(s.scores, i + 1)
                if i >= 2:
                    act.wait_ge(s.weight_done, i - 1)
                done(act, act.activation(E[:, i % 2, 0:n], core.psum[2 + i % 2][:, 0:n], ACT.Exp, bias=gtok[:, j, h:h + 1]), s.weight)
                if i % 8 == 7:
                    act.wait_ge(s.lows, h // 2 + 1)
                    if h > 1:
                        act.wait_ge(s.h_out, h // 2)
                    done(act, act.activation(low[:], core.psum[6], ACT.Exp), s.low_out)
                    act.wait_ge(s.heads_sum, i + 1)
                    done(act, act.activation(den[:], core.psum[5], ACT.Abs), s.low_out)

        @block.tensor
        def _(pe):
            ident = core.const("ident")
            for c in range(2):
                if c:
                    pe.wait_ge(s.vt_out, c)
                for b in range(NT):
                    mm = pe.transpose(core.psum[7][:, b * P:(b + 1) * P], Z[:, 20 + c, b * P:(b + 1) * P], ident)
                mm.then_inc(s.vt, 1)
            ml = slice(32, 36)
            for b in range(NT):
                mm = pe.matmul(core.psum[6][:, 4 * b:4 * b + 4], G[ml, 0, b * P:(b + 1) * P], ident[ml, 32:36], start=True, stop=True)
            mm.then_inc(s.gt, 1)
            pe.wait_ge(s.silu, 4)
            pe.wait_ge(s.gt_out, 1)
            pe.wait_ge(s.vt_out, 2)
            sel = core.const("sel").rearrange("p (h k) -> p h k", k=P)

            def score(i):
                h, j = items[i]
                c, e = h // 2, h % 2
                if i >= 2:
                    pe.wait_ge(s.weight_done, i - 1)
                n = T - j * P
                pe.matmul(core.psum[i % 2][:, 0:n], conv[rows(e), 2 + c, j * P:(j + 1) * P], conv[rows(e), c, j * P:T], start=True, stop=True)
                pe.matmul(core.psum[2 + i % 2][:, 0:n], sel[ml, h, :], G[ml, 2, j * P:T], start=True, stop=False)
                pe.matmul(core.psum[2 + i % 2][:, 0:P], core.mask("identb"), core.mask("prev"), start=False, stop=True).then_inc(s.scores, 1)

            score(0)
            for i, (h, j) in enumerate(items):
                c, e = h // 2, h % 2
                if i + 1 < len(items):
                    score(i + 1)
                if i % 8 == 0 and c:
                    pe.wait_ge(s.h_out, c)
                pe.wait_ge(s.weight_done, i + 1)
                n = T - j * P
                cols = slice(j * P, T)
                if i % 8 == 7:
                    for ee in range(2):
                        mm = pe.matmul(core.psum[6][rows(ee), :], sel[ml, 2 * c + ee, 0:64], G[ml, 3, :], start=True, stop=True)
                    mm.then_inc(s.lows, 1)
                pe.matmul(core.psum[4][rows(e), cols], vtok[:, c, j, rows(e)], PT[:, i % 2, 0:n], start=j == 0, stop=j == NT - 1)
                pe.matmul(core.psum[5][rows(e), cols], core.const("ones")[:, 0:64], PT[:, i % 2, 0:n], start=j == 0,
                          stop=j == NT - 1).then_inc(s.heads_sum, 1)


def hgrn2(core, Z):
    Y = core.Y
    with Stage(core, "hgrn") as st:
        b, kk, tmp, qe, ke = (st.sb(n, [P, 2, T]) for n in ("b", "k", "tmp", "qe", "ke"))
        W = [st.sb(f"W{i}", [P, 2, T]) for i in range(2)]
        S, part = st.sb("S", [P, 2, NCH, C]), st.sb("part", [P, 2, NCH, C])
        tokV, tokK = (st.sb(n, [P, 2, NCH, C]) for n in ("tokV", "tokK"))
        elast = st.sb("elast", [P, 2, NCH])
        H = [st.sb(f"H{i}", [P, 2, C]) for i in range(2)]
        Hd = st.sb("Hd", [P, 2, C])
        delta = [tmp, st.sb("delta", [P, 2, T])]
        s = st.sems("part k ln logsig b eb ebdone rest eke ke_done qe_done last delta expd half w_ready pairs masked summed "
                    "tok tok_out h_ready h_decayed h_out o_ready o_out")
        q, f, v = Z[:, 2:4, :], Z[:, 4:6, :], Z[:, 6:8, :]
        half = lambda e: slice(64 * e, 64 * e + 64)
        levels = (1, 2, 4, 8, 16, 32)
        chunks = lambda ap: ap.rearrange("p c (n t) -> p c n t", t=C)
        blocks = lambda ap, m: ap.rearrange("p c (n u) -> p (c n) u", u=2 * m)

        def pool(gp):
            gp.wait_ge(s.b, 2)
            for i, m in enumerate(levels):
                if i >= 2:
                    gp.wait_ge(s.expd, 2 * i - 2)
                d, bb = blocks(delta[i % 2][:], m), blocks(b[:], m)
                gp.tensor_tensor(d, bb, bb[:, :, m - 1:m].broadcast_to([P, T // m, 2 * m]), ALU.subtract).then_inc(s.delta, 1)
            gp.wait_ge(s.delta, len(levels))

        block = st.block(pool)
        ident = core.const("ident")

        @block.scalar
        def _(act):
            done(act, act.activation(tmp[:], f, ACT.Abs), s.part)
            done(act, act.activation(tmp[:], tmp[:], ACT.Exp, scale=-1.0), s.part)
            done(act, act.activation(tmp[:], tmp[:], ACT.Ln, bias=1.0), s.ln)
            done(act, act.activation(kk[:], f, ACT.Sigmoid, scale=-1.0), s.k)
            act.wait_ge(s.b, 2)
            done(act, act.activation(qe[:], b[:], ACT.Exp), s.eb)
            act.wait_ge(s.rest, 1)
            done(act, act.activation(ke[:], ke[:], ACT.Exp), s.eke)
            for i, m in enumerate(levels):
                w, d = blocks(W[i % 2][:], m), blocks(delta[i % 2][:], m)
                act.wait_ge(s.delta, i + 1)
                if i >= 2:
                    act.wait_ge(s.pairs, i)
                done(act, act.activation(w[:, :, 0:m], d[:, :, 0:m], ACT.Exp, scale=-1.0), s.expd)
                done(act, act.activation(w[:, :, m:], d[:, :, m:], ACT.Exp), s.expd)
            for i in range(4):
                act.wait_ge(s.tok, i + 1)
                to = (tokV, tokK)[i // 2]
                done(act, act.activation(to[:, i % 2], core.psum[4 + i].rearrange("p (n t) -> p n t", t=C), ACT.Copy), s.tok_out)
            act.wait_ge(s.o_ready, NCH)
            for c in range(2):
                done(act, act.activation(Y[:, 2 + c, :], core.psum[4 + c], ACT.Copy), s.o_out)

        @block.vector
        def _(dve):
            dve.wait_ge(s.ln, 1)
            done(dve, dve.scalar_tensor_tensor(tmp[:], f, 0.0, tmp[:], ALU.min, ALU.subtract), s.logsig)
            for c in range(2):
                done(dve, dve.tensor_tensor_scan(b[:, c, :], core.const("chunk"), tmp[:, c, :], 0.0, ALU.mult, ALU.add), s.b)
            b64 = blocks(b[:], 32)
            done(dve, dve.tensor_tensor(blocks(ke[:], 32), b64[:, :, C - 1:C].broadcast_to([P, 2 * NCH, C]), b64, ALU.subtract), s.rest)
            dve.wait_ge(s.eb, 1)
            done(dve, dve.tensor_copy(elast[:], chunks(qe[:])[:, :, :, C - 1]), s.last)
            done(dve, dve.tensor_tensor(qe[:], qe[:], q, ALU.mult), s.qe_done)
            dve.wait_ge(s.eke, 1)
            done(dve, dve.tensor_tensor(ke[:], ke[:], kk[:], ALU.mult), s.ke_done)

            def gather(i):
                dve.wait_ge(s.pairs, i + 1)
                m = 6 if i == 0 else i - 1
                mask = core.const("lmask")[:, m * C:(m + 1) * C].rearrange("p (o t) -> p o t", o=1).broadcast_to([P, 2 * NCH, C])
                bank = core.banks[:, 2 * (i % 2):2 * (i % 2) + 2, :].rearrange("p c (n t) -> p (c n) t", t=C)
                to = S if i == 0 else part
                done(dve, dve.tensor_tensor(to[:].rearrange("p c n t -> p (c n) t"), bank, mask, ALU.mult), s.masked)
                if i:
                    done(dve, dve.tensor_tensor(S[:], S[:], part[:], ALU.add), s.summed)

            for i, m in enumerate(levels):
                w = blocks(W[i % 2][:], m)
                dve.wait_ge(s.expd, 2 * i + 2)
                dve.tensor_tensor(w[:, :, 0:m], w[:, :, 0:m], blocks(kk[:], m)[:, :, 0:m], ALU.mult).then_inc(s.half, 1)
                done(dve, dve.tensor_tensor(w[:, :, m:], w[:, :, m:], blocks(q, m)[:, :, m:], ALU.mult), s.w_ready)
                gather(i)
            gather(6)
            for n in range(NCH - 1):
                new, old = H[(n + 1) % 2], H[n % 2]
                bank = core.psum[6 + n % 2][:, 0:2 * C].rearrange("p (c t) -> p c t", t=C)
                if n:
                    done(dve, dve.tensor_tensor(Hd[:], old[:], elast[:, :, n:n + 1].broadcast_to([P, 2, C]), ALU.mult), s.h_decayed)
                dve.wait_ge(s.h_ready, n + 1)
                if n:
                    dve.wait_ge(s.o_ready, n)
                    done(dve, dve.tensor_tensor(new[:], bank, Hd[:], ALU.add), s.h_out)
                else:
                    done(dve, dve.tensor_copy(new[:], bank), s.h_out)

        @block.tensor
        def _(pe):
            def pairs(i, lhs, rhs):
                if i >= 2:
                    pe.wait_ge(s.masked, i - 1)
                for c in range(2):
                    for n in range(NCH):
                        for e in range(2):
                            cols = slice(n * C, (n + 1) * C)
                            mm = pe.matmul(core.psum[2 * (i % 2) + c][half(e), cols], lhs[half(e), c, cols], rhs[half(e), c, cols], start=True, stop=True)
                mm.then_inc(s.pairs, 1)

            def tok(i, src, c):
                for n in range(NCH):
                    for e in range(2):
                        mm = pe.matmul(core.psum[4 + i][half(e), n * C:(n + 1) * C], src[half(e), c, n * C:(n + 1) * C],
                                       ident[half(e), 64 * e:64 * e + 64], start=True, stop=True)
                mm.then_inc(s.tok, 1)

            tok(0, v, 0)
            tok(1, v, 1)
            pe.wait_ge(s.k, 1)
            pairs(0, kk, q)
            pe.wait_ge(s.ke_done, 1)
            tok(2, ke, 0)
            tok(3, ke, 1)
            for i in range(6):
                pe.wait_ge(s.w_ready, i + 1)
                pairs(i + 1, W[i % 2], W[i % 2])
            pe.wait_ge(s.summed, 6)
            pe.wait_ge(s.qe_done, 1)
            pe.wait_ge(s.tok_out, 4)
            for n in range(NCH):
                if n < NCH - 1:
                    for c in range(2):
                        for e in range(2):
                            mm = pe.matmul(core.psum[6 + n % 2][half(e), c * C:(c + 1) * C], tokK[half(e), c, n], tokV[half(e), c, n], start=True, stop=True)
                    mm.then_inc(s.h_ready, 1)
                if n:
                    pe.wait_ge(s.h_out, n)
                for c in range(2):
                    for e in range(2):
                        cols = slice(n * C, (n + 1) * C)
                        out = core.psum[4 + c][half(e), cols]
                        mm = pe.matmul(out, tokV[half(e), c, n], S[half(e), c, n], start=True, stop=n == 0)
                        if n:
                            mm = pe.matmul(out, H[n % 2][half(e), c, :], qe[half(e), c, cols], start=False, stop=True)
                mm.then_inc(s.o_ready, 1)


TWO_PI_HI = 6.28125
TWO_PI_LO = 2 * np.pi - TWO_PI_HI
ROUND = 1.5 * 2.0 ** 23
PI_BELOW = 3.1415925


def s5_steps(core, st):
    names = "lr dt th k r r2 abr abi t1 t2 den"
    v = {n: st.sb(n, [P, 8]) for n in names.split()}
    one = lambda t: core.s5[t] if t in core.s5 else v[t][:]
    s = st.sems("dt mag angle cossin damping steps")

    def act_side(act):
        done(act, act.activation(one("dt"), core.param("ldt"), ACT.Exp), s.dt)
        act.wait_ge(s.damping, 1)
        done(act, act.activation(one("mag"), one("mag"), ACT.Exp), s.mag)
        act.wait_ge(s.angle, 1)
        done(act, act.activation(one("si"), one("r"), ACT.Sin), s.cossin)
        done(act, act.activation(one("co"), one("r2"), ACT.Sin), s.cossin)

    def dve_side(dve):
        def tt(out, a, b, op, sem=s.steps):
            done(dve, dve.tensor_tensor(out, a, b, op), sem)

        def ts(out, a, x, y, op0, op1=None, sem=s.steps):
            done(dve, dve.tensor_scalar(out, a, x, y, op0, op1) if op1 is not None else dve.tensor_scalar(out, a, x, y, op0), sem)

        li = core.param("lim")
        ts(one("lr"), core.param("lre"), -1e-4, None, ALU.min)
        dve.wait_ge(s.dt, 1)
        tt(one("mag"), one("lr"), one("dt"), ALU.mult, s.damping)
        tt(one("th"), li, one("dt"), ALU.mult)
        ts(one("k"), one("th"), 1 / (2 * np.pi), ROUND, ALU.mult, ALU.add)
        ts(one("k"), one("k"), -ROUND, None, ALU.add)
        done(dve, dve.scalar_tensor_tensor(one("r"), one("k"), -TWO_PI_HI, one("th"), ALU.mult, ALU.add), s.steps)
        done(dve, dve.scalar_tensor_tensor(one("r"), one("k"), -TWO_PI_LO, one("r"), ALU.mult, ALU.add), s.steps)
        ts(one("r"), one("r"), PI_BELOW, -PI_BELOW, ALU.min, ALU.max)
        ts(one("r2"), one("r"), float(np.pi / 2), None, ALU.add)
        ts(one("k"), one("r2"), PI_BELOW, -2 * np.pi, ALU.is_gt, ALU.mult)
        tt(one("r2"), one("r2"), one("k"), ALU.add)
        ts(one("r2"), one("r2"), PI_BELOW, -PI_BELOW, ALU.min, ALU.max, s.angle)
        dve.wait_ge(s.cossin, 2)
        dve.wait_ge(s.mag, 1)
        tt(one("abr"), one("mag"), one("co"), ALU.mult)
        tt(one("abi"), one("mag"), one("si"), ALU.mult)
        tt(one("t1"), one("lr"), one("lr"), ALU.mult)
        tt(one("t2"), li, li, ALU.mult)
        tt(one("den"), one("t1"), one("t2"), ALU.add)
        done(dve, dve.reciprocal(one("den"), one("den")), s.steps)
        ts(one("abr"), one("abr"), -1.0, None, ALU.add)
        tt(one("t1"), one("abr"), one("lr"), ALU.mult)
        tt(one("t2"), one("abi"), li, ALU.mult)
        tt(one("cfr"), one("t1"), one("t2"), ALU.add)
        tt(one("cfr"), one("cfr"), one("den"), ALU.mult)
        tt(one("t1"), one("abi"), one("lr"), ALU.mult)
        tt(one("t2"), one("abr"), li, ALU.mult)
        tt(one("cfi"), one("t1"), one("t2"), ALU.subtract)
        tt(one("cfi"), one("cfi"), one("den"), ALU.mult)
    return act_side, dve_side


def s5_tables(core, st, cs, sn, C_spread):
    v = {n: st.sb("p_" + n, [P, 8]) for n in "t1 t2 pr pi".split()}
    temp = st.sb("p_temp", [P, T])
    cr, ci, tb = (st.sb("p_" + n, [P, 8, 16]) for n in ("cr", "ci", "tb"))
    s = st.sems("tabled")
    one = lambda t: core.s5[t] if t in core.s5 else v[t][:]
    m3 = lambda ap: ap.rearrange("p (j q) -> p j q", j=8)

    def pool(gp):
        def tt(out, a, b, op):
            done(gp, gp.tensor_tensor(out, a, b, op), s.tabled)

        def spread(out, src):
            for j in range(8):
                o = out[:, j, :].rearrange("p (g q) -> p g q", q=16)
                gp.tensor_tensor(o, src[:, j:j + 1, :].broadcast_to([P, 8, 16]),
                                 m3(core.const("s5mask"))[:, j, :].rearrange("p (g q) -> p g q", q=16), ALU.mult).then_inc(s.tabled, 1)
            COUNTS[s.tabled.name] += 8

        cf = lambda n: one(n).rearrange("p (j o) -> p j o", o=1).broadcast_to([P, 8, 16])
        cre, cim = m3(core.param("cre")), m3(core.param("cim"))
        tt(cr[:], cre, cf("cfr"), ALU.mult)
        tt(tb[:], cim, cf("cfi"), ALU.mult)
        tt(cr[:], cr[:], tb[:], ALU.subtract)
        tt(ci[:], cre, cf("cfi"), ALU.mult)
        tt(tb[:], cim, cf("cfr"), ALU.mult)
        tt(ci[:], ci[:], tb[:], ALU.add)
        done(gp, gp.tensor_scalar(ci[:], ci[:], -1.0, None, ALU.mult), s.tabled)
        spread(C_spread[0], cr)
        spread(C_spread[1], ci)
        done(gp, gp.memset(cs[:, :, 0:1], 1.0), s.tabled)
        done(gp, gp.memset(sn[:, :, 0:1], 0.0), s.tabled)
        done(gp, gp.tensor_copy(cs[:, :, 1], one("co")), s.tabled)
        done(gp, gp.tensor_copy(sn[:, :, 1], one("si")), s.tabled)
        n = 2
        while n < T:
            a, b = cs[:, :, n - 1], sn[:, :, n - 1]
            tt(one("t1"), a, one("co"), ALU.mult)
            tt(one("t2"), b, one("si"), ALU.mult)
            tt(one("pr"), one("t1"), one("t2"), ALU.subtract)
            tt(one("t1"), a, one("si"), ALU.mult)
            tt(one("t2"), b, one("co"), ALU.mult)
            tt(one("pi"), one("t1"), one("t2"), ALU.add)
            g = min(8, T // n)
            for j in range(0, 8, g):
                J = slice(j, j + g)
                pc, ps = (one(x)[:, J].rearrange("p (j o) -> p j o", o=1).broadcast_to([P, g, n]) for x in ("pr", "pi"))
                lo_, hi_ = slice(0, n), slice(n, 2 * n)
                t = temp[:, 0:g * n].rearrange("p (j t) -> p j t", j=g)
                tt(cs[:, J, hi_], cs[:, J, lo_], pc, ALU.mult)
                tt(t, sn[:, J, lo_], ps, ALU.mult)
                tt(cs[:, J, hi_], cs[:, J, hi_], t, ALU.subtract)
                tt(sn[:, J, hi_], cs[:, J, lo_], ps, ALU.mult)
                tt(t, sn[:, J, lo_], pc, ALU.mult)
                tt(sn[:, J, hi_], sn[:, J, hi_], t, ALU.add)
            n *= 2
    return pool


def s5(core, Z, sn, C_spread):
    Y, cs = core.Y, core.Y
    with Stage(core, "s5") as st:
        BT = st.sb("BT", [P, 2, 8, P])
        s = st.sems("s5b_in wglu_in bu_ready products turned scan fourth forward x_ready x_used u_out "
                    "steps tanh_in tanhed gelu glu sigm glued sq total inv")
        back = st.sb("back", [P, 4, T])
        R, I, F = (st.sb(n, [P, 2, T]) for n in ("R", "I", "F"))
        fwd = st.sb("fwd", [P, 3, T])
        small = st.sb("wglu", [P, 512])
        u = Z[:, 0:2, :]

        def pool(gp):
            for j in range(8):
                c, d = cs[:, j, :], sn[:, j, :]
                gp.wait_ge(s.scan, 2 * j + 2)
                for i, (a, b) in enumerate(((R, c), (I, d), (R, d))):
                    gp.tensor_tensor(fwd[:, i, :], a[:, j % 2, :], b, ALU.mult).then_inc(s.forward, 1)
                gp.wait_ge(s.forward, 3 * j + 3)
                gp.wait_ge(s.fourth, j + 1)
                gp.tensor_tensor(c, fwd[:, 0, :], fwd[:, 1, :], ALU.subtract).then_inc(s.x_ready, 1)
                gp.tensor_tensor(d, F[:, j % 2, :], fwd[:, 2, :], ALU.add).then_inc(s.x_ready, 1)
                gp.wait_ge(s.x_ready, 2 * j + 2)

        block = st.block(pool)

        @block.sync
        def _(sp):
            sp.dma_start(BT[:], core.io["s5b"].rearrange("p (i j k) -> p i j k", i=2, j=8)).then_inc(s.s5b_in, 16)
            a, b = SMALL_AT["wglu"]
            sp.dma_start(small[:], core.io["small"][:, a:b]).then_inc(s.wglu_in, 16)

        @block.scalar
        def _(act):
            for j in range(2):
                act.wait_ge(s.tanh_in, j + 1)
                done(act, act.activation(sn[:, j, :], sn[:, j, :], ACT.Tanh, scale=float(np.sqrt(2 / np.pi))), s.tanhed)
            for j in range(2):
                act.wait_ge(s.glu, j + 1)
                done(act, act.activation(sn[:, j, :], core.psum[4 + j], ACT.Sigmoid), s.sigm)
            for j in range(2):
                act.wait_ge(s.glued, j + 1)
                done(act, act.activation(sn[:, 2 + j, :], Y[:, j, :], ACT.Square), s.sq)
            act.wait_ge(s.total, 1)
            inv_root(act, sn[:, 4, :], core.psum[6], s.inv, core.eps_rms[:], 1.0 / 256)

        @block.vector
        def _(dve):
            def tt(out, a, b, op, sem=s.steps):
                done(dve, dve.tensor_tensor(out, a, b, op), sem)

            def ts(out, a, x, y, op0, op1=None, sem=s.steps):
                done(dve, dve.tensor_scalar(out, a, x, y, op0, op1) if op1 is not None else dve.tensor_scalar(out, a, x, y, op0), sem)

            for j in range(8):
                c, d = cs[:, j, :], sn[:, j, :]
                dve.wait_ge(s.bu_ready, j + 1)
                br, bi = core.psum[2 * (j % 2)], core.psum[2 * (j % 2) + 1]
                for i, (a, b) in enumerate(((br, c), (bi, d), (bi, c), (br, d))):
                    dve.tensor_tensor(back[:, i, :], a, b, ALU.mult).then_inc(s.products, 1)
                dve.wait_ge(s.products, 4 * j + 4)
                dve.tensor_tensor(back[:, 0, :], back[:, 0, :], back[:, 1, :], ALU.add).then_inc(s.turned, 1)
                dve.tensor_tensor(back[:, 2, :], back[:, 2, :], back[:, 3, :], ALU.subtract).then_inc(s.turned, 1)
                dve.wait_ge(s.turned, 2 * j + 2)
                if j > 1:
                    dve.wait_ge(s.x_ready, 2 * j - 2)
                mag = core.s5["mag"][:, j:j + 1].broadcast_to([P, T])
                dve.tensor_tensor_scan(R[:, j % 2, :], mag, back[:, 0, :], 0.0, ALU.mult, ALU.add).then_inc(s.scan, 1)
                dve.tensor_tensor_scan(I[:, j % 2, :], mag, back[:, 2, :], 0.0, ALU.mult, ALU.add).then_inc(s.scan, 1)
                dve.wait_ge(s.scan, 2 * j + 2)
                dve.tensor_tensor(F[:, j % 2, :], I[:, j % 2, :], c, ALU.mult).then_inc(s.fourth, 1)
            A = back[:, 0, :]
            for j in range(2):
                dve.wait_ge(s.x_used, 8)
                y = Y[:, j, :]
                done(dve, dve.scalar_tensor_tensor(y, u[:, j, :], core.param("s5d", j), core.psum[4 + j], ALU.mult, ALU.add), s.u_out)
                tt(A, y, y, ALU.mult)
                ts(A, A, 0.044715, 1.0, ALU.mult, ALU.add)
                dve.wait_ge(s.x_ready, 16)
                tt(sn[:, j, :], A, y, ALU.mult, s.tanh_in)
            for j in range(2):
                y = Y[:, j, :]
                dve.wait_ge(s.tanhed, j + 1)
                ts(A, y, 0.5, None, ALU.mult)
                done(dve, dve.scalar_tensor_tensor(y, sn[:, j, :], 1.0, A, ALU.add, ALU.mult), s.gelu)
            for j in range(2):
                dve.wait_ge(s.sigm, j + 1)
                dve.wait_ge(s.glu, 2)
                tt(Y[:, j, :], Y[:, j, :], sn[:, j, :], ALU.mult, s.glued)
            dve.wait_ge(s.inv, 2)
            for j in range(2):
                done(dve, dve.scalar_tensor_tensor(Y[:, j, :], Y[:, j, :], core.param("gain", j), sn[:, 4, :], ALU.mult, ALU.mult), s.steps)

        @block.tensor
        def _(pe):
            def bu(j):
                if j >= 2:
                    pe.wait_ge(s.products, 4 * (j - 1))
                for i in range(2):
                    mm = pe.matmul(core.psum[2 * (j % 2) + i], BT[:, i, j, :], u[:, j // 4, :], start=True, stop=True)
                mm.then_inc(s.bu_ready, 1)

            pe.wait_ge(s.s5b_in, 16)
            bu(0)
            for j in range(8):
                if j < 7:
                    bu(j + 1)
                pe.wait_ge(s.x_ready, 2 * j + 2)
                bank = core.psum[4 + j // 4]
                pe.matmul(bank, C_spread[0][:, j, :], cs[:, j, :], start=j % 4 == 0, stop=False)
                mm = pe.matmul(bank, C_spread[1][:, j, :], sn[:, j, :], start=False, stop=j % 4 == 3)
                mm.then_inc(s.x_used, 1)
            pe.wait_ge(s.wglu_in, 16)
            pe.wait_ge(s.gelu, 2)
            wg = small[:].rearrange("p (k n) -> p k n", k=2)
            for j in range(2):
                for k in range(2):
                    mm = pe.matmul(core.psum[4 + j], wg[:, k, j * P:(j + 1) * P], Y[:, k, :], start=k == 0, stop=k == 1)
                mm.then_inc(s.glu, 1)
            for j in range(2):
                pe.wait_ge(s.sq, j + 1)
                mm = pe.matmul(core.psum[6], core.const("ones"), sn[:, 2 + j, :], start=j == 0, stop=j == 1)
            mm.then_inc(s.total, 1)


def head_norms(core, Z):
    Y = core.Y
    with Stage(core, "heads") as st:
        sq, sig = st.sb("sq", [P, 6, T]), st.sb("sig", [P, 4, T])
        s = st.sems("squared total sig log inv normed scaled gated")
        gates = {2: 8, 3: 9, 6: 22, 7: 23}
        block = st.block()

        @block.scalar
        def _(act):
            for i in range(6):
                done(act, act.activation(sq[:, i, :], Y[:, 2 + i, :], ACT.Square), s.squared)
            for i, z in enumerate(gates.values()):
                done(act, act.activation(sig[:, i, :], Z[:, z, :], ACT.Sigmoid), s.sig)
            for i in range(6):
                act.wait_ge(s.total, i + 1)
                done(act, act.activation(sq[:, i, :], core.psum[i], ACT.Ln, bias=core.eps_rms[:], scale=1.0 / 64), s.log)
            for i in range(6):
                act.activation(sq[:, i, :], sq[:, i, :], ACT.Exp, scale=-0.5).then_inc(s.inv, 1)

        @block.tensor
        def _(pe):
            for i in range(6):
                pe.wait_ge(s.squared, i + 1)
                pe.matmul(core.psum[i], core.const("blk"), sq[:, i, :], start=True, stop=True).then_inc(s.total, 1)

        @block.vector
        def _(dve):
            dve.wait_ge(s.sig, 4)
            for i in range(6):
                y = Y[:, 2 + i, :]
                dve.wait_ge(s.inv, i + 1)
                done(dve, dve.scalar_tensor_tensor(y, y, core.param("gain", 2 + i), sq[:, i, :], ALU.mult, ALU.mult), s.normed)
                if 2 + i in gates:
                    g = list(gates).index(2 + i)
                    done(dve, dve.tensor_tensor(y, y, sig[:, g, :], ALU.mult), s.scaled)
                    if i < 2:
                        done(dve, dve.tensor_tensor(y, y, Z[:, gates[2 + i], :], ALU.mult), s.gated)


def second_mixer(core):
    with Stage(core, "second") as st:
        Z = st.sb("Zs", [P, 25, T])
        with Stage(core, "tables") as tables:
            sn = tables.sb("sin", [P, 8, T])
            C_spread = [tables.sb(n, [P, 8, P]) for n in ("Cr", "Ci")]
            dense(core, [(10, Plain(Z)), (2, Plain(Z, 10, 64 ** -0.5)), (13, Plain(Z, 12))], core.Y,
                  norm=("rms", "pre"),
                  pool=lambda g: s5_tables(core, g, core.Y, sn, C_spread))
            s5(core, Z, sn, C_spread)
        G = st.sb("G", [P, 4, T])
        gate_rows(core, Z, G)
        rows = lambda e: slice(64 * e, 64 * e + 64)
        heads = [dict(q=[Z[rows(h % 2), 10 + h // 2, :]], k=Z[rows(h % 2), 12 + h // 2, :], v=Z[rows(h % 2), 14 + h // 2, :],
                      out=core.Y[rows(h % 2), 4 + h // 2, :], row=64 * (h % 2)) for h in range(4)]
        sel = core.const("sel").rearrange("p (h k) -> p h k", k=P)
        attention(core, "fox", heads, ["causal"], bias=lambda h: (sel[0:4, h, :], G[0:4, 1, :]))
        mlstm(core, Z, G)
        hgrn2(core, Z)
        head_norms(core, Z)
        dense(core, [(KD, Plain(core.Y))], core.Y)
    rms_norm(core, core.Y, "post", core.X)


def feed_forward(core):
    with Stage(core, "ffn") as st:
        xh, xl = (st.sb(n, [P, KD, T], F32R) for n in ("xh", "xl"))
        hh, hl = (st.sb(n, [P, FT, T], F32R) for n in ("hh", "hl"))
        slots = weight_slots(st, FT)
        parts = []
        for half in range(2):
            up = Gated(hh, hl)
            parts.append(gemm(st, f"gateup{half}_", slots, [(2 * FT, up)], core.Y, (xh, xl), split_src=half == 0,
                              norm=("rms", "fpre") if half == 0 else None))
            out = Plain(core.Y) if half == 0 else Accumulate(core.Y)
            parts.append(gemm(st, f"down{half}_", slots, [(KD, out)], None, (hh, hl), split_src=False, src_sem=up.s.hidden_lo))
        gemms(st, parts)
    rms_norm(core, core.Y, "fpost", core.X)


def store(core):
    with Stage(core, "store") as st:
        s = st.sems("stored")
        block = st.block()

        @block.sync
        def _(sp):
            sp.dma_start(core.io["out"].rearrange("p (k t) -> p k t", t=T), core.X[:]).then_inc(s.stored, 16)
            sp.wait_ge(s.stored, 16)


def load(core):
    with Stage(core, "load") as st:
        s = st.sems("x_in params_in set_eps")
        act_steps, dve_steps = s5_steps(core, st)
        block = st.block()

        @block.sync
        def _(sp):
            sp.dma_start(core.X[:], core.io["x"].rearrange("p (k t) -> p k t", t=T)).then_inc(s.x_in, 16)
            stream_weights(core, sp, 0, hi=RING)
            sp.wait_ge(s.x_in, 16)

        @block.scalar
        def _(act):
            act.dma_start(core.params[:], core.io["params"]).then_inc(s.params_in, 16)
            act.wait_ge(s.params_in, 16)
            act_steps(act)

        @block.vector
        def _(dve):
            for t, v in ((core.eps_ln, LN_EPS), (core.eps_gn, GN_EPS), (core.eps_rms, RMS_EPS)):
                dve.memset(t[:], v).then_inc(s.set_eps, 1)
            dve.wait_ge(s.params_in, 16)
            dve_steps(dve)


def load_consts(core, st):
    masks = st.sb("masks", [P, MASK_N])
    s = st.sems("cast")

    def pool(gp):
        gp.dma_start(core.consts[:], core.io["consts"]).then_inc(core.consts_in, 16)
        gp.dma_start(masks[:], core.io["masks"]).then_inc(core.consts_in, 16)
        gp.wait_ge(core.consts_in, 32)
        done(gp, gp.tensor_copy(core.masks[:], masks[:]), s.cast)
    return pool


def mlp(core, layer):
    with Stage(core, "mlp") as st:
        xh, xl = (st.sb(n, [P, KD, T], F32R) for n in ("xh", "xl"))
        hh, hl = (st.sb(n, [P, HALF, T], F32R) for n in ("hh", "hl"))
        slots = weight_slots(st, KD)
        parts = []
        for half in range(2):
            up = SquaredRelu(hh, hl)
            parts.append(gemm(st, f"up{half}_", slots, [(HALF, up)], core.X, (xh, xl), split_src=half == 0,
                              norm=("ln", f"ln1g{layer}", f"ln1b{layer}") if half == 0 else None))
            out = Residual(core.Y, core.X) if half == 0 else Accumulate(core.Y, sum=True)
            parts.append(gemm(st, f"down{half}_", slots, [(KD, out)], None, (hh, hl), U=2, split_src=False, src_sem=up.s.hidden_lo))
        gemms(st, parts)


def dense(core, segments, src, pool=None, norm=None):
    with Stage(core, "dense") as st:
        xh, xl = (st.sb(n, [P, KD, T], F32R) for n in ("xh", "xl"))
        gemms(st, [gemm(st, "", weight_slots(st, KD), segments, src, (xh, xl), pool=pool(st) if pool else None, norm=norm)])


def first_mixer(core):
    with Stage(core, "mixer") as st:
        Z = st.sb("Z", [P, 27, T])
        scale = P ** -0.5
        dense(core, [(15, Shift(Z)), (4, Rope(Z, 15, scale)), (4, Rope(Z, 19)), (4, Plain(Z, 23))], core.X,
              pool=lambda g: load_consts(core, g))
        O = st.sb("O", [P, KD, T])
        heads = [dict(q=[Z[:, 15 + h, :]], k=Z[:, 19 + h, :], v=Z[:, 23 + h, :], out=O[:, 4 + h, :], row=0) for h in range(4)]
        attention(core, "moba", heads, ["causal"])
        rwkv(core, Z, O)
        dense(core, [(KD, Residual(core.Y, core.X, sum=True))], O)


def dilated_mixer(core):
    with Stage(core, "dilated") as st:
        Z = st.sb("Z", [P, 40, T])
        dense(core, [(24, Rope(Z, 0, P ** -0.5)), (8, Rope(Z, 24)), (8, Plain(Z, 32))], core.X,
              norm=("ln", "ln2g0", "ln2b0"))
        heads = [dict(q=[Z[:, 8 * g + h, :] for g in range(3)], k=Z[:, 24 + h, :], v=Z[:, 32 + h, :], out=Z[:, 32 + h, :], row=0) for h in range(8)]
        attention(core, "dil", heads, ["band", "mod4", "mod16"])
        dense(core, [(KD, Residual(core.Y, core.X, sum=True))], Z[:, 32:40, :])


def program(nc, io):
    with ExitStack() as ctx:
        core = Core(nc, io, ctx)
        core.gemms = [(io[n], kt, u) for n, kt, u in STREAMS]
        load(core)
        first_mixer(core)
        mlp(core, 0)
        dilated_mixer(core)
        mlp(core, 1)
        layer_norm(core, "ln2g1", "ln2b1")
        second_mixer(core)
        feed_forward(core)
        store(core)


STREAMS = [("w_ab_in", 8, 27), ("w_ab_out", 8, 8),
           ("w1_0_0", 8, HALF), ("w2_0_0", 8, 16), ("w1_0_1", 8, HALF), ("w2_0_1", 8, 16),
           ("w_c_in", 8, 40), ("w_c_out", 8, 8),
           ("w1_1_0", 8, HALF), ("w2_1_0", 8, 16), ("w1_1_1", 8, HALF), ("w2_1_1", 8, 16),
           ("w_in2", 8, 25), ("w_out2", 8, 8),
           ("w_gu_0", 8, 2 * FT), ("w_down_0", FT, 8), ("w_gu_1", 8, 2 * FT), ("w_down_1", FT, 8)]


def weight_units(w, kt, pair=None):
    K, N = w.shape
    w = w.reshape(K // (kt * P), kt, P, N // P, P)
    return np.ascontiguousarray(w.transpose(3, 0, 2, 1, 4)).reshape(-1, P, kt * P)


def padded(w, cols):
    return np.concatenate([w, np.zeros((w.shape[0], cols - w.shape[1]), w.dtype)], 1)


def columns(v):
    return np.asarray(v).reshape(-1, P).T


def layout(i):
    a = {k: np.asarray(v) for k, v in i.items()}
    io = {"x": a["x"][0].reshape(T, KD, P).transpose(2, 1, 0).reshape(P, KD * T), "consts": const_array(), "masks": mask_array()}
    w = a["ab_w_in"][0]
    io["w_ab_in"] = weight_units(np.concatenate([padded(w[:, :1824], 15 * P), w[:, 1824:]], 1), 8)
    io["w_ab_out"] = weight_units(a["ab_w_out"][0], 8)
    io["w_c_in"] = weight_units(a["c_w_in"][0], 8)
    io["w_c_out"] = weight_units(a["c_w_out"][0], 8)
    hid = HALF * P
    for layer in range(2):
        for h in range(2):
            io[f"w1_{layer}_{h}"] = weight_units(a["mlp_w1"][layer][:, h * hid:(h + 1) * hid], 8)
            io[f"w2_{layer}_{h}"] = weight_units(a["mlp_w2"][layer][h * hid:(h + 1) * hid], 8)
    w = a["w_in_2"][0]
    W = 256
    gates = np.zeros((D, P), w.dtype)
    gates[:, 0:4] = w[:, 8 * W:8 * W + 4]
    gates[:, 32:36] = w[:, 12 * W + 4:12 * W + 8]
    gates[:, 64:68] = w[:, 12 * W + 8:12 * W + 12]
    io["w_in2"] = weight_units(np.concatenate([w[:, :8 * W], w[:, 8 * W + 4:12 * W + 4], gates], 1), 8)
    io["w_out2"] = weight_units(a["w_out_2"][0], 8)
    gate, up, down = a["w_ffn_gate_2"][0], a["w_ffn_up_2"][0], a["w_ffn_down_2"][0]
    fh = FT * P
    for h in range(2):
        both = np.stack([m[:, h * fh:(h + 1) * fh].reshape(D, FT, P) for m in (gate, up)], 2)
        io[f"w_gu_{h}"] = weight_units(both.reshape(D, 2 * fh), 8)
        io[f"w_down_{h}"] = weight_units(down[h * fh:(h + 1) * fh], FT)
    small = {n: np.zeros((P, c), np.float32) for n, c in SMALL_COLS.items()}
    small["lora"][0:64], small["lora"][64:128] = a["ab_w_up"][0], a["ab_a_up"][0]
    small["gup0"][:], small["gup1"][0:32] = a["ab_g_up"][0][0:P], a["ab_g_up"][0][P:160]
    small["wglu"][:] = a["s5_w_glu_2"][0].reshape(2, P, 256).transpose(1, 0, 2).reshape(P, 512)
    io["small"] = np.concatenate([small[n] for n in SMALL_COLS], 1)

    p = {}
    mix = a["ab_shift_mix"][0]
    p["mix"] = columns(np.concatenate([mix, np.zeros(15 * P - 1824, mix.dtype)]))
    for n, key in (("w0", "ab_w0"), ("a0", "ab_a0"), ("kk", "ab_k_k"), ("ka", "ab_k_a"), ("gng", "ab_lnx_g"), ("gnb", "ab_lnx_b"),
                   ("pre", "ln_mix_pre_2"), ("post", "ln_mix_post_2"), ("fpre", "ln_ffn_pre_2"), ("fpost", "ln_ffn_post_2"),
                   ("gain", "mix_gain_2"), ("s5d", "s5_d_2")):
        p[n] = columns(a[key][0])
    p["rk"] = columns(a["ab_r_k"][0].reshape(-1))
    for layer in range(2):
        for n in ("ln1", "ln2"):
            for m in "gb":
                p[f"{n}{m}{layer}"] = columns(a[f"{n}_{m}"][layer])
    gb = a["gate_bias_2"][0]
    p["gateb"] = np.zeros((P, 1), np.float32)
    p["gateb"][0:4, 0], p["gateb"][32:36, 0], p["gateb"][64:68, 0] = gb[0:4], gb[4:8], gb[8:12]
    states = lambda v: v.reshape(8, P, *v.shape[2:])
    p["lre"], p["lim"] = states(a["s5_lambda_re_2"][0]).T, states(a["s5_lambda_im_2"][0]).T
    p["ldt"] = np.repeat(a["s5_log_dt_2"][0].reshape(8, 2), 64, axis=1).T
    spread = np.zeros((2, 8, P, P), np.float32)
    for k, b in enumerate((a["s5_b_re_2"][0], a["s5_b_im_2"][0])):
        for g in range(16):
            at = 16 * (g % 8)
            spread[k, g // 2, at:at + 16, 64 * (g % 2):64 * (g % 2) + 64] = b.reshape(16, 64, 16)[g].T
    io["s5b"] = spread.transpose(2, 0, 1, 3).reshape(P, 16 * P)
    p["cre"], p["cim"] = (states(a[k][0].transpose(0, 2, 1)).transpose(1, 0, 2).reshape(P, 128) for k in ("s5_c_re_2", "s5_c_im_2"))
    p["conv"] = a["mlstm_conv_w_2"][0].reshape(4, 4, P).transpose(2, 1, 0).reshape(P, 16)
    io["params"] = np.concatenate([np.asarray(p[n], np.float32).reshape(P, -1) for n in PARAM_COLS], 1)
    return {n: np.ascontiguousarray(v) for n, v in io.items()}


def kernel(**inputs):
    import concourse.bacc as bacc
    from concourse.bass_utils import run_bass_kernel_spmd

    nc = bacc.Bacc("TRN2", target_bir_lowering=False, num_devices=1)
    arrays = layout(inputs)
    io = {n: nc.dram_tensor(f"in_{n}", v.shape, mybir.dt.from_np(v.dtype), kind="ExternalInput").ap() for n, v in arrays.items()}
    io["out"] = nc.dram_tensor("out_x", (P, KD * T), F32, kind="ExternalOutput").ap()
    program(nc, io)
    r = run_bass_kernel_spmd(nc, [{f"in_{n}": v for n, v in arrays.items()}], core_ids=[0])
    out = r.results[0]["out_x"].reshape(P, KD, T)
    return np.ascontiguousarray(out.transpose(2, 1, 0)).reshape(1, T, D)
```
